# Optimizing a Trainium2 kernel written in Bass

```python
import jax
import jax.numpy as jnp
from jax import lax
import numpy as np

D_MODEL = 1024
BATCH = 1
SEQ = 256
DEPTH = 1

MEM_LEN = 256
W_A = D_MODEL
A_CONV = 3
W_B = D_MODEL
B_CONV = 31
X_HEADS = 4
X_HEAD_DIM = D_MODEL // X_HEADS
W_X = X_HEADS * X_HEAD_DIM
N_BRANCH = 3
N_IN = 3 * W_A + 2 * W_B + W_X + N_BRANCH * D_MODEL
SPLITS = [W_A, 2 * W_A, 3 * W_A, 3 * W_A + 2 * W_B, 3 * W_A + 2 * W_B + W_X]
N_GROUPS = 4
EXPERTS_PER_GROUP = 8
N_EXPERTS = N_GROUPS * EXPERTS_PER_GROUP
TOP_K_IN_GROUP = 2
D_FF_EXPERT = D_MODEL // 2
EPS = 1e-6

kernel_name = "hybrid_gated_conv_xattn_hmoe"

def rms_norm(x, g):
    xf = x.astype(jnp.float32)
    y = xf * lax.rsqrt(jnp.mean(xf * xf, axis=-1, keepdims=True) + EPS)
    return (y * g.astype(jnp.float32)).astype(x.dtype)

def layer_norm(x, g, b):
    xf = x.astype(jnp.float32)
    mu = jnp.mean(xf, axis=-1, keepdims=True)
    xc = xf - mu
    var = jnp.mean(xc * xc, axis=-1, keepdims=True)
    y = xc * lax.rsqrt(var + EPS) * g.astype(jnp.float32) + b.astype(jnp.float32)
    return y.astype(x.dtype)

def causal_depthwise_conv(u, w):
    k, c = w.shape
    return lax.conv_general_dilated(
        u, w[:, None, :].astype(u.dtype), window_strides=(1,), padding=[(k - 1, 0)],
        dimension_numbers=("NWC", "WIO", "NWC"), feature_group_count=c)

def setup_inputs(seed: int = 0) -> dict:
    key = jax.random.key(seed)
    ks = jax.random.split(key, 26)
    f32 = jnp.float32
    nrm = lambda k, shape, scale: jax.random.normal(k, shape, f32) * scale
    L, D = DEPTH, D_MODEL
    return {
        "x": nrm(ks[0], (BATCH, SEQ, D), 1.0),
        "mem": nrm(ks[1], (BATCH, MEM_LEN, D), 1.0),
        "mix_norm_g": 1.0 + nrm(ks[2], (L, D), 0.02),
        "mem_norm_g": 1.0 + nrm(ks[3], (L, D), 0.02),
        "w_in": nrm(ks[4], (L, D, N_IN), D ** -0.5),
        "b_gate": nrm(ks[5], (L, N_BRANCH * D), 0.02),
        "conv_a_w": nrm(ks[6], (L, A_CONV, W_A), A_CONV ** -0.5),
        "w_out_a": nrm(ks[7], (L, W_A, D), W_A ** -0.5),
        "b_glu": nrm(ks[8], (L, 2 * W_B), 0.02),
        "conv_b_w": nrm(ks[9], (L, B_CONV, W_B), B_CONV ** -0.5),
        "conv_b_b": nrm(ks[10], (L, W_B), 0.02),
        "ln_b_g": 1.0 + nrm(ks[11], (L, W_B), 0.02),
        "ln_b_b": nrm(ks[12], (L, W_B), 0.02),
        "w_out_b": nrm(ks[13], (L, W_B, D), W_B ** -0.5),
        "b_out_b": nrm(ks[14], (L, D), 0.02),
        "w_kv": nrm(ks[15], (L, D, 2 * W_X), D ** -0.5),
        "w_out_x": nrm(ks[16], (L, W_X, D), W_X ** -0.5),
        "w_o": nrm(ks[17], (L, D, D), D ** -0.5),
        "ffn_norm_g": 1.0 + nrm(ks[18], (L, D), 0.02),
        "w_group": nrm(ks[19], (L, D, N_GROUPS), D ** -0.5),
        "b_group": nrm(ks[20], (L, N_GROUPS), 0.01),
        "w_router": nrm(ks[21], (L, D, N_EXPERTS), D ** -0.5),
        "b_router": nrm(ks[22], (L, N_EXPERTS), 0.01),
        "w_gate_up": nrm(ks[23], (L, N_EXPERTS, D, 2 * D_FF_EXPERT), D ** -0.5),
        "w_down": nrm(ks[24], (L, N_EXPERTS, D_FF_EXPERT, D), D_FF_EXPERT ** -0.5),
        "final_norm_g": 1.0 + nrm(ks[25], (D,), 0.02),
    }

def cross_attention(q, mem_n, w_kv):
    b, s, _ = q.shape
    kv = mem_n @ w_kv
    k, v = jnp.split(kv, 2, axis=-1)
    qh = q.reshape(b, s, X_HEADS, X_HEAD_DIM)
    kh = k.reshape(b, -1, X_HEADS, X_HEAD_DIM)
    vh = v.reshape(b, -1, X_HEADS, X_HEAD_DIM)
    scores = jnp.einsum("bshd,bmhd->bhsm", qh, kh).astype(jnp.float32) * (X_HEAD_DIM ** -0.5)
    probs = jax.nn.softmax(scores, axis=-1).astype(vh.dtype)
    out = jnp.einsum("bhsm,bmhd->bshd", probs, vh)
    return out.reshape(b, s, W_X)

def hierarchical_moe(z, w_group, b_group, w_router, b_router, w_gate_up, w_down):
    g_logits = (z @ w_group).astype(jnp.float32) + b_group.astype(jnp.float32)
    g_probs = jax.nn.softmax(g_logits, axis=-1)
    g_sel = jnp.argmax(g_probs, axis=-1)
    g_p = jnp.max(g_probs, axis=-1)
    e_logits = (z @ w_router).astype(jnp.float32) + b_router.astype(jnp.float32)
    e_logits = e_logits.reshape(z.shape[0], z.shape[1], N_GROUPS, EXPERTS_PER_GROUP)
    e_in_group = jnp.take_along_axis(e_logits, g_sel[..., None, None], axis=2)[..., 0, :]
    e_probs = jax.nn.softmax(e_in_group, axis=-1)
    top_p, top_i = lax.top_k(e_probs, TOP_K_IN_GROUP)
    top_w = top_p / jnp.sum(top_p, axis=-1, keepdims=True)
    global_idx = g_sel[..., None] * EXPERTS_PER_GROUP + top_i
    combine = jnp.sum(jax.nn.one_hot(global_idx, N_EXPERTS, dtype=jnp.float32) * top_w[..., None], axis=-2)
    combine = (combine * g_p[..., None]).astype(z.dtype)
    y = jnp.zeros_like(z)
    for e in range(N_EXPERTS):
        gate, up = jnp.split(z @ w_gate_up[e], 2, axis=-1)
        y = y + combine[..., e:e + 1] * ((jax.nn.silu(gate) * up) @ w_down[e])
    return y

def reference(x, mem, mix_norm_g, mem_norm_g, w_in, b_gate, conv_a_w, w_out_a, b_glu,
              conv_b_w, conv_b_b, ln_b_g, ln_b_b, w_out_b, b_out_b, w_kv, w_out_x, w_o,
              ffn_norm_g, w_group, b_group, w_router, b_router, w_gate_up, w_down,
              final_norm_g):
    b, s, d = x.shape
    for l in range(DEPTH):
        x_n = rms_norm(x, mix_norm_g[l])
        h = x_n @ w_in[l]
        a_val, a_gb, a_gc, h_glu, q, h_gate = jnp.split(h, SPLITS, axis=-1)

        y_a = (a_gb * causal_depthwise_conv(a_gc * a_val, conv_a_w[l])) @ w_out_a[l]

        glu_val, glu_gate = jnp.split(h_glu + b_glu[l], 2, axis=-1)
        u = glu_val * jax.nn.sigmoid(glu_gate)
        u = causal_depthwise_conv(u, conv_b_w[l]) + conv_b_b[l]
        u = jax.nn.silu(layer_norm(u, ln_b_g[l], ln_b_b[l]))
        y_b = u @ w_out_b[l] + b_out_b[l]

        mem_n = rms_norm(mem, mem_norm_g[l])
        y_x = cross_attention(q, mem_n, w_kv[l]) @ w_out_x[l]

        gates = jax.nn.sigmoid(h_gate + b_gate[l]).reshape(b, s, N_BRANCH, d)
        merged = gates[..., 0, :] * y_a + gates[..., 1, :] * y_b + gates[..., 2, :] * y_x
        x = x + merged @ w_o[l]

        z = rms_norm(x, ffn_norm_g[l])
        x = x + hierarchical_moe(z, w_group[l], b_group[l], w_router[l], b_router[l],
                                 w_gate_up[l], w_down[l])
    return rms_norm(x, final_norm_g)


_drawn_inputs = setup_inputs


def setup_inputs(seed=0):
    import zlib

    import numpy as np

    out = dict(_drawn_inputs(seed))
    spreads = {}
    factors = {'mem_norm_g': 8.0,
     'b_gate': 5.542,
     'b_glu': 2.888,
     'conv_b_b': 2.955,
     'ln_b_g': 28.153,
     'ln_b_b': 24.594,
     'b_out_b': 19.254,
     'b_group': 50.04,
     'b_router': 36.1,
     'final_norm_g': 7.851,
     'ffn_norm_g': 6.869}
    for name, (base, spread) in spreads.items():
        noise = np.random.default_rng([zlib.crc32(name.encode()), seed]).standard_normal(out[name].shape)
        drawn = base * np.exp(spread * noise) if base else spread * noise
        out[name] = jnp.asarray(drawn.astype(out[name].dtype))
    for name, factor in factors.items():
        out[name] = (out[name] * factor).astype(out[name].dtype)
    return out
```

```python
import concourse.bass as bass
from concourse import mybir
from contextlib import ExitStack

D = 1024
T = 256
P = 128
KT = D // P
TT = T // P
HEADS = 4
HEAD_DIM = D // HEADS
TAPS_A = 3
TAPS_B = 31
GROUPS = 4
EPG = 8
E = GROUPS * EPG
FF = 512
EPS = 1e-6
SLOTS = 64
MAX_ROUNDS = T // SLOTS
HALF = 2048
UNIT = 2 * HALF
RAW = 6
RAW_DENSE = 4
CONV = 3
BIG = 1.0e30

COL = {}
_at = 0
for _name, _n in (("mix_g", 1), ("mem_g", 1), ("b_gate", 3), ("b_glu", 2), ("conv_a", TAPS_A),
                  ("conv_b", TAPS_B), ("conv_b_b", 1), ("ln_g", 1), ("ln_b", 1), ("b_out", 1)):
    COL[_name] = _at
    _at += _n * KT
N_COLS = _at

CST = {}
_at = 0
for _name, _n in (("ident", P), ("ones", P), ("before", P), ("fold", SLOTS), ("slot_row", P),
                  ("slot_col", MAX_ROUNDS * E), ("desc_g", GROUPS), ("desc_e", E)):
    CST[_name] = (_at, _at + _n)
    _at += _n
N_CST = _at

UNITS = []
for _g in range(2):
    UNITS += [("glu_value", "w_in", 3 * D + 512 * _g), ("glu_gate", "w_in", 4 * D + 512 * _g)]
for _g in range(2):
    UNITS += [("a_value", "w_in", 512 * _g), ("a_c", "w_in", 2 * D + 512 * _g), ("a_b", "w_in", D + 512 * _g)]
for _name, _m, _c in (("gate0", "w_in", 6 * D), ("out_a", "w_out_a", 0), ("q", "w_in", 5 * D),
                      ("k", "w_kv", 0), ("v", "w_kv", D), ("gate2", "w_in", 8 * D),
                      ("out_x", "w_out_x", 0), ("gate1", "w_in", 7 * D), ("out_b", "w_out_b", 0),
                      ("w_o", "w_o", 0)):
    UNITS += [(_name, _m, _c + 512 * _g) for _g in range(2)]
N_UNITS = len(UNITS)
DENSE = 2 * N_UNITS
FIRST = {}
for _u, (_name, _, _) in enumerate(UNITS):
    FIRST.setdefault(_name, 2 * _u)
K_SPLIT = ("v", "w_o")
RING = 6
LOOPED = 12

f32 = mybir.dt.float32
r32 = mybir.dt.float32r
bf16 = mybir.dt.bfloat16
i32 = mybir.dt.int32
ACT = mybir.ActivationFunctionType
ALU = mybir.AluOpType
AX = mybir.AxisListType


def hybrid_moe_kernel(nc, x, mem, w_in, w_out_a, w_out_b, w_out_x, w_kv, w_o, w_gate_up, w_down,
                      w_route, cols, rows, b_route, consts, out):
    matrices = {"w_in": w_in, "w_out_a": w_out_a, "w_out_b": w_out_b, "w_out_x": w_out_x,
                "w_kv": w_kv, "w_o": w_o}
    ctx = ExitStack()
    with ctx:
        base = (nc.sbuf_base + 63) // 64 * 64

        def at(name, offset, shape, dt=f32):
            return nc.alloc_sbuf_tensor_at(name, [P] + shape, dt, offset=base + offset)

        KB = 1024
        raw = at("raw", 0, [RAW, UNIT])
        hi = at("hi", 96 * KB, [CONV, HALF], r32)
        lo = at("lo", 120 * KB, [CONV, HALF], r32)
        kT = at("kT", 64 * KB, [KT, T])
        v_sb = at("v_sb", 72 * KB, [TT, D])
        qT = at("qT", 80 * KB, [KT, T])
        probsT = at("probsT", 80 * KB, [HEADS, TT, T])
        mem_sb = at("mem_sb", 88 * KB, [TT, D])
        probs = at("probs", 88 * KB, [HEADS, TT, T])
        A0 = 144 * KB
        inA = at("inA", A0, [2, KT, T], r32)
        z_parts = at("z_parts", A0, [2, TT, D], r32)
        inB = at("inB", A0 + 16 * KB, [2, KT, T], r32)
        ffn_row = at("ffn_row", A0 + 16 * KB, [D])
        route = at("route", A0 + 20 * KB, [768])
        xeT = at("xeT", A0 + 16 * KB, [2, KT, 2 * SLOTS], r32)
        y_parts = at("y_parts", A0 + 24 * KB, [2, D], r32)
        B0 = A0 + 32 * KB
        a_mid = at("a_mid", B0, [KT, T])
        merged = at("merged", B0, [KT, T])
        x2 = at("x2", B0, [TT, D])
        gate = at("gate", B0 + 8 * KB, [KT, T])
        zT = at("zT", B0 + 8 * KB, [KT, T])
        conv = at("conv", B0 + 16 * KB, [KT, T])
        x_again = at("x_again", B0 + 16 * KB, [TT, D])
        rank_rows = at("rank_rows", B0 + 8 * KB, [E, T], bf16)
        u_sb = at("u_sb", B0 + 24 * KB, [KT, T])
        x_sb = at("x_sb", B0 + 24 * KB, [TT, D])
        z_sb = at("z_sb", B0 + 24 * KB, [TT, D])
        gu_sb = at("gu_sb", B0 + 24 * KB, [2 * FF])
        silu_sb = at("silu_sb", B0 + 28 * KB, [4, SLOTS])
        h_sb = at("h_sb", B0 + 29 * KB, [4, SLOTS])
        x3 = at("x3", B0 + 24 * KB, [TT, D])
        S0 = B0 + 32 * KB
        pick = at("pick", S0, [2, TT, 2 * SLOTS], r32)
        put = at("put", S0 + 2 * KB, [T], r32)
        hT = at("hT", S0 + 3 * KB, [4, 2 * SLOTS], r32)
        part = at("part", S0, [2, T])
        ln_mean = at("ln_mean", S0 + 2 * KB, [T])
        ln_rstd = at("ln_rstd", S0 + 3 * KB, [T])
        S1 = S0 + 5 * KB
        cst = at("cst", S1, [N_CST])
        S2 = S1 + (4 * N_CST + 63) // 64 * 64
        col = at("col", S2, [N_COLS])
        S3 = S2 + (4 * N_COLS + 63) // 64 * 64
        wr = at("wr", S3, [KT, GROUPS + E])
        S4 = S3 + (4 * KT * (GROUPS + E) + 63) // 64 * 64
        rank_tab = at("rank_tab", S4, [TT, (MAX_ROUNDS + 1) * E])
        S5 = S4 + 4 * TT * (MAX_ROUNDS + 1) * E
        comb = at("comb", S5, [TT, E, 2], r32)
        S6 = S5 + 8 * TT * E
        stat = at("stat", S6, [24])
        comb_slot = at("comb_slot", S6 + 96, [2])
        loops = at("loops", S6 + 128, [2], i32)
        rank_bf = at("rank_bf", S6 + 160, [T], bf16)
        br = at("br", S6 + 160 + 2 * T, [GROUPS + E])

        ps = ctx.enter_context(nc.psum_tensor("ps", [P, 8, 512], f32))
        rank_dram = nc.dram_tensor("rank_dram", [E, T], bf16, kind="Internal").ap()

        def c_(name):
            return cst[:, CST[name][0]:CST[name][1]]

        ident, ones, before, fold = c_("ident"), c_("ones"), c_("before"), c_("fold")

        def vec(name, c, k=0):
            a = COL[name] + k * KT + c
            return col[:, a:a + 1]

        def sem(name):
            return ctx.enter_context(nc.semaphore(name))

        raw_loaded = [sem(f"raw_loaded{s}") for s in range(RAW)]
        hi_made, lo_made, half_used = sem("hi_made"), sem("lo_made"), sem("half_used")
        bank_free = [sem(f"bank_free{b}") for b in range(RING)]
        x_loaded, mem_loaded, cst_loaded, col_loaded = map(sem, ("x_loaded", "mem_loaded", "cst_loaded", "col_loaded"))
        wr_loaded, ffn_loaded, final_loaded, xagain_loaded = map(sem, ("wr_loaded", "ffn_loaded", "final_loaded", "xagain_loaded"))
        sumsq, meansq, root, scaled, xT_turned, x_hi, x_lo = map(sem, ("sumsq", "meansq", "root", "scaled", "xT_turned", "x_hi", "x_lo"))
        memT_turned, mem_hi, mem_lo = map(sem, ("memT_turned", "mem_hi", "mem_lo"))
        glu_value, glu_gate, u_ready = map(sem, ("glu_value", "glu_gate", "u_ready"))
        a_value, a_cv, a_prod, a_hi, a_lo = map(sem, ("a_value", "a_cv", "a_prod", "a_hi", "a_lo"))
        gate_made, merged_a, merged_x, merged_all, merged_hi, merged_lo = map(
            sem, ("gate_made", "merged_a", "merged_x", "merged_all", "merged_hi", "merged_lo"))
        q_made, k_made, v_made = map(sem, ("q_made", "k_made", "v_made"))
        scored, score_max, exps, prob_made, probs_turned, probsT_made, attended, att_hi, att_lo = map(
            sem, ("scored", "score_max", "exps", "prob_made", "probs_turned", "probsT_made", "attended", "att_hi", "att_lo"))
        conv_step, ln_sum, ln_centred, ln_square, ln_sumsq, ln_var, ln_root, ln_scaled, b_silu, b_hi, b_lo = map(
            sem, ("conv_step", "ln_sum", "ln_centred", "ln_square", "ln_sumsq", "ln_var", "ln_root", "ln_scaled", "b_silu", "b_hi", "b_lo"))
        x2_made, z_made, z_hi, z_lo, zT_turned, zT_made, logits_done = map(
            sem, ("x2_made", "z_made", "z_hi", "z_lo", "zT_turned", "zT_made", "logits_done"))
        route_for_exp, route_exp, member_made, ranked, rank_made, rank_turned, rank_copied, rank_stored, rank_rows_loaded = map(
            sem, ("route_for_exp", "route_exp", "member_made", "ranked", "rank_made", "rank_turned", "rank_copied", "rank_stored", "rank_rows_loaded"))
        loops_made, comb_made = sem("loops_made"), sem("comb_made")
        pick_made, put_made, gathered, xeT_made = map(sem, ("pick_made", "put_made", "gathered", "xeT_made"))
        gate_out, up_out, slotted, comb_slot_made, folded = map(sem, ("gate_out", "up_out", "slotted", "comb_slot_made", "folded"))
        silu_made, h_made, h_hi, h_lo = map(sem, ("silu_made", "h_made", "h_hi", "h_lo"))
        y_hi, y_lo, y_seeded, combined = map(sem, ("y_hi", "y_lo", "y_seeded", "combined"))
        x3_made, sumsq3, root3, out_made, stored = map(sem, ("x3_made", "sumsq3", "root3", "out_made", "stored"))
        dve_chain = sem("dve_chain")

        Y = [ps[:, b, :] for b in range(4)]
        G0, G1 = ps[:, 4, :], ps[:, 5, :]
        DN = [ps[:, 6, :], ps[:, 7, :]]

        def sums(t):
            return ps[:, 2 * t:2 * t + 2, :].rearrange("p a b -> p (a b)")

        def raw_slot(u):
            return (u + 2) % RAW_DENSE, u // RAW_DENSE

        RAW_BASE = [0] * RAW
        for u in range(N_UNITS):
            RAW_BASE[raw_slot(u)[0]] += 1

        def expert_slot(m):
            return (m + 4) % RAW

        def raw_half(slot, h, k_split):
            flat = raw[:, slot, :]
            if k_split:
                return flat[:, h * HALF:(h + 1) * HALF].rearrange("p (a b) -> p a b", b=T)
            return flat.rearrange("p (a b) -> p a b", b=2 * T)[:, :, h * T:(h + 1) * T]

        def conv_half(buf, N):
            return buf[:, N % CONV, :].rearrange("p (a b) -> p a b", b=T)

        block = ctx.enter_context(nc.Block())

        @block.sync
        def _(sp):
            for u, (name, matrix, c0) in enumerate(UNITS):
                slot = raw_slot(u)[0]
                if u >= RAW_DENSE:
                    sp.wait_ge(lo_made, 2 * (u - RAW_DENSE) + 2)
                src = matrices[matrix][:, c0:c0 + 512].rearrange("(k p) n -> p k n", p=P)
                sp.dma_start(raw[:, slot, :].rearrange("p (k n) -> p k n", n=512), src)\
                    .then_inc(raw_loaded[slot], 16)

            gate_up = w_gate_up.rearrange("(j u) (k p) n -> u p j k n", u=2, p=P)
            down = w_down.rearrange("(j u) (k p) n -> u p j k n", u=2, p=P)

            def load_gate_up(slot, parity, j, c):
                src = gate_up[parity, :, bass.ds(j, 1), :, c * FF:(c + 1) * FF]
                sp.dma_start(raw[:, slot, :].rearrange("p (a k n) -> p a k n", a=1, n=FF), src)\
                    .then_inc(raw_loaded[slot], 16)

            def load_down(slot, parity, j):
                src = down[parity, :, bass.ds(j, 1), :, :]
                sp.dma_start(raw[:, slot, :].rearrange("p (a k n) -> p a k n", a=1, n=D), src)\
                    .then_inc(raw_loaded[slot], 16)

            def lo_of(m):
                return DENSE + 2 * (m - RAW) + 2

            sp.wait_ge(attended, HEADS)
            load_gate_up(expert_slot(0), 0, 0, 0)
            load_gate_up(expert_slot(1), 0, 0, 1)
            for m in (2, 3, 4):
                sp.wait_ge(lo_made, lo_of(m))
                if m < 4:
                    load_gate_up(expert_slot(m), 1, 0, m - 2)
                else:
                    load_down(expert_slot(m), 0, 0)

            def pair(j, j_mod, j_before):
                for r, load in enumerate((lambda s: load_gate_up(s, 0, j_mod, 0),
                                          lambda s: load_gate_up(s, 0, j_mod, 1),
                                          lambda s: load_down(s, 1, j_before),
                                          lambda s: load_gate_up(s, 1, j_mod, 0),
                                          lambda s: load_gate_up(s, 1, j_mod, 1),
                                          lambda s: load_down(s, 0, j_mod))):
                    sp.wait_ge(lo_made, 12 * j + (lo_of(r - 1)))
                    load(expert_slot(5 + r))

            with sp.Fori(1, E // 2) as j:
                pair(j, j, j - 1)
            sp.wait_ge(loops_made, 1)
            last_pair = nc.sync.value_load(loops[0:1, 0:1], min_val=E // 2 - 1, max_val=MAX_ROUNDS * E // 2 - 1)
            with sp.If(last_pair > E // 2 - 1):
                with sp.Fori(E // 2, last_pair + 1) as j:
                    pair(j, j % (E // 2), (j + (E // 2 - 1)) % (E // 2))
            sp.wait_ge(lo_made, 12 * last_pair + lo_of(5))
            load_down(expert_slot(5), 1, E // 2 - 1)
            sp.wait_ge(lo_made, 12 * last_pair + (DENSE + 6))
            sp.dma_start(raw[:, 0, 0:D], rows[1:2, :].to_broadcast([P, D])).then_inc(final_loaded, 16)
            for t in range(TT):
                sp.wait_ge(out_made, t + 1)
                sp.dma_start(out[t * P:(t + 1) * P, :], x3[:, t, :]).then_inc(stored, 16)
            sp.wait_ge(stored, 16 * TT)

        @block.gpsimd
        def _(pool):
            for i in range(4):
                pool.wait_ge(glu_value, i + 1)
                pool.wait_ge(glu_gate, i + 1)
                nc.gpsimd.tensor_tensor(u_sb[:, 2 * i:2 * i + 2, :], u_sb[:, 2 * i:2 * i + 2, :],
                                        gate[:, 2 * i:2 * i + 2, :], ALU.mult).then_inc(u_ready, 1)

        def stage_of(n):
            name = UNITS[n // 2][0]
            g = UNITS[n // 2][2] % D // 512
            return name, 2 * g + n % 2

        @block.scalar
        def _(act):
            act.dma_start(x_sb[:, :, :], x.rearrange("(t p) d -> p t d", p=P)).then_inc(x_loaded, 16)
            act.dma_start(cst[:, :], consts).then_inc(cst_loaded, 16)
            act.dma_start(col[:, :], cols).then_inc(col_loaded, 16)
            act.dma_start(mem_sb[:, :, :], mem.rearrange("(t p) d -> p t d", p=P)).then_inc(mem_loaded, 16)
            act.dma_start(wr[:, :, :], w_route.rearrange("(k p) n -> p k n", p=P)).then_inc(wr_loaded, 16)
            act.dma_start(br[:, :], b_route.to_broadcast([P, GROUPS + E])).then_inc(wr_loaded, 16)

            def make_hi(N, slot, loaded, h, k_split):
                act.wait_ge(raw_loaded[slot], loaded)
                if isinstance(N, int) and N < CONV:
                    pass
                else:
                    act.wait_ge(half_used, N - (CONV - 1))
                return nc.scalar.activation(conv_half(hi, N if isinstance(N, int) else 0), raw_half(slot, h, k_split), ACT.Copy)

            def dense_hi(N):
                if N < DENSE:
                    slot, before_ = raw_slot(N // 2)
                    make_hi(N, slot, 16 * (before_ + 1), N % 2, UNITS[N // 2][0] in K_SPLIT).then_inc(hi_made, 1)
                else:
                    m = (N - DENSE) // 2
                    slot = expert_slot(m)
                    make_hi(N, slot, 16 * (RAW_BASE[slot] + 1 + m // RAW), N % 2, True).then_inc(hi_made, 1)

            act.wait_ge(x_loaded, 16)
            for t in range(TT):
                nc.scalar.activation(conv[:, 4 * t:4 * t + 4, :].rearrange("p a b -> p (a b)"), x_sb[:, t, :],
                                     ACT.Square, accum_out=stat[:, t:t + 1]).then_inc(sumsq, 1)
            act.wait_ge(meansq, 1)
            nc.scalar.activation(stat[:, 6:8], stat[:, 4:6], ACT.Sqrt).then_inc(root, 1)
            for N in range(2):
                dense_hi(N)
            act.wait_ge(col_loaded, 16)
            for c in range(KT):
                act.wait_ge(xT_turned, c // 2 + 1)
                nc.scalar.activation(inA[:, 0, c, :], ps[:, c // 2, (c % 2) * T:(c % 2 + 1) * T], ACT.Copy,
                                     scale=vec("mix_g", c)).then_inc(x_hi, 1)
            dense_hi(2)
            act.wait_ge(mem_loaded, 16)
            act.wait_ge(sumsq, 2)
            for t in range(TT):
                nc.scalar.activation(conv[:, 4 * t:4 * t + 4, :].rearrange("p a b -> p (a b)"), mem_sb[:, t, :],
                                     ACT.Square, accum_out=stat[:, 2 + t:3 + t]).then_inc(sumsq, 1)
            act.wait_ge(meansq, 2)
            nc.scalar.activation(stat[:, 10:12], stat[:, 8:10], ACT.Sqrt).then_inc(root, 1)

            def mem_parts(pair_):
                for c in (2 * pair_, 2 * pair_ + 1):
                    act.wait_ge(memT_turned, pair_ + 1)
                    nc.scalar.activation(inB[:, 0, c, :], ps[:, 6 + pair_ % 2, (c % 2) * T:(c % 2 + 1) * T],
                                         ACT.Copy, scale=vec("mem_g", c)).then_inc(mem_hi, 1)

            def softmax_exp(h):
                for t in range(TT):
                    act.wait_ge(score_max, h + 1)
                    nc.scalar.activation(probs[:, h, t, :], ps[:, 6 + h % 2, t * T:(t + 1) * T], ACT.Exp,
                                         bias=stat[:, 12 + t + 2 * (h % 2):13 + t + 2 * (h % 2)],
                                         scale=HEAD_DIM ** -0.5,
                                         accum_out=stat[:, 16 + t + 2 * (h % 2):17 + t + 2 * (h % 2)]).then_inc(exps, 1)

            def turned_probs(h):
                act.wait_ge(probs_turned, h + 1)
                nc.scalar.activation(probsT[:, h, :, :].rearrange("p a b -> p (a b)"), ps[:, 6 + h % 2, :],
                                     ACT.Copy).then_inc(probsT_made, 1)

            def attention_hi(h):
                act.wait_ge(attended, h + 1)
                nc.scalar.activation(inB[:, 0, 2 * h:2 * h + 2, :].rearrange("p a b -> p (a b)"),
                                     ps[:, 6 + h % 2, :], ACT.Copy).then_inc(att_hi, 1)

            def ln_squares():
                act.wait_ge(ln_centred, 1)
                nc.scalar.activation(u_sb[:, :, :], conv[:, :, :], ACT.Square).then_inc(ln_square, 1)

            def ln_sqrt():
                act.wait_ge(ln_var, 1)
                nc.scalar.activation(ln_rstd[:, :], ln_rstd[:, :], ACT.Sqrt).then_inc(ln_root, 1)

            def branch_b_act():
                act.wait_ge(ln_scaled, 1)
                for c in range(KT):
                    nc.scalar.activation(u_sb[:, c, :], conv[:, c, :], ACT.Silu, bias=vec("ln_b", c),
                                         scale=vec("ln_g", c)).then_inc(b_silu, 1)
                act.wait_ge(b_silu, KT)
                act.dma_start(x_again[:, :, :], x.rearrange("(t p) d -> p t d", p=P)).then_inc(xagain_loaded, 16)
                act.wait_ge(half_used, FIRST["out_x"] + 4)
                nc.scalar.activation(inB[:, 0, :, :], u_sb[:, :, :], ACT.Copy).then_inc(b_hi, 1)

            def load_ffn_row():
                act.wait_ge(half_used, FIRST["w_o"])
                act.dma_start(ffn_row[:, :], rows[0:1, :].to_broadcast([P, D])).then_inc(ffn_loaded, 16)

            F = FIRST
            extra = {F["q"] - 1: [lambda: mem_parts(0), lambda: mem_parts(1)],
                     F["q"] + 1: [lambda: mem_parts(2), lambda: mem_parts(3)],
                     F["v"] - 1: [lambda: softmax_exp(0), lambda: softmax_exp(1)],
                     F["v"] + 1: [lambda: softmax_exp(2), lambda: softmax_exp(3)],
                     F["v"] + 2: [lambda: turned_probs(0), lambda: turned_probs(1)],
                     F["v"] + 3: [lambda: turned_probs(2), lambda: turned_probs(3)],
                     F["gate2"]: [lambda: attention_hi(0), lambda: attention_hi(1)],
                     F["gate2"] + 1: [lambda: attention_hi(2), lambda: attention_hi(3)],
                     F["gate1"] - 1: [ln_squares], F["gate1"] + 1: [ln_sqrt, branch_b_act],
                     F["w_o"]: [load_ffn_row]}
            gates_done = 0
            for n in range(DENSE):
                name, q4 = stage_of(n)
                bank, b = ps[:, n % RING, :], n % RING
                two = slice(2 * q4, 2 * q4 + 2)
                if name in ("glu_value", "glu_gate", "gate0", "gate1", "gate2", "a_value", "q", "k"):
                    act.wait_ge(half_used, n + 1)
                if name in ("glu_value", "glu_gate"):
                    dst = u_sb if name == "glu_value" else gate
                    fn = ACT.Identity if name == "glu_value" else ACT.Sigmoid
                    for k in range(2):
                        last = nc.scalar.activation(dst[:, 2 * q4 + k, :], bank[:, k * T:(k + 1) * T], fn,
                                                    bias=vec("b_glu", 2 * q4 + k, int(name == "glu_gate")))
                    last.then_inc(bank_free[b], 1)
                    act.wait_ge(bank_free[b], n // RING + 1)
                    act.sem_inc(glu_value if name == "glu_value" else glu_gate, 1)
                elif name in ("gate0", "gate1", "gate2"):
                    if name == "gate0":
                        act.wait_ge(a_lo, 4)
                    elif name == "gate2":
                        act.wait_ge(merged_a, 4)
                    else:
                        act.wait_ge(merged_x, 4)
                    for k in range(2):
                        last = nc.scalar.activation(gate[:, 2 * q4 + k, :], bank[:, k * T:(k + 1) * T], ACT.Sigmoid,
                                                    bias=vec("b_gate", 2 * q4 + k, int(name[-1])))
                    last.then_inc(bank_free[b], 1)
                    act.wait_ge(bank_free[b], n // RING + 1)
                    act.sem_inc(gate_made, 1)
                elif name in ("a_value", "q", "k"):
                    dst, made = {"a_value": (a_mid, a_value), "q": (qT, q_made), "k": (kT, k_made)}[name]
                    nc.scalar.activation(dst[:, two, :].rearrange("p a b -> p (a b)"), bank, ACT.Copy).then_inc(made, 1)
                    act.wait_ge(made, q4 + 1)
                    act.sem_inc(bank_free[b], 1)
                elif name == "a_b":
                    act.wait_ge(a_prod, q4 + 1)
                    nc.scalar.activation(inB[:, 0, two, :], gate[:, two, :], ACT.Copy).then_inc(a_hi, 1)
                elif name == "v" and n % 2 == 1:
                    act.wait_ge(half_used, n + 1)
                    g = q4 // 2
                    for t in range(TT):
                        nc.scalar.activation(v_sb[:, t, 512 * g:512 * g + 512], ps[:, (n - 1 + t) % RING, :],
                                             ACT.Copy).then_inc(bank_free[(n - 1 + t) % RING], 1)
                    for t in range(TT):
                        act.wait_ge(bank_free[(n - 1 + t) % RING], n // RING + 1)
                    act.sem_inc(v_made, 1)
                elif name == "out_b":
                    act.wait_ge(merged_all, q4 + 1)
                    nc.scalar.activation(inA[:, 0, two, :], merged[:, two, :], ACT.Copy).then_inc(merged_hi, 1)
                for work in extra.get(n, ()):
                    work()
                dense_hi(n + 3)

            for t in range(TT):
                act.wait_ge(x2_made, 4)
                nc.scalar.activation(gate[:, 4 * t:4 * t + 4, :].rearrange("p a b -> p (a b)"), x2[:, t, :],
                                     ACT.Square, accum_out=stat[:, t:t + 1]).then_inc(sumsq, 1)
            act.wait_ge(meansq, 3)
            nc.scalar.activation(stat[:, 6:8], stat[:, 4:6], ACT.Sqrt).then_inc(root, 1)
            for t in range(TT):
                act.wait_ge(z_made, t + 1)
                nc.scalar.activation(z_parts[:, 0, t, :], z_sb[:, t, :], ACT.Copy).then_inc(z_hi, 1)
            for b2, bank in enumerate((0, 1, 6, 7)):
                act.wait_ge(zT_turned, b2 + 1)
                nc.scalar.activation(zT[:, 2 * b2:2 * b2 + 2, :].rearrange("p a b -> p (a b)"), ps[:, bank, :],
                                     ACT.Copy).then_inc(zT_made, 1)
            act.wait_ge(route_for_exp, 1)
            nc.scalar.activation(route[:, 80:88], route[:, 80:88], ACT.Exp).then_inc(route_exp, 1)
            act.wait_ge(route_for_exp, 2)
            nc.scalar.activation(route[:, 88:90], route[:, 88:90], ACT.Exp).then_inc(route_exp, 1)
            act.wait_ge(rank_turned, 2)
            nc.scalar.activation(rank_bf[0:E, :], ps[0:E, 0, 0:T], ACT.Copy).then_inc(rank_copied, 1)
            act.wait_ge(rank_copied, 1)
            act.dma_start(rank_dram, rank_bf[0:E, :]).then_inc(rank_stored, 16)
            act.wait_ge(rank_stored, 16)
            act.wait_ge(logits_done, 2)
            act.dma_start(rank_rows[:, :, :].rearrange("p e t -> p (e t)"),
                          rank_dram.rearrange("e t -> (e t)").rearrange("(a n) -> a n", a=1).to_broadcast([P, E * T]))\
                .then_inc(rank_rows_loaded, 16)

            def expert_xeT(i, par):
                act.wait_ge(gathered, i + 1)
                nc.scalar.activation(xeT[:, par, :, :].rearrange("p a b -> p (a b)"),
                                     ps[:, 6:8, :].rearrange("p a b -> p (a b)"), ACT.Copy).then_inc(xeT_made, 1)

            expert_xeT(0, 0)
            act.wait_ge(loops_made, 1)
            last_pair = nc.scalar.value_load(loops[0:1, 0:1], min_val=E // 2 - 1, max_val=MAX_ROUNDS * E // 2 - 1)

            def expert_hi(j, m0, k):
                m = m0 + k // 2
                slot = expert_slot(m)
                N0 = DENSE + 2 * m0 + k
                act.wait_ge(raw_loaded[slot], 16 * j + 16 * (RAW_BASE[slot] + 1 + m // RAW))
                act.wait_ge(half_used, 12 * j + (N0 - (CONV - 1)))
                nc.scalar.activation(conv_half(hi, N0), raw_half(slot, k % 2, True), ACT.Copy).then_inc(hi_made, 1)

            def y_out_hi(i, par):
                act.wait_ge(comb_slot_made, i + 1)
                nc.scalar.activation(y_parts[:, 0, :], ps[:, 6:8, :].rearrange("p a b -> p (a b)"), ACT.Copy,
                                     scale=comb_slot[:, par:par + 1]).then_inc(y_hi, 1)

            def step(j, r):
                first = isinstance(j, int)
                i = 2 * j + r
                m0 = 0 if first and i == 0 else 3 * r - 1
                done = 12 * j + (DENSE + 2 * m0 + 1)

                def more(k):
                    expert_hi(j, m0, k)
                start = first and i == 0
                if not start:
                    more(2)
                more(3)
                act.wait_ge(half_used, done + 1)
                if not start:
                    act.wait_ge(folded, i)
                nc.scalar.activation(gu_sb[:, 0:FF], G0, ACT.Copy).then_inc(gate_out, 1)
                more(4)
                expert_xeT(i + 1, (r + 1) % 2)
                more(5)
                act.wait_ge(half_used, done + 3)
                nc.scalar.activation(gu_sb[:, FF:2 * FF], G1, ACT.Copy).then_inc(up_out, 1)
                if not start:
                    more(6)
                    more(7)
                    act.wait_ge(half_used, done + 5)
                    y_out_hi(i - 1, (r + 1) % 2)
                act.wait_ge(folded, i + 1)
                if not start:
                    act.wait_ge(h_made, i)
                nc.scalar.activation(silu_sb[:, :, :], G1.rearrange("p (a b) -> p a b", b=SLOTS)[:, 0:4, :],
                                     ACT.Silu).then_inc(silu_made, 1)
                act.wait_ge(h_made, i + 1)
                nc.scalar.activation(hT[:, :, 0:SLOTS], h_sb[:, :, :], ACT.Copy).then_inc(h_hi, 1)

            step(0, 0)
            step(0, 1)
            with act.Fori(1, last_pair + 1) as j:
                step(j, 0)
                step(j, 1)
            act.wait_ge(half_used, 12 * last_pair + (DENSE + 12))
            y_out_hi(2 * last_pair + 1, 1)

            act.wait_ge(combined, 2 * last_pair + 2)
            for t in range(TT):
                nc.scalar.activation(gate[:, 4 * t:4 * t + 4, :].rearrange("p a b -> p (a b)"), sums(t),
                                     ACT.Square, accum_out=stat[:, t:t + 1]).then_inc(sumsq3, 1)
            act.wait_ge(meansq, 4)
            nc.scalar.activation(stat[:, 6:8], stat[:, 4:6], ACT.Sqrt).then_inc(root3, 1)

        @block.vector
        def _(dve):
            chain = [0]

            def link(ins):
                chain[0] += 1
                ins.then_inc(dve_chain, 1)
                dve.wait_ge(dve_chain, chain[0])

            def make_lo(N, slot, h, k_split):
                dve.wait_ge(hi_made, N + 1)
                nc.vector.tensor_tensor(conv_half(lo, N), raw_half(slot, h, k_split), conv_half(hi, N).bitcast(f32),
                                        ALU.subtract).then_inc(lo_made, 1)

            def dense_lo(N):
                if N < DENSE:
                    make_lo(N, raw_slot(N // 2)[0], N % 2, UNITS[N // 2][0] in K_SPLIT)
                else:
                    make_lo(N, expert_slot((N - DENSE) // 2), N % 2, True)

            def rstd(sums, mean, rooted, r, need, root_need, root_sem=root):
                dve.wait_ge(*need)
                nc.vector.tensor_scalar(stat[:, mean:mean + 2], stat[:, sums:sums + 2], 1.0 / D, EPS,
                                        ALU.mult, ALU.add).then_inc(meansq, 1)
                dve.wait_ge(root_sem, root_need)
                link(nc.vector.reciprocal(stat[:, r:r + 2], stat[:, rooted:rooted + 2]))

            rstd(0, 4, 6, 20, (sumsq, 2), 1)
            for t in range(TT):
                nc.vector.tensor_scalar(x_sb[:, t, :], x_sb[:, t, :], stat[:, 20 + t:21 + t], None,
                                        ALU.mult).then_inc(scaled, 1)
            dve.wait_ge(col_loaded, 16)
            for c in range(KT):
                dve.wait_ge(x_hi, c // 2 * 2 + 2)
                nc.vector.scalar_tensor_tensor(inA[:, 1, c, :], ps[:, c // 2, (c % 2) * T:(c % 2 + 1) * T],
                                               vec("mix_g", c), inA[:, 0, c, :].bitcast(f32), ALU.mult,
                                               ALU.subtract).then_inc(x_lo, 1)
            dense_lo(0)
            dense_lo(1)
            rstd(2, 8, 10, 22, (sumsq, 4), 2)
            for t in range(TT):
                nc.vector.tensor_scalar(mem_sb[:, t, :], mem_sb[:, t, :], stat[:, 22 + t:23 + t], None,
                                        ALU.mult).then_inc(scaled, 1)

            def mem_parts(pair_):
                for c in (2 * pair_, 2 * pair_ + 1):
                    dve.wait_ge(mem_hi, 2 * pair_ + 2)
                    nc.vector.scalar_tensor_tensor(inB[:, 1, c, :], ps[:, 6 + pair_ % 2, (c % 2) * T:(c % 2 + 1) * T],
                                                   vec("mem_g", c), inB[:, 0, c, :].bitcast(f32), ALU.mult,
                                                   ALU.subtract).then_inc(mem_lo, 1)

            def softmax_max(h):
                dve.wait_ge(scored, h + 1)
                if h >= 2:
                    dve.wait_ge(exps, 2 * (h - 1))
                m = stat[:, 12 + 2 * (h % 2):14 + 2 * (h % 2)]
                link(nc.vector.tensor_reduce(m, ps[:, 6 + h % 2, :].rearrange("p (t m) -> p t m", t=TT), AX.X,
                                             ALU.max, negate=True))
                nc.vector.tensor_scalar(m, m, HEAD_DIM ** -0.5, None, ALU.mult).then_inc(score_max, 1)

            def softmax_norm(h):
                dve.wait_ge(exps, 2 * h + 2)
                s = 16 + 2 * (h % 2)
                link(nc.vector.reciprocal(stat[:, s:s + 2], stat[:, s:s + 2]))
                for t in range(TT):
                    nc.vector.tensor_scalar(probs[:, h, t, :], probs[:, h, t, :], stat[:, s + t:s + t + 1], None,
                                            ALU.mult).then_inc(prob_made, 1)

            def attention_lo(h):
                dve.wait_ge(att_hi, h + 1)
                nc.vector.tensor_tensor(inB[:, 1, 2 * h:2 * h + 2, :].rearrange("p a b -> p (a b)"),
                                        ps[:, 6 + h % 2, :],
                                        inB[:, 0, 2 * h:2 * h + 2, :].rearrange("p a b -> p (a b)").bitcast(f32),
                                        ALU.subtract).then_inc(att_lo, 1)

            conv_done = [0]

            def conv_taps(count):
                for s in range(conv_done[0], min(conv_done[0] + count, TAPS_B * KT)):
                    shift, c = s // KT, s % KT
                    w = vec("conv_b", c, TAPS_B - 1 - shift)
                    if shift == 0:
                        dve.wait_ge(u_ready, c // 2 + 1)
                        nc.vector.tensor_scalar(conv[:, c, :], u_sb[:, c, :], w, vec("conv_b_b", c), ALU.mult,
                                                ALU.add).then_inc(conv_step, 1)
                    else:
                        dve.wait_ge(conv_step, s - KT + 1)
                        nc.vector.scalar_tensor_tensor(conv[:, c, shift:T], u_sb[:, c, 0:T - shift], w,
                                                       conv[:, c, shift:T], ALU.mult, ALU.add).then_inc(conv_step, 1)
                    conv_done[0] += 1

            def all_channels(a):
                return a.rearrange("p (o t) -> p o t", o=1).to_broadcast([P, KT, T])

            def ln_centre():
                dve.wait_ge(ln_sum, 1)
                link(nc.vector.tensor_scalar(ln_mean[:, :], ps[:, 6, 0:T], 1.0 / D, None, ALU.mult))
                nc.vector.tensor_tensor(conv[:, :, :], conv[:, :, :], all_channels(ln_mean[:, :]),
                                        ALU.subtract).then_inc(ln_centred, 1)

            def ln_variance():
                dve.wait_ge(ln_sumsq, 1)
                nc.vector.tensor_scalar(ln_rstd[:, :], ps[:, 7, 0:T], 1.0 / D, EPS, ALU.mult, ALU.add).then_inc(ln_var, 1)

            def ln_scale():
                dve.wait_ge(ln_root, 1)
                link(nc.vector.reciprocal(ln_mean[:, :], ln_rstd[:, :]))
                nc.vector.tensor_tensor(conv[:, :, :], conv[:, :, :], all_channels(ln_mean[:, :]),
                                        ALU.mult).then_inc(ln_scaled, 1)

            def branch_b_lo():
                dve.wait_ge(b_hi, 1)
                nc.vector.tensor_tensor(inB[:, 1, :, :], u_sb[:, :, :], inB[:, 0, :, :].bitcast(f32),
                                        ALU.subtract).then_inc(b_lo, 1)

            F = FIRST
            extra = {F["q"] - 1: [lambda: mem_parts(0), lambda: mem_parts(1)],
                     F["q"] + 1: [lambda: mem_parts(2), lambda: mem_parts(3)],
                     F["v"] - 1: [lambda: softmax_max(0), lambda: softmax_max(1), lambda: softmax_norm(0),
                                  lambda: softmax_norm(1)],
                     F["v"] + 1: [lambda: softmax_max(2), lambda: softmax_max(3), lambda: softmax_norm(2),
                                  lambda: softmax_norm(3)],
                     F["gate2"]: [lambda: attention_lo(0), lambda: attention_lo(1)],
                     F["gate2"] + 1: [lambda: attention_lo(2), lambda: attention_lo(3)],
                     F["gate1"] - 1: [ln_centre], F["gate1"] + 1: [ln_variance, ln_scale, branch_b_lo]}
            for n in range(DENSE):
                dense_lo(n + 2)
                name, q4 = stage_of(n)
                b = n % RING
                bank = ps[:, b, :]
                bank2 = bank.rearrange("p (a b) -> p a b", b=T)
                two = slice(2 * q4, 2 * q4 + 2)
                if name in ("a_c", "a_b", "out_a", "out_x", "out_b"):
                    dve.wait_ge(half_used, n + 1)
                if name == "a_c":
                    dve.wait_ge(a_value, q4 + 1)
                    nc.vector.tensor_tensor(a_mid[:, two, :], bank2, a_mid[:, two, :], ALU.mult).then_inc(bank_free[b], 1)
                    dve.wait_ge(bank_free[b], n // RING + 1)
                    dve.wait_ge(u_ready, 4)
                    for c in (2 * q4, 2 * q4 + 1):
                        nc.vector.tensor_scalar(gate[:, c, :], a_mid[:, c, :], vec("conv_a", c, TAPS_A - 1), None,
                                                ALU.mult).then_inc(a_cv, 1)
                    for shift in range(1, TAPS_A):
                        for c in (2 * q4, 2 * q4 + 1):
                            dve.wait_ge(a_cv, 2 * TAPS_A * q4 + 2 * (shift - 1) + c % 2 + 1)
                            nc.vector.scalar_tensor_tensor(gate[:, c, shift:T], a_mid[:, c, 0:T - shift],
                                                           vec("conv_a", c, TAPS_A - 1 - shift),
                                                           gate[:, c, shift:T], ALU.mult, ALU.add).then_inc(a_cv, 1)
                elif name == "a_b":
                    dve.wait_ge(a_cv, 2 * TAPS_A * (q4 + 1))
                    nc.vector.tensor_tensor(gate[:, two, :], bank2, gate[:, two, :], ALU.mult).then_inc(a_prod, 1)
                    dve.wait_ge(a_prod, q4 + 1)
                    dve.sem_inc(bank_free[b], 1)
                    dve.wait_ge(a_hi, q4 + 1)
                    nc.vector.tensor_tensor(inB[:, 1, two, :], gate[:, two, :], inB[:, 0, two, :].bitcast(f32),
                                            ALU.subtract).then_inc(a_lo, 1)
                elif name == "out_a":
                    dve.wait_ge(gate_made, q4 + 1)
                    nc.vector.tensor_tensor(merged[:, two, :], bank2, gate[:, two, :], ALU.mult).then_inc(merged_a, 1)
                    dve.wait_ge(merged_a, q4 + 1)
                    dve.sem_inc(bank_free[b], 1)
                elif name == "out_x":
                    dve.wait_ge(gate_made, 4 + q4 + 1)
                    link(nc.vector.tensor_tensor(part[:, :, :], bank2, gate[:, two, :], ALU.mult))
                    dve.sem_inc(bank_free[b], 1)
                    nc.vector.tensor_tensor(merged[:, two, :], merged[:, two, :], part[:, :, :], ALU.add).then_inc(merged_x, 1)
                    dve.wait_ge(merged_x, q4 + 1)
                elif name == "out_b":
                    dve.wait_ge(gate_made, 8 + q4 + 1)
                    for k in range(2):
                        c = 2 * q4 + k
                        link(nc.vector.scalar_tensor_tensor(part[:, k, :], bank2[:, k, :], vec("b_out", c),
                                                            gate[:, c, :], ALU.add, ALU.mult))
                    dve.sem_inc(bank_free[b], 1)
                    nc.vector.tensor_tensor(merged[:, two, :], merged[:, two, :], part[:, :, :], ALU.add).then_inc(merged_all, 1)
                    dve.wait_ge(merged_hi, q4 + 1)
                    nc.vector.tensor_tensor(inA[:, 1, two, :], merged[:, two, :], inA[:, 0, two, :].bitcast(f32),
                                            ALU.subtract).then_inc(merged_lo, 1)
                elif name == "w_o" and n % 2 == 1:
                    dve.wait_ge(half_used, n + 1)
                    dve.wait_ge(xagain_loaded, 16)
                    dve.wait_ge(merged_lo, 4)
                    g = q4 // 2
                    for t in range(TT):
                        nc.vector.tensor_tensor(x2[:, t, 512 * g:512 * g + 512], ps[:, (n - 1 + t) % RING, :],
                                                x_again[:, t, 512 * g:512 * g + 512], ALU.add).then_inc(x2_made, 1)
                for work in extra.get(n, ()):
                    work()
                if n >= F["a_value"] and n < F["gate1"] - 2:
                    conv_taps(7)
                if n == F["gate1"] - 3:
                    conv_taps(TAPS_B * KT)

            rstd(0, 4, 6, 20, (sumsq, 6), 3)
            dve.wait_ge(ffn_loaded, 16)
            for t in range(TT):
                nc.vector.scalar_tensor_tensor(z_sb[:, t, :], x2[:, t, :], stat[:, 20 + t:21 + t], ffn_row[:, :],
                                               ALU.mult, ALU.mult).then_inc(z_made, 1)
            for t in range(TT):
                dve.wait_ge(z_hi, t + 1)
                nc.vector.tensor_tensor(z_parts[:, 1, t, :], z_sb[:, t, :], z_parts[:, 0, t, :].bitcast(f32),
                                        ALU.subtract).then_inc(z_lo, 1)

            def r_(a, *shape):
                n = 1
                for s in shape:
                    n *= s
                v = route[:, a:a + n]
                return v if len(shape) == 1 else v.rearrange("p (a b) -> p a b", b=shape[-1])

            NL = GROUPS + E
            logit = r_(0, TT, NL)
            g_max, g_exp, diff, p_g, w1, w2 = (r_(72, TT), r_(80, TT, GROUPS), r_(88, TT), r_(90, TT),
                                               r_(92, TT), r_(94, TT))
            g_hot, e_masked, e1, e2, tmp, m1, m2 = (r_(96, TT, GROUPS), r_(104, TT, E), r_(168, TT, E),
                                                    r_(232, TT, E), r_(296, TT, E), r_(74, TT), r_(76, TT))
            member, weight, rank, low = r_(360, TT, E), r_(424, TT, E), r_(488, TT, E), r_(78, TT)

            def wide(a, n):
                return a.rearrange("p (t o) -> p t o", o=1).to_broadcast([P, TT, n])

            def first_hot(hot, values, top, desc, n):
                link(nc.vector.tensor_reduce(top, values, AX.X, ALU.max))
                link(nc.vector.tensor_tensor(hot, values, wide(top, n), ALU.is_equal))
                link(nc.vector.tensor_tensor(hot, hot, desc.rearrange("p (o n) -> p o n", o=1).to_broadcast([P, TT, n]),
                                             ALU.mult))
                link(nc.vector.tensor_reduce(low, hot, AX.X, ALU.max))
                link(nc.vector.tensor_tensor(hot, hot, wide(low, n), ALU.is_equal))

            dve.wait_ge(logits_done, 2)
            for t in range(TT):
                link(nc.vector.tensor_tensor(logit[:, t, :], ps[:, 2, 64 * t:64 * t + NL], br[:, :], ALU.add))
            first_hot(g_hot, logit[:, :, 0:GROUPS], g_max, c_("desc_g"), GROUPS)
            nc.vector.tensor_tensor(g_exp, logit[:, :, 0:GROUPS], wide(g_max, GROUPS), ALU.subtract).then_inc(route_for_exp, 1)
            link(nc.vector.tensor_scalar(g_hot, g_hot, -1.0, BIG, ALU.add, ALU.mult))
            for t in range(TT):
                link(nc.vector.tensor_tensor(e_masked[:, t, :].rearrange("p (g e) -> p g e", e=EPG),
                                             logit[:, t, GROUPS:NL].rearrange("p (g e) -> p g e", e=EPG),
                                             g_hot[:, t, :].rearrange("p (g o) -> p g o", o=1).to_broadcast([P, GROUPS, EPG]),
                                             ALU.add))
            first_hot(e1, e_masked, m1, c_("desc_e"), E)
            link(nc.vector.tensor_scalar(tmp, e1, -4.0 * BIG, None, ALU.mult))
            link(nc.vector.tensor_tensor(e_masked, e_masked, tmp, ALU.add))
            first_hot(e2, e_masked, m2, c_("desc_e"), E)
            nc.vector.tensor_tensor(diff, m2, m1, ALU.subtract).then_inc(route_for_exp, 1)
            nc.vector.tensor_tensor(member, e1, e2, ALU.add).then_inc(member_made, 1)
            dve.wait_ge(route_exp, 1)
            link(nc.vector.tensor_reduce(p_g, g_exp, AX.X, ALU.add))
            link(nc.vector.reciprocal(p_g, p_g))
            dve.wait_ge(route_exp, 2)
            link(nc.vector.tensor_scalar(w1, diff, 1.0, None, ALU.add))
            link(nc.vector.reciprocal(w1, w1))
            link(nc.vector.tensor_tensor(w2, diff, w1, ALU.mult))
            link(nc.vector.tensor_tensor(w1, w1, p_g, ALU.mult))
            link(nc.vector.tensor_tensor(w2, w2, p_g, ALU.mult))
            dve.wait_ge(ranked, 1)
            rk = ps[:, 3, 0:2 * E].rearrange("p (t e) -> p t e", e=E)
            link(nc.vector.scalar_tensor_tensor(rank, rk, 1.0, member, ALU.add, ALU.mult))
            link(nc.vector.tensor_scalar(rank, rank, -1.0, None, ALU.add))
            for r in range(MAX_ROUNDS + 1):
                ins = nc.vector.tensor_scalar(rank_tab[:, :, r * E:(r + 1) * E], rank, -float(SLOTS * r), None, ALU.add)
                if r == MAX_ROUNDS:
                    ins.then_inc(rank_made, 1)
            link(nc.vector.tensor_reduce(stat[:, 12:13], ps[:, 3, 2 * E:3 * E], AX.X, ALU.max))
            link(nc.vector.tensor_scalar(stat[:, 13:14], stat[:, 12:13], float(SLOTS), float(E // 2), ALU.is_gt, ALU.mult))
            for r in range(2, MAX_ROUNDS):
                link(nc.vector.tensor_scalar(stat[:, 14:15], stat[:, 12:13], float(SLOTS * r), float(E // 2), ALU.is_gt, ALU.mult))
                link(nc.vector.tensor_tensor(stat[:, 13:14], stat[:, 13:14], stat[:, 14:15], ALU.add))
            nc.vector.tensor_scalar(loops[:, 0:1], stat[:, 13:14], float(E // 2 - 1), None, ALU.add).then_inc(loops_made, 1)
            link(nc.vector.tensor_tensor(weight, e1, wide(w1, E), ALU.mult))
            link(nc.vector.tensor_tensor(tmp, e2, wide(w2, E), ALU.mult))
            link(nc.vector.tensor_tensor(weight, weight, tmp, ALU.add))
            link(nc.vector.tensor_copy(comb[:, :, :, 0], weight))
            nc.vector.tensor_tensor(comb[:, :, :, 1], weight, comb[:, :, :, 0].bitcast(f32), ALU.subtract).then_inc(comb_made, 1)

            def make_pick(par, i):
                for t in range(TT):
                    ins = nc.vector.tensor_scalar(pick[:, par, t, :], c_("slot_row"), rank_tab[:, t, i], None, ALU.is_equal)
                ins.then_inc(pick_made, 1)

            dve.wait_ge(rank_made, 1)
            make_pick(0, slice(0, 1))
            make_pick(1, slice(1, 2))
            dve.wait_ge(loops_made, 1)
            last_pair = nc.vector.value_load(loops[0:1, 0:1], min_val=E // 2 - 1, max_val=MAX_ROUNDS * E // 2 - 1)

            def expert_lo(j, m0, k):
                m = m0 + k // 2
                N0 = DENSE + 2 * m0 + k
                dve.wait_ge(hi_made, 12 * j + (N0 + 1))
                nc.vector.tensor_tensor(conv_half(lo, N0), raw_half(expert_slot(m), k % 2, True),
                                        conv_half(hi, N0).bitcast(f32), ALU.subtract).then_inc(lo_made, 1)

            def y_out_lo(i, par):
                dve.wait_ge(y_hi, i + 1)
                nc.vector.scalar_tensor_tensor(y_parts[:, 1, :], ps[:, 6:8, :].rearrange("p a b -> p (a b)"),
                                               comb_slot[:, par:par + 1], y_parts[:, 0, :].bitcast(f32),
                                               ALU.mult, ALU.subtract).then_inc(y_lo, 1)

            def step(j, r, put_of):
                first = isinstance(j, int)
                i = 2 * j + r
                start = first and i == 0
                m0 = 0 if start else 3 * r - 1
                expert_lo(j, m0, 2)
                expert_lo(j, m0, 3)
                if not start:
                    if first:
                        dve.wait_ge(rank_rows_loaded, 16)
                    else:
                        dve.wait_ge(combined, i - 1)
                    e_col, t_col = put_of
                    nc.vector.tensor_scalar(put[:, :], rank_rows[:, e_col, :].rearrange("p o t -> p (o t)"),
                                            c_("slot_col")[:, t_col], None, ALU.is_equal).then_inc(put_made, 1)
                expert_lo(j, m0, 4)
                expert_lo(j, m0, 5)
                dve.wait_ge(slotted, i + 1)
                nc.vector.tensor_reduce(comb_slot[:, r:r + 1], G0[:, 0:2], AX.X, ALU.add).then_inc(comb_slot_made, 1)
                make_pick(r, slice(r + 2, r + 3) if first else bass.ds(2 * j + (r + 2), 1))
                if not start:
                    expert_lo(j, m0, 6)
                    y_out_lo(i - 1, (r + 1) % 2)
                    expert_lo(j, m0, 7)
                dve.wait_ge(silu_made, i + 1)
                nc.vector.tensor_tensor(h_sb[:, :, :], silu_sb[:, :, :],
                                        G1.rearrange("p (a b) -> p a b", b=SLOTS)[:, 4:8, :], ALU.mult).then_inc(h_made, 1)
                dve.wait_ge(h_hi, i + 1)
                nc.vector.tensor_tensor(hT[:, :, SLOTS:2 * SLOTS], h_sb[:, :, :], hT[:, :, 0:SLOTS].bitcast(f32),
                                        ALU.subtract).then_inc(h_lo, 1)

            dve.wait_ge(comb_made, 1)
            step(0, 0, None)
            step(0, 1, (slice(0, 1), slice(0, 1)))
            with dve.Fori(1, last_pair + 1) as j:
                step(j, 0, (bass.ds((j + (E // 2 - 1)) % (E // 2) * 2 + 1, 1), bass.ds(2 * j - 1, 1)))
                step(j, 1, (bass.ds(j % (E // 2) * 2, 1), bass.ds(2 * j, 1)))
            y_out_lo(2 * last_pair + 1, 1)
            dve.wait_ge(combined, 2 * last_pair + 1)
            nc.vector.tensor_scalar(put[:, :], rank_rows[:, E - 1, :], c_("slot_col")[:, bass.ds(2 * last_pair + 1, 1)],
                                    None, ALU.is_equal).then_inc(put_made, 1)

            rstd(0, 4, 6, 20, (sumsq3, 2), 1, root3)
            dve.wait_ge(final_loaded, 16)
            for t in range(TT):
                nc.vector.scalar_tensor_tensor(x3[:, t, :], sums(t), stat[:, 20 + t:21 + t], raw[:, 0, 0:D],
                                               ALU.mult, ALU.mult).then_inc(out_made, 1)

        @block.tensor
        def _(pe):
            mm = nc.tensor.matmul
            pe.wait_ge(cst_loaded, 16)

            def turn(dst_bank, src, need, done):
                for k in range(2):
                    for t in range(TT):
                        last = nc.tensor.transpose(ps[:, dst_bank, k * T + t * P:k * T + (t + 1) * P], src(t, k), ident)
                last.then_inc(done, 1)

            pe.wait_ge(scaled, 2)
            for c2 in range(4):
                turn(c2, lambda t, k: x_sb[:, t, (2 * c2 + k) * P:(2 * c2 + k + 1) * P], None, xT_turned)

            def columns(N, acts):
                w_hi, w_lo = conv_half(hi, N), conv_half(lo, N)
                for c in range(2):
                    dst = ps[:, N % RING, c * T:(c + 1) * T]
                    for k in range(KT):
                        mm(dst, w_hi[:, k, c * P:(c + 1) * P], acts[:, 0, k, :], start=(k == 0), stop=False)
                        mm(dst, w_hi[:, k, c * P:(c + 1) * P], acts[:, 1, k, :], start=False, stop=False)
                        last = mm(dst, w_lo[:, k, c * P:(c + 1) * P], acts[:, 0, k, :], start=False, stop=(k == KT - 1))
                last.then_inc(half_used, 1)

            def contraction(N, acts):
                h = N % 2
                w_hi = hi[:, N % CONV, :].rearrange("p (k n) -> p k n", n=512)
                w_lo = lo[:, N % CONV, :].rearrange("p (k n) -> p k n", n=512)
                for t in range(TT):
                    dst = ps[:, (N - h + t) % RING, :]
                    for k in range(4):
                        tok = slice(t * P, (t + 1) * P)
                        first, end = h == 0 and k == 0, h == 1 and k == 3
                        mm(dst, acts[:, 0, 4 * h + k, tok], w_hi[:, k, :], start=first, stop=False, skip_group_check=True)
                        mm(dst, acts[:, 1, 4 * h + k, tok], w_hi[:, k, :], start=False, stop=False, skip_group_check=True)
                        last = mm(dst, acts[:, 0, 4 * h + k, tok], w_lo[:, k, :], start=False, stop=end, skip_group_check=True)
                last.then_inc(half_used, 1)

            pe.wait_ge(x_lo, KT)
            for N in range(RING):
                pe.wait_ge(lo_made, N + 1)
                columns(N, inA)
            with pe.Fori(1, 2 * LOOPED // RING) as it:
                for b in range(RING):
                    pe.wait_ge(lo_made, RING * it + (b + 1))
                    pe.wait_ge(bank_free[b], it)
                    columns(b, inA)

            def scores(h):
                pe.wait_ge(q_made, h // 2 * 2 + 2)
                pe.wait_ge(k_made, h // 2 * 2 + 2)
                if h < 2:
                    pe.wait_ge(mem_lo, KT)
                else:
                    pe.wait_ge(exps, 2 * (h - 1))
                for t in range(TT):
                    for c in range(2):
                        last = mm(ps[:, 6 + h % 2, t * T:(t + 1) * T], qT[:, 2 * h + c, t * P:(t + 1) * P],
                                  kT[:, 2 * h + c, :], start=(c == 0), stop=(c == 1))
                last.then_inc(scored, 1)

            def turn_probs(h):
                pe.wait_ge(prob_made, 2 * h + 2)
                if h < 2:
                    pe.wait_ge(exps, 2 * (h + 2) + 2)
                else:
                    pe.wait_ge(probsT_made, h - 1)
                for m in range(TT):
                    for t in range(TT):
                        last = nc.tensor.transpose(ps[:, 6 + h % 2, m * T + t * P:m * T + (t + 1) * P],
                                                   probs[:, h, t, m * P:(m + 1) * P], ident)
                last.then_inc(probs_turned, 1)

            def attend(h):
                pe.wait_ge(v_made, h // 2 + 1)
                pe.wait_ge(probsT_made, 4 if h < 2 else 4)
                if h >= 2:
                    pe.wait_ge(att_lo, h - 1)
                for c in range(2):
                    for m in range(TT):
                        last = mm(ps[:, 6 + h % 2, c * T:(c + 1) * T],
                                  v_sb[:, m, (2 * h + c) * P:(2 * h + c + 1) * P], probsT[:, h, m, :],
                                  start=(m == 0), stop=(m == TT - 1))
                last.then_inc(attended, 1)

            def mem_turn(c2):
                if c2 >= 2:
                    pe.wait_ge(mem_lo, 2 * (c2 - 2) + 2)
                turn(6 + c2 % 2, lambda t, k: mem_sb[:, t, (2 * c2 + k) * P:(2 * c2 + k + 1) * P], None, memT_turned)

            def channel_sum(bank, src, need, done):
                pe.wait_ge(*need)
                for c in range(KT):
                    last = mm(ps[:, bank, 0:T], ones, src[:, c, :], start=(c == 0), stop=(c == KT - 1))
                last.then_inc(done, 1)

            F = FIRST
            extra = {F["q"] - 1: [lambda: pe.wait_ge(scaled, 4), lambda: mem_turn(0), lambda: mem_turn(1)],
                     F["q"] + 1: [lambda: mem_turn(2), lambda: mem_turn(3)],
                     F["v"] - 1: [lambda: scores(0), lambda: scores(1)],
                     F["v"] + 1: [lambda: scores(2), lambda: scores(3)],
                     F["v"] + 2: [lambda: turn_probs(0), lambda: turn_probs(1)],
                     F["v"] + 3: [lambda: turn_probs(2), lambda: turn_probs(3)],
                     F["gate2"]: [lambda: attend(0), lambda: attend(1)],
                     F["gate2"] + 1: [lambda: attend(2), lambda: attend(3)],
                     F["gate1"] - 2: [lambda: channel_sum(6, conv, (conv_step, TAPS_B * KT), ln_sum)],
                     F["gate1"]: [lambda: channel_sum(7, u_sb, (ln_square, 1), ln_sumsq)]}
            ready = {F["out_a"]: (a_lo, 4), F["k"]: (mem_lo, KT), F["out_x"]: (att_lo, HEADS),
                     F["out_b"]: (b_lo, 1), F["w_o"]: (merged_lo, 4)}
            for N in range(2 * LOOPED, DENSE):
                name = UNITS[N // 2][0]
                if N in ready:
                    pe.wait_ge(*ready[N])
                acts = inB if name in ("out_a", "k", "v", "out_x", "out_b") else inA
                pe.wait_ge(lo_made, N + 1)
                if name in K_SPLIT:
                    if N % 2 == 0:
                        for t in range(TT):
                            pe.wait_ge(bank_free[(N + t) % RING], N // RING)
                    contraction(N, acts)
                else:
                    pe.wait_ge(bank_free[N % RING], N // RING)
                    columns(N, acts)
                for work in extra.get(N, ()):
                    work()

            pe.wait_ge(z_made, 2)
            for b2, bank in enumerate((0, 1, 6, 7)):
                turn(bank, lambda t, k: z_sb[:, t, (2 * b2 + k) * P:(2 * b2 + k + 1) * P], None, zT_turned)
            pe.wait_ge(wr_loaded, 32)
            pe.wait_ge(zT_made, 4)
            NL = GROUPS + E
            for t in range(TT):
                for c in range(KT):
                    last = mm(ps[:, 2, 64 * t:64 * t + NL], zT[:, c, t * P:(t + 1) * P], wr[:, c, :],
                              start=(c == 0), stop=(c == KT - 1))
                last.then_inc(logits_done, 1)
            pe.wait_ge(member_made, 1)
            member = route[:, 360:360 + TT * E].rearrange("p (t e) -> p t e", e=E)
            mm(ps[:, 3, 0:E], before, member[:, 0, :], start=True, stop=True)
            mm(ps[:, 3, E:2 * E], ones, member[:, 0, :], start=True, stop=False)
            mm(ps[:, 3, E:2 * E], before, member[:, 1, :], start=False, stop=True)
            mm(ps[:, 3, 2 * E:3 * E], ones, member[:, 0, :], start=True, stop=False)
            mm(ps[:, 3, 2 * E:3 * E], ones, member[:, 1, :], start=False, stop=True).then_inc(ranked, 1)
            pe.wait_ge(rank_made, 1)
            rank = route[:, 488:488 + TT * E].rearrange("p (t e) -> p t e", e=E)
            for t in range(TT):
                nc.tensor.transpose(ps[0:E, 0, t * P:(t + 1) * P], rank[:, t, :], ident).then_inc(rank_turned, 1)

            def gather(i, par):
                pe.wait_ge(pick_made, i + 1)
                for c in range(KT):
                    for part_ in range(2):
                        col0 = (c * 2 + part_) * SLOTS
                        dst = ps[:, 6 + col0 // 512, col0 % 512:col0 % 512 + SLOTS]
                        for t in range(TT):
                            last = mm(dst, z_parts[:, part_, t, c * P:(c + 1) * P], pick[:, par, t, 0:SLOTS],
                                      start=(t == 0), stop=(t == TT - 1))
                last.then_inc(gathered, 1)

            def gate_or_up(j, m0, k, par):
                N = DENSE + 2 * m0 + k
                pe.wait_ge(lo_made, 12 * j + (N + 1))
                dst = G0 if k < 2 else G1
                for kt in range(4):
                    for w in (hi, lo):
                        last = mm(dst, xeT[:, par, 4 * (k % 2) + kt, :], w[:, N % CONV, kt * 512:(kt + 1) * 512],
                                  start=(k % 2 == 0 and kt == 0 and w is hi),
                                  stop=(k % 2 == 1 and kt == 3 and w is lo), skip_group_check=True)
                last.then_inc(half_used, 1)

            def down(j, m0, k, h):
                N = DENSE + 2 * m0 + k
                pe.wait_ge(lo_made, 12 * j + (N + 1))
                for kt in range(2):
                    for w in (hi, lo):
                        for g in range(2):
                            a = kt * D + g * 512
                            last = mm(DN[g], hT[:, 2 * h + kt, :], w[:, N % CONV, a:a + 512],
                                      start=(h == 0 and kt == 0 and w is hi),
                                      stop=(h == 1 and kt == 1 and w is lo), skip_group_check=True)
                last.then_inc(half_used, 1)

            def combine(i):
                pe.wait_ge(put_made, i + 1)
                pe.wait_ge(y_lo, i + 1)
                for t in range(TT):
                    for part_ in range(2):
                        for g in range(2):
                            last = mm(Y[2 * t + g], put[:, t * P:(t + 1) * P], y_parts[:, part_, g * 512:(g + 1) * 512],
                                      start=False, stop=False, skip_group_check=True)
                last.then_inc(combined, 1)

            pe.wait_ge(z_lo, 2)
            gather(0, 0)
            pe.wait_ge(rank_copied, 1)
            pe.wait_ge(loops_made, 1)
            pe.wait_ge(comb_made, 1)
            last_pair = nc.tensor.value_load(loops[0:1, 0:1], min_val=E // 2 - 1, max_val=MAX_ROUNDS * E // 2 - 1)
            for b in range(4):
                g = b % 2
                mm(Y[b], ident, x2[:, b // 2, g * 512:(g + 1) * 512], start=True, stop=False, skip_group_check=True)

            def step(j, r, e_col):
                first = isinstance(j, int)
                i = 2 * j + r
                start = first and i == 0
                m0 = 0 if start else 3 * r - 1
                pe.wait_ge(xeT_made, i + 1)
                if not start:
                    pe.wait_ge(comb_slot_made, i)
                gate_or_up(j, m0, 0, r)
                gate_or_up(j, m0, 1, r)
                if not first:
                    combine(i - 2)
                gather(i + 1, (r + 1) % 2)
                if not start:
                    pe.wait_ge(h_made, i)
                gate_or_up(j, m0, 2, r)
                gate_or_up(j, m0, 3, r)
                pe.wait_ge(gate_out, i + 1)
                for t in range(TT):
                    last = mm(G0[:, 0:2], pick[:, r, t, :], comb[:, t, e_col, :].rearrange("p a b -> p (a b)"),
                              start=(t == 0), stop=(t == TT - 1), skip_group_check=True)
                last.then_inc(slotted, 1)
                if not start:
                    pe.wait_ge(xeT_made, i + 2)
                    pe.wait_ge(h_lo, i)
                    down(j, m0, 4, 0)
                    down(j, m0, 5, 1)
                pe.wait_ge(up_out, i + 1)
                for f in range(2 * FF // P):
                    last = mm(G1[:, f * SLOTS:(f + 1) * SLOTS], gu_sb[:, f * P:(f + 1) * P], fold,
                              start=True, stop=True, skip_group_check=True)
                last.then_inc(folded, 1)

            step(0, 0, slice(0, 1))
            step(0, 1, slice(1, 2))
            with pe.Fori(1, last_pair + 1) as j:
                step(j, 0, bass.ds(j % (E // 2) * 2, 1))
                step(j, 1, bass.ds(j % (E // 2) * 2 + 1, 1))
            combine(2 * last_pair)
            pe.wait_ge(xeT_made, 2 * last_pair + 3)
            pe.wait_ge(h_lo, 2 * last_pair + 2)
            down(last_pair, 5, 0, 0)
            down(last_pair, 5, 1, 1)
            combine(2 * last_pair + 1)


def kernel(x, mem, mix_norm_g, mem_norm_g, w_in, b_gate, conv_a_w, w_out_a, b_glu,
           conv_b_w, conv_b_b, ln_b_g, ln_b_b, w_out_b, b_out_b, w_kv, w_out_x, w_o,
           ffn_norm_g, w_group, b_group, w_router, b_router, w_gate_up, w_down, final_norm_g):
    import numpy as np
    import concourse.bacc as bacc
    from concourse.bass_utils import run_bass_kernel_spmd as run

    def per_channel(v):
        return np.asarray(v).reshape(-1, P).T

    consts = np.zeros((P, N_CST), np.float32)

    def put_const(name, values):
        consts[:, CST[name][0]:CST[name][1]] = values

    put_const("ident", np.eye(P))
    put_const("ones", 1.0)
    put_const("before", np.triu(np.ones((P, P)), 1))
    put_const("fold", np.concatenate([np.eye(SLOTS), np.eye(SLOTS)]))
    put_const("slot_row", np.arange(P) % SLOTS)
    put_const("slot_col", np.arange(P)[:, None] % SLOTS + SLOTS * (np.arange(MAX_ROUNDS * E)[None, :] // E))
    put_const("desc_g", np.arange(GROUPS, 0, -1))
    put_const("desc_e", np.arange(E, 0, -1))
    vectors = (mix_norm_g, mem_norm_g, b_gate, b_glu, conv_a_w, conv_b_w, conv_b_b, ln_b_g, ln_b_b, b_out_b)
    arrays = {
        "x": x[0], "mem": mem[0], "w_in": w_in[0], "w_out_a": w_out_a[0], "w_out_b": w_out_b[0],
        "w_out_x": w_out_x[0], "w_kv": w_kv[0], "w_o": w_o[0], "w_gate_up": w_gate_up[0], "w_down": w_down[0],
        "w_route": np.concatenate([w_group[0], w_router[0]], axis=1),
        "cols": np.concatenate([per_channel(v[0]) for v in vectors], axis=1),
        "rows": np.stack([np.asarray(ffn_norm_g[0]), np.asarray(final_norm_g)]),
        "b_route": np.concatenate([b_group[0], b_router[0]])[None, :],
        "consts": consts,
    }
    nc = bacc.Bacc("TRN2", target_bir_lowering=False, num_devices=1, dynamic_dma_scratch_size=1024)
    feeds, args = {}, []
    for name, a in arrays.items():
        a = np.ascontiguousarray(a)
        feeds[f"in_{name}"] = a
        args.append(nc.dram_tensor(f"in_{name}", a.shape, mybir.dt.from_np(a.dtype), kind="ExternalInput").ap())
    out = nc.dram_tensor("out", (T, D), f32, kind="ExternalOutput").ap()
    hybrid_moe_kernel(nc, *args, out)
    return run(nc, [feeds], core_ids=[0]).results[0]["out"].reshape(1, T, D)
```

```python
import concourse.bass as bass
from concourse import mybir
from contextlib import ExitStack

D = 1024
T = 256
P = 128
KT = D // P
TT = T // P
HEADS = 4
HEAD_DIM = D // HEADS
TAPS_A = 3
TAPS_B = 31
GROUPS = 4
EPG = 8
E = GROUPS * EPG
FF = 512
EPS = 1e-6
SLOTS = 64
MAX_ROUNDS = T // SLOTS
HALF = 2048
UNIT = 2 * HALF
RAW = 6
RAW_DENSE = 4
CONV = 3
BIG = 1.0e30

COL = {}
_at = 0
for _name, _n in (("mix_g", 1), ("mem_g", 1), ("b_gate", 3), ("b_glu", 2), ("conv_a", TAPS_A),
                  ("conv_b", TAPS_B), ("conv_b_b", 1), ("ln_g", 1), ("ln_b", 1), ("b_out", 1), ("ffn_g", 1)):
    COL[_name] = _at
    _at += _n * KT
N_COLS = _at

CST = {}
_at = 0
for _name, _n in (("ident", P), ("ones", P), ("before", P), ("fold", SLOTS), ("slot_row", P),
                  ("slot_col", MAX_ROUNDS * E), ("desc_g", GROUPS), ("desc_e", E)):
    CST[_name] = (_at, _at + _n)
    _at += _n
N_CST = _at

UNITS = []
for _g in range(2):
    UNITS += [("glu_value", "w_in", 3 * D + 512 * _g), ("glu_gate", "w_in", 4 * D + 512 * _g)]
for _g in range(2):
    UNITS += [("a_value", "w_in", 512 * _g), ("a_c", "w_in", 2 * D + 512 * _g), ("a_b", "w_in", D + 512 * _g)]
for _name, _m, _c in (("gate0", "w_in", 6 * D), ("out_a", "w_out_a", 0), ("q", "w_in", 5 * D),
                      ("k", "w_kv", 0), ("v", "w_kv", D), ("gate2", "w_in", 8 * D),
                      ("out_x", "w_out_x", 0), ("gate1", "w_in", 7 * D), ("out_b", "w_out_b", 0),
                      ("w_o", "w_o", 0)):
    UNITS += [(_name, _m, _c + 512 * _g) for _g in range(2)]
N_UNITS = len(UNITS)
DENSE = 2 * N_UNITS
FIRST = {}
for _u, (_name, _, _) in enumerate(UNITS):
    FIRST.setdefault(_name, 2 * _u)
K_SPLIT = ("v", "w_o")
RING = 6
DVE_TILES = 6
LOOPED = 12

f32 = mybir.dt.float32
r32 = mybir.dt.float32r
bf16 = mybir.dt.bfloat16
i32 = mybir.dt.int32
ACT = mybir.ActivationFunctionType
ALU = mybir.AluOpType
AX = mybir.AxisListType


def hybrid_moe_kernel(nc, x, mem, w_in, w_out_a, w_out_b, w_out_x, w_kv, w_o, w_gate_up, w_down,
                      w_route, cols, rows, b_route, consts, out):
    matrices = {"w_in": w_in, "w_out_a": w_out_a, "w_out_b": w_out_b, "w_out_x": w_out_x,
                "w_kv": w_kv, "w_o": w_o}
    ctx = ExitStack()
    with ctx:
        base = (nc.sbuf_base + 63) // 64 * 64

        def at(name, offset, shape, dt=f32):
            return nc.alloc_sbuf_tensor_at(name, [P] + shape, dt, offset=base + offset)

        KB = 1024
        raw = at("raw", 0, [RAW, UNIT])
        hi = at("hi", 96 * KB, [CONV, HALF], r32)
        lo = at("lo", 120 * KB, [CONV, HALF], r32)
        kT = at("kT", 64 * KB, [KT, T])
        v_sb = at("v_sb", 72 * KB, [TT, D])
        qT = at("qT", 80 * KB, [KT, T])
        probsT = at("probsT", 80 * KB, [HEADS, TT, T])
        mem_sb = at("mem_sb", 88 * KB, [TT, D])
        probs = at("probs", 88 * KB, [HEADS, TT, T])
        A0 = 144 * KB
        inA = at("inA", A0, [2, KT, T], r32)
        z_parts = at("z_parts", A0, [3, TT, D], bf16)
        inB = at("inB", A0 + 16 * KB, [2, KT, T], r32)
        ffn_row = at("ffn_row", A0 + 16 * KB, [D])
        route = at("route", A0 + 28 * KB, [768])
        xeT = at("xeT", A0 + 16 * KB, [2, KT, 2 * SLOTS], r32)
        y_parts = at("y_parts", A0 + 24 * KB, [2, D], r32)
        B0 = A0 + 32 * KB
        a_mid = at("a_mid", B0, [KT, T])
        merged = at("merged", B0, [KT, T])
        x2 = at("x2", B0, [TT, D])
        gate = at("gate", B0 + 8 * KB, [KT, T])
        zT = at("zT", B0 + 8 * KB, [KT, T])
        conv = at("conv", B0 + 16 * KB, [KT, T])
        x_again = at("x_again", B0 + 16 * KB, [TT, D])
        rank_rows = at("rank_rows", B0 + 8 * KB, [E, T], bf16)
        u_sb = at("u_sb", B0 + 24 * KB, [KT, T])
        x_sb = at("x_sb", B0 + 24 * KB, [TT, D])
        z_sb = at("z_sb", B0 + 24 * KB, [TT, D])
        gu_sb = at("gu_sb", B0 + 24 * KB, [2 * FF])
        silu_sb = at("silu_sb", B0 + 28 * KB, [4, SLOTS])
        h_sb = at("h_sb", B0 + 29 * KB, [4, SLOTS])
        x3 = at("x3", B0 + 24 * KB, [TT, D])
        S0 = B0 + 32 * KB
        pick = at("pick", S0, [2, TT, 2 * SLOTS], bf16)
        put = at("put", S0 + 2 * KB, [T], r32)
        hT = at("hT", S0 + 3 * KB, [4, 2 * SLOTS], r32)
        part = at("part", S0, [2, T])
        square_out = at("square_out", S0, [512])
        conv_prod = at("conv_prod", S0 + 2 * KB, [KT - DVE_TILES, T])
        ln_mean = at("ln_mean", S0 + 2 * KB, [T])
        ln_rstd = at("ln_rstd", S0 + 3 * KB, [T])
        S1 = S0 + 5 * KB
        cst = at("cst", S1, [N_CST])
        S2 = S1 + (4 * N_CST + 63) // 64 * 64
        col = at("col", S2, [N_COLS])
        S3 = S2 + (4 * N_COLS + 63) // 64 * 64
        wr = at("wr", S3, [KT, GROUPS + E])
        S4 = S3 + (4 * KT * (GROUPS + E) + 63) // 64 * 64
        rank_tab = at("rank_tab", S4, [TT, (MAX_ROUNDS + 1) * E])
        S5 = S4 + 4 * TT * (MAX_ROUNDS + 1) * E
        comb = at("comb", S5, [TT, E, 4], bf16)
        S6 = S5 + 8 * TT * E
        stat = at("stat", S6, [24])
        comb_slot = at("comb_slot", S6 + 96, [2])
        loops = at("loops", S6 + 128, [2], i32)
        rank_bf = at("rank_bf", S6 + 160, [T], bf16)
        br = at("br", S6 + 160 + 2 * T, [GROUPS + E])

        ps = ctx.enter_context(nc.psum_tensor("ps", [P, 8, 512], f32))
        rank_dram = nc.dram_tensor("rank_dram", [E, T], bf16, kind="Internal").ap()

        def c_(name):
            return cst[:, CST[name][0]:CST[name][1]]

        ident, ones, before, fold = c_("ident"), c_("ones"), c_("before"), c_("fold")

        def vec(name, c, k=0):
            a = COL[name] + k * KT + c
            return col[:, a:a + 1]

        def sem(name):
            return ctx.enter_context(nc.semaphore(name))

        first_loaded = sem("first_loaded")
        raw_loaded = [sem(f"raw_loaded{s}") for s in range(RAW)]
        hi_made, lo_made, half_used = sem("hi_made"), sem("lo_made"), sem("half_used")
        bank_free = [sem(f"bank_free{b}") for b in range(RING)]
        x_loaded, mem_loaded, cst_loaded, col_loaded = map(sem, ("x_loaded", "mem_loaded", "cst_loaded", "col_loaded"))
        wr_loaded, ffn_loaded, final_loaded, xagain_loaded = map(sem, ("wr_loaded", "ffn_loaded", "final_loaded", "xagain_loaded"))
        sumsq, meansq, root, scaled, xT_turned, x_hi, x_lo = map(sem, ("sumsq", "meansq", "root", "scaled", "xT_turned", "x_hi", "x_lo"))
        memT_turned, mem_hi, mem_lo = map(sem, ("memT_turned", "mem_hi", "mem_lo"))
        glu_value, glu_gate, u_ready = map(sem, ("glu_value", "glu_gate", "u_ready"))
        a_value, a_cv, a_prod, a_hi, a_lo = map(sem, ("a_value", "a_cv", "a_prod", "a_hi", "a_lo"))
        gate_made, merged_a, merged_x, merged_all, merged_hi, merged_lo = map(
            sem, ("gate_made", "merged_a", "merged_x", "merged_all", "merged_hi", "merged_lo"))
        q_made, k_made, v_made = map(sem, ("q_made", "k_made", "v_made"))
        scored, score_max, exps, prob_made, probs_turned, probsT_made, attended, att_hi, att_lo = map(
            sem, ("scored", "score_max", "exps", "prob_made", "probs_turned", "probsT_made", "attended", "att_hi", "att_lo"))
        conv_step, ln_sum, ln_centred, ln_square, ln_sumsq, ln_var, ln_root, ln_scaled, b_silu, b_hi, b_lo = map(
            sem, ("conv_step", "ln_sum", "ln_centred", "ln_square", "ln_sumsq", "ln_var", "ln_root", "ln_scaled", "b_silu", "b_hi", "b_lo"))
        x2_made, z_made, z_part0, z_rest, z_part1, z_part2, zT_turned, zT_made, logits_done = map(
            sem, ("x2_made", "z_made", "z_part0", "z_rest", "z_part1", "z_part2", "zT_turned", "zT_made", "logits_done"))
        route_for_exp, route_exp, member_made, ranked, rank_made, rank_turned, rank_copied, rank_stored, rank_rows_loaded = map(
            sem, ("route_for_exp", "route_exp", "member_made", "ranked", "rank_made", "rank_turned", "rank_copied", "rank_stored", "rank_rows_loaded"))
        loops_made, comb_made = sem("loops_made"), sem("comb_made")
        pick_made, put_made, gathered, xeT_hi, xeT_made = map(sem, ("pick_made", "put_made", "gathered", "xeT_hi", "xeT_made"))
        gate_out, up_out, slotted, comb_slot_made, folded = map(sem, ("gate_out", "up_out", "slotted", "comb_slot_made", "folded"))
        silu_made, h_made, h_hi, h_lo = map(sem, ("silu_made", "h_made", "h_hi", "h_lo"))
        y_hi, y_lo, y_seeded, combined = map(sem, ("y_hi", "y_lo", "y_seeded", "combined"))
        x3_made, sumsq3, root3, out_made, stored = map(sem, ("x3_made", "sumsq3", "root3", "out_made", "stored"))
        dve_chain, warm_ready, warm_used = map(sem, ("dve_chain", "warm_ready", "warm_used"))
        conv_pool, ln_mean_made, ln_rstd_made, ln_centred_b, ln_scaled_b = map(
            sem, ("conv_pool", "ln_mean_made", "ln_rstd_made", "ln_centred_b", "ln_scaled_b"))

        Y = [ps[:, b, :] for b in range(4)]
        G0, G1 = ps[:, 4, :], ps[:, 5, :]
        DN = [ps[:, 6, :], ps[:, 7, :]]

        def sums(t):
            return ps[:, 2 * t:2 * t + 2, :].rearrange("p a b -> p (a b)")

        def raw_slot(u):
            return (u + 2) % RAW_DENSE, u // RAW_DENSE

        RAW_BASE = [0] * RAW
        for u in range(N_UNITS):
            RAW_BASE[raw_slot(u)[0]] += 1

        def expert_slot(m):
            return (m + 4) % RAW

        def raw_half(slot, h, k_split):
            flat = raw[:, slot, :]
            if k_split:
                return flat[:, h * HALF:(h + 1) * HALF].rearrange("p (a b) -> p a b", b=T)
            return flat.rearrange("p (a b) -> p a b", b=2 * T)[:, :, h * T:(h + 1) * T]

        def conv_half(buf, N):
            return buf[:, N % CONV, :].rearrange("p (a b) -> p a b", b=T)

        block = ctx.enter_context(nc.Block())

        @block.sync
        def _(sp):
            sp.dma_start(x_sb[:, :, :], x.rearrange("(t p) d -> p t d", p=P)).then_inc(x_loaded, 16)
            sp.dma_start(cst[:, :], consts).then_inc(cst_loaded, 16)
            sp.dma_start(col[:, :], cols).then_inc(col_loaded, 16)
            for u, (name, matrix, c0) in enumerate(UNITS):
                slot = raw_slot(u)[0]
                if u >= RAW_DENSE:
                    sp.wait_ge(lo_made, 2 * (u - RAW_DENSE) + 2)
                src = matrices[matrix][:, c0:c0 + 512].rearrange("(k p) n -> p k n", p=P)
                dst = raw[:, slot, :].rearrange("p (k n) -> p k n", n=512)
                if u == 0:
                    sp.dma_start(dst[:, :, 0:T], src[:, :, 0:T]).then_inc(first_loaded, 16)
                    sp.dma_start(dst[:, :, T:2 * T], src[:, :, T:2 * T]).then_inc(raw_loaded[slot], 16)
                else:
                    sp.dma_start(dst, src).then_inc(raw_loaded[slot], 16)

            gate_up = w_gate_up.rearrange("(j u) (k p) n -> u p j k n", u=2, p=P)
            down = w_down.rearrange("(j u) (k p) n -> u p j k n", u=2, p=P)

            def load_gate_up(slot, parity, j, c):
                src = gate_up[parity, :, bass.ds(j, 1), :, c * FF:(c + 1) * FF]
                sp.dma_start(raw[:, slot, :].rearrange("p (a k n) -> p a k n", a=1, n=FF), src)\
                    .then_inc(raw_loaded[slot], 16)

            def load_down(slot, parity, j):
                src = down[parity, :, bass.ds(j, 1), :, :]
                sp.dma_start(raw[:, slot, :].rearrange("p (a k n) -> p a k n", a=1, n=D), src)\
                    .then_inc(raw_loaded[slot], 16)

            def lo_of(m):
                return DENSE + 2 * (m - RAW) + 2

            sp.wait_ge(attended, HEADS)
            load_gate_up(expert_slot(0), 0, 0, 0)
            load_gate_up(expert_slot(1), 0, 0, 1)
            for m in (2, 3, 4):
                sp.wait_ge(lo_made, lo_of(m))
                if m < 4:
                    load_gate_up(expert_slot(m), 1, 0, m - 2)
                else:
                    load_down(expert_slot(m), 0, 0)

            def pair(j, j_mod, j_before):
                for r, load in enumerate((lambda s: load_gate_up(s, 0, j_mod, 0),
                                          lambda s: load_gate_up(s, 0, j_mod, 1),
                                          lambda s: load_down(s, 1, j_before),
                                          lambda s: load_gate_up(s, 1, j_mod, 0),
                                          lambda s: load_gate_up(s, 1, j_mod, 1),
                                          lambda s: load_down(s, 0, j_mod))):
                    sp.wait_ge(lo_made, 12 * j + (lo_of(r - 1)))
                    load(expert_slot(5 + r))

            with sp.Fori(1, E // 2) as j:
                pair(j, j, j - 1)
            sp.wait_ge(loops_made, 1)
            last_pair = nc.sync.value_load(loops[0:1, 0:1], min_val=E // 2 - 1, max_val=MAX_ROUNDS * E // 2 - 1)
            with sp.If(last_pair > E // 2 - 1):
                with sp.Fori(E // 2, last_pair + 1) as j:
                    pair(j, j % (E // 2), (j + (E // 2 - 1)) % (E // 2))
            sp.wait_ge(lo_made, 12 * last_pair + lo_of(5))
            load_down(expert_slot(5), 1, E // 2 - 1)
            sp.wait_ge(lo_made, 12 * last_pair + (DENSE + 6))
            sp.dma_start(raw[:, 0, 0:D], rows[1:2, :].to_broadcast([P, D])).then_inc(final_loaded, 16)
            for t in range(TT):
                sp.wait_ge(out_made, t + 1)
                sp.dma_start(out[t * P:(t + 1) * P, :], x3[:, t, :]).then_inc(stored, 16)
            sp.wait_ge(stored, 16 * TT)

        @block.gpsimd
        def _(pool):
            for i in range(4):
                pool.wait_ge(glu_value, i + 1)
                pool.wait_ge(glu_gate, i + 1)
                nc.gpsimd.tensor_tensor(u_sb[:, 2 * i:2 * i + 2, :], u_sb[:, 2 * i:2 * i + 2, :],
                                        gate[:, 2 * i:2 * i + 2, :], ALU.mult).then_inc(u_ready, 1)

            pool_tiles = list(enumerate(range(DVE_TILES, KT)))
            n_pool = len(pool_tiles)
            pool.wait_ge(u_ready, 4)
            pool.wait_ge(sumsq, 4)
            for k, c in pool_tiles:
                nc.gpsimd.tensor_scalar(conv[:, c, :], u_sb[:, c, :], vec("conv_b", c, TAPS_B - 1), vec("conv_b_b", c),
                                        ALU.mult, ALU.add).then_inc(conv_pool, 1)
            for shift in range(1, TAPS_B):
                done = n_pool + 2 * n_pool * (shift - 1)
                for k, c in pool_tiles:
                    pool.wait_ge(conv_pool, done - n_pool + k + 1)
                    nc.gpsimd.tensor_scalar(conv_prod[:, k, shift:T], u_sb[:, c, 0:T - shift],
                                            vec("conv_b", c, TAPS_B - 1 - shift), None, ALU.mult).then_inc(conv_pool, 1)
                for k, c in pool_tiles:
                    pool.wait_ge(conv_pool, done + k + 1)
                    nc.gpsimd.tensor_tensor(conv[:, c, shift:T], conv[:, c, shift:T], conv_prod[:, k, shift:T],
                                            ALU.add).then_inc(conv_pool, 1)
            def all_channels(a):
                return a.rearrange("p (o t) -> p o t", o=1).to_broadcast([P, KT // 2, T])

            pool.wait_ge(ln_mean_made, 1)
            nc.gpsimd.tensor_tensor(conv[:, 4:8, :], conv[:, 4:8, :], all_channels(ln_mean[:, :]),
                                    ALU.subtract).then_inc(ln_centred_b, 1)
            pool.wait_ge(ln_rstd_made, 1)
            nc.gpsimd.tensor_tensor(conv[:, 4:8, :], conv[:, 4:8, :], all_channels(ln_mean[:, :]),
                                    ALU.mult).then_inc(ln_scaled_b, 1)

            for t in range(TT):
                pool.wait_ge(z_part0, t + 1)
                nc.gpsimd.tensor_tensor(z_sb[:, t, :], z_sb[:, t, :], z_parts[:, 0, t, :], ALU.subtract).then_inc(z_rest, 1)
            for t in range(TT):
                pool.wait_ge(z_part1, t + 1)
                nc.gpsimd.tensor_tensor(z_parts[:, 2, t, :], z_sb[:, t, :], z_parts[:, 1, t, :],
                                        ALU.subtract).then_inc(z_part2, 1)

            def hidden_lo(i):
                pool.wait_ge(h_hi, i + 1)
                nc.gpsimd.tensor_tensor(hT[:, :, SLOTS:2 * SLOTS], h_sb[:, :, :], hT[:, :, 0:SLOTS].bitcast(f32),
                                        ALU.subtract).then_inc(h_lo, 1)

            hidden_lo(0)
            hidden_lo(1)
            pool.wait_ge(loops_made, 1)
            last_pair = nc.gpsimd.value_load(loops[0:1, 0:1], min_val=E // 2 - 1, max_val=MAX_ROUNDS * E // 2 - 1)
            with pool.Fori(1, last_pair + 1) as j:
                hidden_lo(2 * j)
                hidden_lo(2 * j + 1)

        def stage_of(n):
            name = UNITS[n // 2][0]
            g = UNITS[n // 2][2] % D // 512
            return name, 2 * g + n % 2

        @block.scalar
        def _(act):
            def make_hi(N, slot, loaded, h, k_split):
                if N == 0:
                    act.wait_ge(first_loaded, 16)
                else:
                    act.wait_ge(raw_loaded[slot], loaded)
                if N >= CONV:
                    act.wait_ge(half_used, N - (CONV - 1))
                return nc.scalar.activation(conv_half(hi, N), raw_half(slot, h, k_split), ACT.Copy)

            def dense_hi(N):
                if N < DENSE:
                    slot, before_ = raw_slot(N // 2)
                    make_hi(N, slot, 16 * (before_ + 1), N % 2, UNITS[N // 2][0] in K_SPLIT).then_inc(hi_made, 1)
                else:
                    m = (N - DENSE) // 2
                    slot = expert_slot(m)
                    make_hi(N, slot, 16 * (RAW_BASE[slot] + 1 + m // RAW), N % 2, True).then_inc(hi_made, 1)

            act.wait_ge(warm_ready, 1)
            nc.scalar.activation(stat[:, 23:24], stat[:, 23:24], ACT.Sqrt).then_inc(warm_used, 1)
            act.wait_ge(x_loaded, 16)
            for t in range(TT):
                nc.scalar.activation(conv[:, 4 * t:4 * t + 4, :].rearrange("p a b -> p (a b)"), x_sb[:, t, :],
                                     ACT.Square, accum_out=stat[:, t:t + 1]).then_inc(sumsq, 1)
            act.wait_ge(meansq, 1)
            nc.scalar.activation(stat[:, 6:8], stat[:, 4:6], ACT.Sqrt).then_inc(root, 1)
            dense_hi(0)
            act.wait_ge(col_loaded, 16)
            for c in range(KT):
                act.wait_ge(xT_turned, c // 2 + 1)
                nc.scalar.activation(inA[:, 0, c, :], ps[:, 4 + c // 2, (c % 2) * T:(c % 2 + 1) * T], ACT.Copy,
                                     scale=vec("mix_g", c)).then_inc(x_hi, 1)
            act.dma_start(mem_sb[:, :, :], mem.rearrange("(t p) d -> p t d", p=P)).then_inc(mem_loaded, 16)
            act.dma_start(wr[:, :, :], w_route.rearrange("(k p) n -> p k n", p=P)).then_inc(wr_loaded, 16)
            act.dma_start(br[:, :], b_route.to_broadcast([P, GROUPS + E])).then_inc(wr_loaded, 16)
            dense_hi(1)
            dense_hi(2)

            def mem_squares():
                act.wait_ge(mem_loaded, 16)
                act.wait_ge(sumsq, 2)
                for t in range(TT):
                    nc.scalar.activation(conv[:, 4 * t:4 * t + 4, :].rearrange("p a b -> p (a b)"), mem_sb[:, t, :],
                                         ACT.Square, accum_out=stat[:, 2 + t:3 + t]).then_inc(sumsq, 1)
                act.wait_ge(meansq, 2)
                nc.scalar.activation(stat[:, 10:12], stat[:, 8:10], ACT.Sqrt).then_inc(root, 1)

            def mem_parts(pair_):
                for c in (2 * pair_, 2 * pair_ + 1):
                    act.wait_ge(memT_turned, pair_ + 1)
                    nc.scalar.activation(inB[:, 0, c, :], ps[:, 6 + pair_ % 2, (c % 2) * T:(c % 2 + 1) * T],
                                         ACT.Copy, scale=vec("mem_g", c)).then_inc(mem_hi, 1)

            def softmax_exp(h):
                for t in range(TT):
                    act.wait_ge(score_max, h + 1)
                    nc.scalar.activation(probs[:, h, t, :], ps[:, 6 + h % 2, t * T:(t + 1) * T], ACT.Exp,
                                         bias=stat[:, 12 + t + 2 * (h % 2):13 + t + 2 * (h % 2)],
                                         scale=HEAD_DIM ** -0.5,
                                         accum_out=stat[:, 16 + t + 2 * (h % 2):17 + t + 2 * (h % 2)]).then_inc(exps, 1)

            def turned_probs(h):
                act.wait_ge(probs_turned, h + 1)
                nc.scalar.activation(probsT[:, h, :, :].rearrange("p a b -> p (a b)"), ps[:, 6 + h % 2, :],
                                     ACT.Copy).then_inc(probsT_made, 1)

            def attention_hi(h):
                act.wait_ge(attended, h + 1)
                nc.scalar.activation(inB[:, 0, 2 * h:2 * h + 2, :].rearrange("p a b -> p (a b)"),
                                     ps[:, 6 + h % 2, :], ACT.Copy).then_inc(att_hi, 1)

            def ln_squares():
                for h, centred in enumerate((ln_centred, ln_centred_b)):
                    act.wait_ge(centred, 1)
                    nc.scalar.activation(u_sb[:, 4 * h:4 * h + 4, :], conv[:, 4 * h:4 * h + 4, :],
                                         ACT.Square).then_inc(ln_square, 1)

            def branch_b_act():
                act.wait_ge(ln_var, 1)
                nc.scalar.activation(ln_rstd[:, :], ln_rstd[:, :], ACT.Sqrt).then_inc(ln_root, 1)
                for c in range(KT):
                    if c % 4 == 0:
                        act.wait_ge((ln_scaled, ln_scaled_b)[c // 4], 1)
                    nc.scalar.activation(u_sb[:, c, :], conv[:, c, :], ACT.Silu, bias=vec("ln_b", c),
                                         scale=vec("ln_g", c)).then_inc(b_silu, 1)
                act.wait_ge(b_silu, KT)
                act.dma_start(x_again[:, :, :], x.rearrange("(t p) d -> p t d", p=P)).then_inc(xagain_loaded, 16)
                act.wait_ge(half_used, FIRST["out_x"] + 4)
                nc.scalar.activation(inB[:, 0, :, :], u_sb[:, :, :], ACT.Copy).then_inc(b_hi, 1)

            def expert_xeT(i, par):
                act.wait_ge(gathered, i + 1)
                nc.scalar.activation(xeT[:, par, :, 0:SLOTS], ps[:, 6, :].rearrange("p (a b) -> p a b", b=SLOTS),
                                     ACT.Copy).then_inc(xeT_hi, 1)

            def x2_squares(g):
                for t in range(TT):
                    act.wait_ge(sumsq, 4 + 2 * g + t)
                    nc.scalar.activation(square_out[:, :],
                                         x2[:, t, 512 * g:512 * g + 512], ACT.Square,
                                         accum_out=stat[:, 2 * t + g:2 * t + g + 1]).then_inc(sumsq, 1)

            def x2_turned(c2):
                act.wait_ge(zT_turned, c2 + 1)
                for k in range(2):
                    nc.scalar.activation(zT[:, 2 * c2 + k, :], ps[:, 6 + c2 % 2, k * T:(k + 1) * T], ACT.Copy,
                                         scale=vec("ffn_g", 2 * c2 + k)).then_inc(zT_made, 1)

            def ffn_first_half():
                act.wait_ge(x2_made, 2)
                x2_squares(0)

            def load_ffn_row():
                act.wait_ge(half_used, FIRST["w_o"])
                act.dma_start(ffn_row[:, :], rows[0:1, :].to_broadcast([P, D])).then_inc(ffn_loaded, 16)

            F = FIRST
            extra = {4: [mem_squares],
                     F["q"] - 1: [lambda: mem_parts(0), lambda: mem_parts(1)],
                     F["q"] + 1: [lambda: mem_parts(2), lambda: mem_parts(3)],
                     F["v"] - 1: [lambda: softmax_exp(0), lambda: softmax_exp(1)],
                     F["v"] + 1: [lambda: softmax_exp(2), lambda: softmax_exp(3)],
                     F["v"] + 2: [lambda: turned_probs(0), lambda: turned_probs(1)],
                     F["v"] + 3: [lambda: turned_probs(2), lambda: turned_probs(3)],
                     F["gate2"]: [lambda: attention_hi(0), lambda: attention_hi(1)],
                     F["gate2"] + 1: [lambda: attention_hi(2), lambda: attention_hi(3)],
                     F["out_x"] + 1: [ln_squares], F["out_x"] + 3: [branch_b_act],
                     F["w_o"]: [load_ffn_row], F["w_o"] + 2: [ffn_first_half, lambda: x2_turned(0), lambda: x2_turned(1)]}
            gates_done = 0
            for n in range(DENSE):
                name, q4 = stage_of(n)
                bank, b = ps[:, n % RING, :], n % RING
                two = slice(2 * q4, 2 * q4 + 2)
                if name in ("glu_value", "glu_gate", "gate0", "gate1", "gate2", "a_value", "q", "k"):
                    act.wait_ge(half_used, n + 1)
                if name in ("glu_value", "glu_gate"):
                    dst = u_sb if name == "glu_value" else gate
                    fn = ACT.Identity if name == "glu_value" else ACT.Sigmoid
                    for k in range(2):
                        last = nc.scalar.activation(dst[:, 2 * q4 + k, :], bank[:, k * T:(k + 1) * T], fn,
                                                    bias=vec("b_glu", 2 * q4 + k, int(name == "glu_gate")))
                    last.then_inc(bank_free[b], 1)
                    act.wait_ge(bank_free[b], n // RING + 1)
                    act.sem_inc(glu_value if name == "glu_value" else glu_gate, 1)
                elif name in ("gate0", "gate1", "gate2"):
                    if name == "gate0":
                        act.wait_ge(a_lo, 4)
                    elif name == "gate2":
                        act.wait_ge(merged_a, 4)
                    else:
                        act.wait_ge(merged_x, 4)
                    for k in range(2):
                        last = nc.scalar.activation(gate[:, 2 * q4 + k, :], bank[:, k * T:(k + 1) * T], ACT.Sigmoid,
                                                    bias=vec("b_gate", 2 * q4 + k, int(name[-1])))
                    last.then_inc(bank_free[b], 1)
                    act.wait_ge(bank_free[b], n // RING + 1)
                    act.sem_inc(gate_made, 1)
                elif name in ("a_value", "q", "k"):
                    dst, made = {"a_value": (a_mid, a_value), "q": (qT, q_made), "k": (kT, k_made)}[name]
                    nc.scalar.activation(dst[:, two, :].rearrange("p a b -> p (a b)"), bank, ACT.Copy).then_inc(made, 1)
                    act.wait_ge(made, q4 + 1)
                    act.sem_inc(bank_free[b], 1)
                elif name == "a_b":
                    act.wait_ge(a_prod, q4 + 1)
                    nc.scalar.activation(inB[:, 0, two, :], gate[:, two, :], ACT.Copy).then_inc(a_hi, 1)
                elif name == "v" and n % 2 == 1:
                    act.wait_ge(half_used, n + 1)
                    g = q4 // 2
                    for t in range(TT):
                        nc.scalar.activation(v_sb[:, t, 512 * g:512 * g + 512], ps[:, (n - 1 + t) % RING, :],
                                             ACT.Copy).then_inc(bank_free[(n - 1 + t) % RING], 1)
                    for t in range(TT):
                        act.wait_ge(bank_free[(n - 1 + t) % RING], n // RING + 1)
                    act.sem_inc(v_made, 1)
                elif name == "out_b":
                    act.wait_ge(merged_all, q4 + 1)
                    nc.scalar.activation(inA[:, 0, two, :], merged[:, two, :], ACT.Copy).then_inc(merged_hi, 1)
                dense_hi(n + 3)
                for work in extra.get(n, ()):
                    work()

            act.wait_ge(x2_made, 4)
            x2_squares(1)
            act.wait_ge(meansq, 3)
            nc.scalar.activation(stat[:, 6:8], stat[:, 4:6], ACT.Sqrt).then_inc(root, 1)
            x2_turned(2)
            x2_turned(3)
            for t in range(TT):
                act.wait_ge(z_made, t + 1)
                nc.scalar.activation(z_parts[:, 0, t, :], z_sb[:, t, :], ACT.Copy).then_inc(z_part0, 1)
            for t in range(TT):
                act.wait_ge(z_rest, t + 1)
                nc.scalar.activation(z_parts[:, 1, t, :], z_sb[:, t, :], ACT.Copy).then_inc(z_part1, 1)
            act.wait_ge(route_for_exp, 1)
            nc.scalar.activation(route[:, 80:88], route[:, 80:88], ACT.Exp).then_inc(route_exp, 1)
            act.wait_ge(route_for_exp, 2)
            nc.scalar.activation(route[:, 88:90], route[:, 88:90], ACT.Exp).then_inc(route_exp, 1)
            expert_xeT(0, 0)
            act.wait_ge(rank_turned, 2)
            nc.scalar.activation(rank_bf[0:E, :], ps[0:E, 5, 256:256 + T], ACT.Copy).then_inc(rank_copied, 1)
            act.wait_ge(rank_copied, 1)
            act.dma_start(rank_dram, rank_bf[0:E, :]).then_inc(rank_stored, 16)
            act.wait_ge(rank_stored, 16)
            act.dma_start(rank_rows[:, :, :].rearrange("p e t -> p (e t)"),
                          rank_dram.rearrange("e t -> (e t)").rearrange("(a n) -> a n", a=1).to_broadcast([P, E * T]))\
                .then_inc(rank_rows_loaded, 16)

            act.wait_ge(loops_made, 1)
            last_pair = nc.scalar.value_load(loops[0:1, 0:1], min_val=E // 2 - 1, max_val=MAX_ROUNDS * E // 2 - 1)

            def expert_hi(j, m0, k):
                m = m0 + k // 2
                slot = expert_slot(m)
                N0 = DENSE + 2 * m0 + k
                act.wait_ge(raw_loaded[slot], 16 * j + 16 * (RAW_BASE[slot] + 1 + m // RAW))
                act.wait_ge(half_used, 12 * j + (N0 - (CONV - 1)))
                nc.scalar.activation(conv_half(hi, N0), raw_half(slot, k % 2, True), ACT.Copy).then_inc(hi_made, 1)

            def y_out_hi(i, par):
                act.wait_ge(comb_slot_made, i + 1)
                nc.scalar.activation(y_parts[:, 0, :], ps[:, 6:8, :].rearrange("p a b -> p (a b)"), ACT.Copy,
                                     scale=comb_slot[:, par:par + 1]).then_inc(y_hi, 1)

            def hidden_hi(i):
                act.wait_ge(h_made, i + 1)
                nc.scalar.activation(hT[:, :, 0:SLOTS], h_sb[:, :, :], ACT.Copy).then_inc(h_hi, 1)

            def step(j, r):
                first = isinstance(j, int)
                i = 2 * j + r
                m0 = 0 if first and i == 0 else 3 * r - 1
                done = 12 * j + (DENSE + 2 * m0 + 1)

                def more(k):
                    expert_hi(j, m0, k)
                start = first and i == 0
                if not start:
                    more(2)
                more(3)
                if not start:
                    hidden_hi(i - 1)
                act.wait_ge(half_used, done + 1)
                if not start:
                    act.wait_ge(folded, i)
                nc.scalar.activation(gu_sb[:, 0:FF], G0, ACT.Copy).then_inc(gate_out, 1)
                more(4)
                expert_xeT(i + 1, (r + 1) % 2)
                more(5)
                act.wait_ge(half_used, done + 3)
                nc.scalar.activation(gu_sb[:, FF:2 * FF], G1, ACT.Copy).then_inc(up_out, 1)
                if not start:
                    more(6)
                    more(7)
                    act.wait_ge(half_used, done + 5)
                    y_out_hi(i - 1, (r + 1) % 2)
                act.wait_ge(folded, i + 1)
                if not start:
                    act.wait_ge(h_made, i)
                nc.scalar.activation(silu_sb[:, :, :], G1.rearrange("p (a b) -> p a b", b=SLOTS)[:, 0:4, :],
                                     ACT.Silu).then_inc(silu_made, 1)

            step(0, 0)
            step(0, 1)
            with act.Fori(1, last_pair + 1) as j:
                step(j, 0)
                step(j, 1)
            hidden_hi(2 * last_pair + 1)
            act.wait_ge(half_used, 12 * last_pair + (DENSE + 12))
            y_out_hi(2 * last_pair + 1, 1)

            act.wait_ge(combined, 2 * last_pair + 2)
            for t in range(TT):
                nc.scalar.activation(gate[:, 4 * t:4 * t + 4, :].rearrange("p a b -> p (a b)"), sums(t),
                                     ACT.Square, accum_out=stat[:, t:t + 1]).then_inc(sumsq3, 1)
            act.wait_ge(meansq, 4)
            nc.scalar.activation(stat[:, 6:8], stat[:, 4:6], ACT.Sqrt).then_inc(root, 1)

        @block.vector
        def _(dve):
            chain = [0]

            def link(ins):
                chain[0] += 1
                ins.then_inc(dve_chain, 1)
                dve.wait_ge(dve_chain, chain[0])

            def make_lo(N, slot, h, k_split):
                dve.wait_ge(hi_made, N + 1)
                nc.vector.tensor_tensor(conv_half(lo, N), raw_half(slot, h, k_split), conv_half(hi, N).bitcast(f32),
                                        ALU.subtract).then_inc(lo_made, 1)

            def dense_lo(N):
                if N < DENSE:
                    make_lo(N, raw_slot(N // 2)[0], N % 2, UNITS[N // 2][0] in K_SPLIT)
                else:
                    make_lo(N, expert_slot((N - DENSE) // 2), N % 2, True)

            roots = [0]

            def rstd(sums, mean, rooted, r):
                roots[0] += 1
                nc.vector.tensor_scalar(stat[:, mean:mean + 2], stat[:, sums:sums + 2], 1.0 / D, EPS,
                                        ALU.mult, ALU.add).then_inc(meansq, 1)
                dve.wait_ge(root, roots[0])
                link(nc.vector.reciprocal(stat[:, r:r + 2], stat[:, rooted:rooted + 2]))

            nc.vector.memset(stat[:, 23:24], 1.0).then_inc(warm_ready, 1)
            dve.wait_ge(sumsq, 2)
            rstd(0, 4, 6, 20)
            for t in range(TT):
                nc.vector.tensor_scalar(x_sb[:, t, :], x_sb[:, t, :], stat[:, 20 + t:21 + t], None,
                                        ALU.mult).then_inc(scaled, 1)
            dense_lo(0)
            dve.wait_ge(col_loaded, 16)
            for c in range(KT):
                dve.wait_ge(x_hi, c // 2 * 2 + 2)
                nc.vector.scalar_tensor_tensor(inA[:, 1, c, :], ps[:, 4 + c // 2, (c % 2) * T:(c % 2 + 1) * T],
                                               vec("mix_g", c), inA[:, 0, c, :].bitcast(f32), ALU.mult,
                                               ALU.subtract).then_inc(x_lo, 1)
            dense_lo(1)

            def mem_scale():
                dve.wait_ge(sumsq, 4)
                dve.wait_ge(warm_used, 1)
                rstd(2, 8, 10, 22)
                for t in range(TT):
                    nc.vector.tensor_scalar(mem_sb[:, t, :], mem_sb[:, t, :], stat[:, 22 + t:23 + t], None,
                                            ALU.mult).then_inc(scaled, 1)

            def mem_parts(pair_):
                for c in (2 * pair_, 2 * pair_ + 1):
                    dve.wait_ge(mem_hi, 2 * pair_ + 2)
                    nc.vector.scalar_tensor_tensor(inB[:, 1, c, :], ps[:, 6 + pair_ % 2, (c % 2) * T:(c % 2 + 1) * T],
                                                   vec("mem_g", c), inB[:, 0, c, :].bitcast(f32), ALU.mult,
                                                   ALU.subtract).then_inc(mem_lo, 1)

            def softmax_max(h):
                dve.wait_ge(scored, h + 1)
                if h >= 2:
                    dve.wait_ge(exps, 2 * (h - 1))
                m = stat[:, 12 + 2 * (h % 2):14 + 2 * (h % 2)]
                link(nc.vector.tensor_reduce(m, ps[:, 6 + h % 2, :].rearrange("p (t m) -> p t m", t=TT), AX.X,
                                             ALU.max, negate=True))
                nc.vector.tensor_scalar(m, m, HEAD_DIM ** -0.5, None, ALU.mult).then_inc(score_max, 1)

            def softmax_norm(h):
                dve.wait_ge(exps, 2 * h + 2)
                s = 16 + 2 * (h % 2)
                link(nc.vector.reciprocal(stat[:, s:s + 2], stat[:, s:s + 2]))
                for t in range(TT):
                    nc.vector.tensor_scalar(probs[:, h, t, :], probs[:, h, t, :], stat[:, s + t:s + t + 1], None,
                                            ALU.mult).then_inc(prob_made, 1)

            def attention_lo(h):
                dve.wait_ge(att_hi, h + 1)
                nc.vector.tensor_tensor(inB[:, 1, 2 * h:2 * h + 2, :].rearrange("p a b -> p (a b)"),
                                        ps[:, 6 + h % 2, :],
                                        inB[:, 0, 2 * h:2 * h + 2, :].rearrange("p a b -> p (a b)").bitcast(f32),
                                        ALU.subtract).then_inc(att_lo, 1)

            conv_done = [0]

            def conv_taps(count):
                for s in range(conv_done[0], min(conv_done[0] + count, TAPS_B * DVE_TILES)):
                    shift, c = s // DVE_TILES, s % DVE_TILES
                    w = vec("conv_b", c, TAPS_B - 1 - shift)
                    if shift == 0:
                        dve.wait_ge(u_ready, c // 2 + 1)
                        nc.vector.tensor_scalar(conv[:, c, :], u_sb[:, c, :], w, vec("conv_b_b", c), ALU.mult,
                                                ALU.add).then_inc(conv_step, 1)
                    else:
                        dve.wait_ge(conv_step, s - DVE_TILES + 1)
                        nc.vector.scalar_tensor_tensor(conv[:, c, shift:T], u_sb[:, c, 0:T - shift], w,
                                                       conv[:, c, shift:T], ALU.mult, ALU.add).then_inc(conv_step, 1)
                    conv_done[0] += 1

            def all_channels(a):
                return a.rearrange("p (o t) -> p o t", o=1).to_broadcast([P, KT // 2, T])

            def ln_centre():
                dve.wait_ge(ln_sum, 1)
                nc.vector.tensor_scalar(ln_mean[:, :], ps[:, 6, 0:T], 1.0 / D, None, ALU.mult).then_inc(ln_mean_made, 1)
                dve.wait_ge(ln_mean_made, 1)
                nc.vector.tensor_tensor(conv[:, 0:4, :], conv[:, 0:4, :], all_channels(ln_mean[:, :]),
                                        ALU.subtract).then_inc(ln_centred, 1)

            def ln_variance():
                dve.wait_ge(ln_sumsq, 1)
                nc.vector.tensor_scalar(ln_rstd[:, :], ps[:, 7, 0:T], 1.0 / D, EPS, ALU.mult, ALU.add).then_inc(ln_var, 1)

            def ln_scale():
                dve.wait_ge(ln_root, 1)
                dve.wait_ge(ln_centred_b, 1)
                nc.vector.reciprocal(ln_mean[:, :], ln_rstd[:, :]).then_inc(ln_rstd_made, 1)
                dve.wait_ge(ln_rstd_made, 1)
                dve.wait_ge(ln_centred, 1)
                nc.vector.tensor_tensor(conv[:, 0:4, :], conv[:, 0:4, :], all_channels(ln_mean[:, :]),
                                        ALU.mult).then_inc(ln_scaled, 1)

            def branch_b_lo():
                dve.wait_ge(b_hi, 1)
                nc.vector.tensor_tensor(inB[:, 1, :, :], u_sb[:, :, :], inB[:, 0, :, :].bitcast(f32),
                                        ALU.subtract).then_inc(b_lo, 1)

            F = FIRST
            extra = {4: [mem_scale],
                     F["q"] - 1: [lambda: mem_parts(0), lambda: mem_parts(1)],
                     F["q"] + 1: [lambda: mem_parts(2), lambda: mem_parts(3)],
                     F["v"] - 1: [lambda: softmax_max(0), lambda: softmax_max(1), lambda: softmax_norm(0),
                                  lambda: softmax_norm(1)],
                     F["v"] + 1: [lambda: softmax_max(2), lambda: softmax_max(3), lambda: softmax_norm(2),
                                  lambda: softmax_norm(3)],
                     F["gate2"]: [lambda: attention_lo(0), lambda: attention_lo(1)],
                     F["gate2"] + 1: [lambda: attention_lo(2), lambda: attention_lo(3)],
                     F["out_x"] + 3: [ln_scale], F["gate1"]: [branch_b_lo]}
            urgent = {F["out_x"] + 1: ln_centre, F["out_x"] + 3: ln_variance}
            taps = {"a_value": [7] * 4, "a_c": [2] * 4, "a_b": [3] * 4, "gate0": [7] * 4, "out_a": [6, 6, 6, 3],
                    "q": [7, 3, 7, 7], "k": [7, 7, 7, 0], "v": [7, 0, 7, 7], "gate2": [5, 5, 99, 0]}
            for n in range(DENSE):
                name, q4 = stage_of(n)
                b = n % RING
                bank = ps[:, b, :]
                bank2 = bank.rearrange("p (a b) -> p a b", b=T)
                two = slice(2 * q4, 2 * q4 + 2)
                if name in ("a_c", "a_b", "out_a", "out_x", "out_b"):
                    dve.wait_ge(half_used, n + 1)
                if name == "a_c":
                    dve.wait_ge(a_value, q4 + 1)
                    nc.vector.tensor_tensor(a_mid[:, two, :], bank2, a_mid[:, two, :], ALU.mult).then_inc(bank_free[b], 1)
                    dve.wait_ge(bank_free[b], n // RING + 1)
                    dve.wait_ge(u_ready, 4)
                    for c in (2 * q4, 2 * q4 + 1):
                        nc.vector.tensor_scalar(gate[:, c, :], a_mid[:, c, :], vec("conv_a", c, TAPS_A - 1), None,
                                                ALU.mult).then_inc(a_cv, 1)
                    for shift in range(1, TAPS_A):
                        for c in (2 * q4, 2 * q4 + 1):
                            dve.wait_ge(a_cv, 2 * TAPS_A * q4 + 2 * (shift - 1) + c % 2 + 1)
                            nc.vector.scalar_tensor_tensor(gate[:, c, shift:T], a_mid[:, c, 0:T - shift],
                                                           vec("conv_a", c, TAPS_A - 1 - shift),
                                                           gate[:, c, shift:T], ALU.mult, ALU.add).then_inc(a_cv, 1)
                elif name == "a_b":
                    dve.wait_ge(a_cv, 2 * TAPS_A * (q4 + 1))
                    nc.vector.tensor_tensor(gate[:, two, :], bank2, gate[:, two, :], ALU.mult).then_inc(a_prod, 1)
                    dve.wait_ge(a_prod, q4 + 1)
                    dve.sem_inc(bank_free[b], 1)
                elif name == "out_a":
                    dve.wait_ge(gate_made, q4 + 1)
                    nc.vector.tensor_tensor(merged[:, two, :], bank2, gate[:, two, :], ALU.mult).then_inc(merged_a, 1)
                    dve.wait_ge(merged_a, q4 + 1)
                    dve.sem_inc(bank_free[b], 1)
                elif name == "out_x":
                    dve.wait_ge(gate_made, 4 + q4 + 1)
                    link(nc.vector.tensor_tensor(part[:, :, :], bank2, gate[:, two, :], ALU.mult))
                    dve.sem_inc(bank_free[b], 1)
                    nc.vector.tensor_tensor(merged[:, two, :], merged[:, two, :], part[:, :, :], ALU.add).then_inc(merged_x, 1)
                    dve.wait_ge(merged_x, q4 + 1)
                elif name == "out_b":
                    dve.wait_ge(gate_made, 8 + q4 + 1)
                    for k in range(2):
                        c = 2 * q4 + k
                        link(nc.vector.scalar_tensor_tensor(part[:, k, :], bank2[:, k, :], vec("b_out", c),
                                                            gate[:, c, :], ALU.add, ALU.mult))
                    dve.sem_inc(bank_free[b], 1)
                    nc.vector.tensor_tensor(merged[:, two, :], merged[:, two, :], part[:, :, :], ALU.add).then_inc(merged_all, 1)
                elif name == "w_o" and n % 2 == 1:
                    dve.wait_ge(half_used, n + 1)
                    dve.wait_ge(xagain_loaded, 16)
                    dve.wait_ge(merged_lo, 4)
                    g = q4 // 2
                    for t in range(TT):
                        nc.vector.tensor_tensor(x2[:, t, 512 * g:512 * g + 512], ps[:, (n - 1 + t) % RING, :],
                                                x_again[:, t, 512 * g:512 * g + 512], ALU.add).then_inc(x2_made, 1)
                if n in urgent:
                    urgent[n]()
                dense_lo(n + 2)
                if name == "a_b":
                    dve.wait_ge(a_hi, q4 + 1)
                    nc.vector.tensor_tensor(inB[:, 1, two, :], gate[:, two, :], inB[:, 0, two, :].bitcast(f32),
                                            ALU.subtract).then_inc(a_lo, 1)
                elif name == "out_b":
                    dve.wait_ge(merged_hi, q4 + 1)
                    nc.vector.tensor_tensor(inA[:, 1, two, :], merged[:, two, :], inA[:, 0, two, :].bitcast(f32),
                                            ALU.subtract).then_inc(merged_lo, 1)
                for work in extra.get(n, ()):
                    work()
                if name in taps:
                    conv_taps(taps[name][q4])

            dve.wait_ge(sumsq, 8)
            link(nc.vector.tensor_reduce(stat[:, 8:10], stat[:, 0:4].rearrange("p (t g) -> p t g", g=2), AX.X, ALU.add))
            rstd(8, 4, 6, 20)
            dve.wait_ge(ffn_loaded, 16)
            for t in range(TT):
                nc.vector.scalar_tensor_tensor(z_sb[:, t, :], x2[:, t, :], stat[:, 20 + t:21 + t], ffn_row[:, :],
                                               ALU.mult, ALU.mult).then_inc(z_made, 1)

            def r_(a, *shape):
                n = 1
                for s in shape:
                    n *= s
                v = route[:, a:a + n]
                return v if len(shape) == 1 else v.rearrange("p (a b) -> p a b", b=shape[-1])

            NL = GROUPS + E
            logit = r_(0, TT, NL)
            g_max, g_exp, diff, p_g, w1, w2 = (r_(72, TT), r_(80, TT, GROUPS), r_(88, TT), r_(90, TT),
                                               r_(92, TT), r_(94, TT))
            g_hot, e_masked, e1, e2, tmp, m1, m2 = (r_(96, TT, GROUPS), r_(104, TT, E), r_(168, TT, E),
                                                    r_(232, TT, E), r_(296, TT, E), r_(74, TT), r_(76, TT))
            member, weight, rank, low = r_(360, TT, E), r_(424, TT, E), r_(488, TT, E), r_(78, TT)

            def wide(a, n):
                return a.rearrange("p (t o) -> p t o", o=1).to_broadcast([P, TT, n])

            def first_hot(hot, values, top, desc):
                link(nc.vector.tensor_reduce(top, values, AX.X, ALU.max))
                nc.vector.scalar_tensor_tensor(hot[:, 0, :], values[:, 0, :], top[:, 0:1], desc, ALU.is_equal, ALU.mult)
                link(nc.vector.scalar_tensor_tensor(hot[:, 1, :], values[:, 1, :], top[:, 1:2], desc, ALU.is_equal,
                                                    ALU.mult))
                link(nc.vector.tensor_reduce(low, hot, AX.X, ALU.max))

            def is_low(hot, t, n):
                return nc.vector.tensor_scalar(hot[:, t, :], hot[:, t, :], low[:, t:t + 1], None, ALU.is_equal)

            dve.wait_ge(logits_done, 2)
            nc.vector.scalar_tensor_tensor(logit[:, 0, :], ps[:, 4, 0:NL], stat[:, 20:21], br[:, :], ALU.mult, ALU.add)
            link(nc.vector.scalar_tensor_tensor(logit[:, 1, :], ps[:, 4, 64:64 + NL], stat[:, 21:22], br[:, :], ALU.mult, ALU.add))
            first_hot(g_hot, logit[:, :, 0:GROUPS], g_max, c_("desc_g"))
            nc.vector.tensor_tensor(g_exp, logit[:, :, 0:GROUPS], wide(g_max, GROUPS), ALU.subtract).then_inc(route_for_exp, 1)
            is_low(g_hot, 0, GROUPS)
            link(is_low(g_hot, 1, GROUPS))
            link(nc.vector.tensor_scalar(g_hot, g_hot, -1.0, BIG, ALU.add, ALU.mult))
            for t in range(TT):
                ins = nc.vector.tensor_tensor(e_masked[:, t, :].rearrange("p (g e) -> p g e", e=EPG),
                                              logit[:, t, GROUPS:NL].rearrange("p (g e) -> p g e", e=EPG),
                                              g_hot[:, t, :].rearrange("p (g o) -> p g o", o=1).to_broadcast([P, GROUPS, EPG]),
                                              ALU.add)
            link(ins)
            first_hot(e1, e_masked, m1, c_("desc_e"))
            is_low(e1, 0, E)
            link(is_low(e1, 1, E))
            link(nc.vector.scalar_tensor_tensor(e_masked, e1, -4.0 * BIG, e_masked, ALU.mult, ALU.add))
            first_hot(e2, e_masked, m2, c_("desc_e"))
            nc.vector.tensor_tensor(diff, m2, m1, ALU.subtract).then_inc(route_for_exp, 1)
            is_low(e2, 0, E)
            link(is_low(e2, 1, E))
            nc.vector.tensor_tensor(member, e1, e2, ALU.add).then_inc(member_made, 1)
            def xeT_lo(i, par):
                dve.wait_ge(xeT_hi, i + 1)
                nc.vector.tensor_tensor(xeT[:, par, :, SLOTS:2 * SLOTS],
                                        ps[:, 6, :].rearrange("p (a b) -> p a b", b=SLOTS),
                                        xeT[:, par, :, 0:SLOTS].bitcast(f32), ALU.subtract).then_inc(xeT_made, 1)

            def make_pick(par, i):
                for t in range(TT):
                    ins = nc.vector.tensor_scalar(pick[:, par, t, :], c_("slot_row"), rank_tab[:, t, i], None, ALU.is_equal)
                ins.then_inc(pick_made, 1)

            dve.wait_ge(ranked, 1)
            rk = ps[:, 5, 0:2 * E].rearrange("p (t e) -> p t e", e=E)
            link(nc.vector.scalar_tensor_tensor(rank, rk, 1.0, member, ALU.add, ALU.mult))
            nc.vector.tensor_scalar(rank_tab[:, :, 0:E], rank, -1.0, None, ALU.add).then_inc(rank_made, 1)
            dve.wait_ge(rank_made, 1)
            make_pick(0, slice(0, 1))
            make_pick(1, slice(1, 2))
            for r in range(1, MAX_ROUNDS + 1):
                ins = nc.vector.tensor_scalar(rank_tab[:, :, r * E:(r + 1) * E], rank, -1.0 - float(SLOTS * r), None, ALU.add)
            link(ins)
            link(nc.vector.tensor_reduce(stat[:, 12:13], ps[:, 5, 2 * E:3 * E], AX.X, ALU.max))
            link(nc.vector.tensor_scalar(stat[:, 13:14], stat[:, 12:13], float(SLOTS), float(E // 2), ALU.is_gt, ALU.mult))
            for r in range(2, MAX_ROUNDS):
                link(nc.vector.tensor_scalar(stat[:, 14:15], stat[:, 12:13], float(SLOTS * r), float(E // 2), ALU.is_gt, ALU.mult))
                link(nc.vector.tensor_tensor(stat[:, 13:14], stat[:, 13:14], stat[:, 14:15], ALU.add))
            nc.vector.tensor_scalar(loops[:, 0:1], stat[:, 13:14], float(E // 2 - 1), None, ALU.add).then_inc(loops_made, 1)
            xeT_lo(0, 0)
            dve.wait_ge(route_exp, 1)
            link(nc.vector.tensor_reduce(p_g, g_exp, AX.X, ALU.add))
            link(nc.vector.reciprocal(p_g, p_g))
            dve.wait_ge(route_exp, 2)
            link(nc.vector.tensor_scalar(w1, diff, 1.0, None, ALU.add))
            link(nc.vector.reciprocal(w1, w1))
            link(nc.vector.tensor_tensor(w2, diff, w1, ALU.mult))
            link(nc.vector.tensor_tensor(w1, w1, p_g, ALU.mult))
            link(nc.vector.tensor_tensor(w2, w2, p_g, ALU.mult))
            link(nc.vector.tensor_tensor(weight, e1, wide(w1, E), ALU.mult))
            link(nc.vector.tensor_tensor(tmp, e2, wide(w2, E), ALU.mult))
            link(nc.vector.tensor_tensor(weight, weight, tmp, ALU.add))
            for k in range(2):
                link(nc.vector.tensor_copy(comb[:, :, :, k], weight))
                link(nc.vector.tensor_tensor(weight, weight, comb[:, :, :, k], ALU.subtract))
            nc.vector.tensor_copy(comb[:, :, :, 2], weight).then_inc(comb_made, 1)

            dve.wait_ge(loops_made, 1)
            last_pair = nc.vector.value_load(loops[0:1, 0:1], min_val=E // 2 - 1, max_val=MAX_ROUNDS * E // 2 - 1)

            def expert_lo(j, m0, k):
                m = m0 + k // 2
                N0 = DENSE + 2 * m0 + k
                dve.wait_ge(hi_made, 12 * j + (N0 + 1))
                nc.vector.tensor_tensor(conv_half(lo, N0), raw_half(expert_slot(m), k % 2, True),
                                        conv_half(hi, N0).bitcast(f32), ALU.subtract).then_inc(lo_made, 1)

            def y_out_lo(i, par):
                dve.wait_ge(y_hi, i + 1)
                nc.vector.scalar_tensor_tensor(y_parts[:, 1, :], ps[:, 6:8, :].rearrange("p a b -> p (a b)"),
                                               comb_slot[:, par:par + 1], y_parts[:, 0, :].bitcast(f32),
                                               ALU.mult, ALU.subtract).then_inc(y_lo, 1)

            def step(j, r, put_of):
                first = isinstance(j, int)
                i = 2 * j + r
                start = first and i == 0
                m0 = 0 if start else 3 * r - 1
                expert_lo(j, m0, 2)
                expert_lo(j, m0, 3)
                if not start:
                    if first:
                        dve.wait_ge(rank_rows_loaded, 16)
                    else:
                        dve.wait_ge(combined, i - 1)
                    e_col, t_col = put_of
                    nc.vector.tensor_scalar(put[:, :], rank_rows[:, e_col, :].rearrange("p o t -> p (o t)"),
                                            c_("slot_col")[:, t_col], None, ALU.is_equal).then_inc(put_made, 1)
                xeT_lo(i + 1, (r + 1) % 2)
                expert_lo(j, m0, 4)
                expert_lo(j, m0, 5)
                dve.wait_ge(slotted, i + 1)
                nc.vector.tensor_reduce(comb_slot[:, r:r + 1], G0[:, 0:3], AX.X, ALU.add).then_inc(comb_slot_made, 1)
                make_pick(r, slice(r + 2, r + 3) if first else bass.ds(2 * j + (r + 2), 1))
                if not start:
                    expert_lo(j, m0, 6)
                    expert_lo(j, m0, 7)
                    y_out_lo(i - 1, (r + 1) % 2)
                dve.wait_ge(silu_made, i + 1)
                nc.vector.tensor_tensor(h_sb[:, :, :], silu_sb[:, :, :],
                                        G1.rearrange("p (a b) -> p a b", b=SLOTS)[:, 4:8, :], ALU.mult).then_inc(h_made, 1)

            dve.wait_ge(comb_made, 1)
            step(0, 0, None)
            step(0, 1, (slice(0, 1), slice(0, 1)))
            with dve.Fori(1, last_pair + 1) as j:
                step(j, 0, (bass.ds((j + (E // 2 - 1)) % (E // 2) * 2 + 1, 1), bass.ds(2 * j - 1, 1)))
                step(j, 1, (bass.ds(j % (E // 2) * 2, 1), bass.ds(2 * j, 1)))
            y_out_lo(2 * last_pair + 1, 1)
            dve.wait_ge(combined, 2 * last_pair + 1)
            nc.vector.tensor_scalar(put[:, :], rank_rows[:, E - 1, :], c_("slot_col")[:, bass.ds(2 * last_pair + 1, 1)],
                                    None, ALU.is_equal).then_inc(put_made, 1)

            dve.wait_ge(sumsq3, 2)
            rstd(0, 4, 6, 20)
            dve.wait_ge(final_loaded, 16)
            for t in range(TT):
                nc.vector.scalar_tensor_tensor(x3[:, t, :], sums(t), stat[:, 20 + t:21 + t], raw[:, 0, 0:D],
                                               ALU.mult, ALU.mult).then_inc(out_made, 1)

        @block.tensor
        def _(pe):
            mm = nc.tensor.matmul
            pe.wait_ge(cst_loaded, 16)

            def turn(dst_bank, src, need, done):
                for k in range(2):
                    for t in range(TT):
                        last = nc.tensor.transpose(ps[:, dst_bank, k * T + t * P:k * T + (t + 1) * P], src(t, k), ident)
                last.then_inc(done, 1)

            pe.wait_ge(scaled, 2)
            for c2 in range(4):
                turn(4 + c2, lambda t, k: x_sb[:, t, (2 * c2 + k) * P:(2 * c2 + k + 1) * P], None, xT_turned)

            def x2_turn(c2):
                pe.wait_ge(x2_made, 2 * (c2 // 2) + 2)
                if c2 >= 2:
                    pe.wait_ge(zT_made, 2 * (c2 - 2) + 2)
                turn(6 + c2 % 2, lambda t, k: x2[:, t, (2 * c2 + k) * P:(2 * c2 + k + 1) * P], None, zT_turned)

            def columns(N, acts, arriving=False):
                w_hi, w_lo = conv_half(hi, N), conv_half(lo, N)
                for c in range(2):
                    dst = ps[:, N % RING, c * T:(c + 1) * T]
                    for k in range(KT):
                        if arriving and c == 0:
                            pe.wait_ge(x_lo, k + 1)
                        mm(dst, w_hi[:, k, c * P:(c + 1) * P], acts[:, 0, k, :], start=(k == 0), stop=False)
                        mm(dst, w_hi[:, k, c * P:(c + 1) * P], acts[:, 1, k, :], start=False, stop=False)
                        last = mm(dst, w_lo[:, k, c * P:(c + 1) * P], acts[:, 0, k, :], start=False, stop=(k == KT - 1))
                last.then_inc(half_used, 1)

            def contraction(N, acts):
                h = N % 2
                w_hi = hi[:, N % CONV, :].rearrange("p (k n) -> p k n", n=512)
                w_lo = lo[:, N % CONV, :].rearrange("p (k n) -> p k n", n=512)
                for t in range(TT):
                    dst = ps[:, (N - h + t) % RING, :]
                    for k in range(4):
                        tok = slice(t * P, (t + 1) * P)
                        first, end = h == 0 and k == 0, h == 1 and k == 3
                        mm(dst, acts[:, 0, 4 * h + k, tok], w_hi[:, k, :], start=first, stop=False, skip_group_check=True)
                        mm(dst, acts[:, 1, 4 * h + k, tok], w_hi[:, k, :], start=False, stop=False, skip_group_check=True)
                        last = mm(dst, acts[:, 0, 4 * h + k, tok], w_lo[:, k, :], start=False, stop=end, skip_group_check=True)
                last.then_inc(half_used, 1)

            for N in range(RING):
                pe.wait_ge(lo_made, N + 1)
                columns(N, inA, arriving=(N == 0))
            with pe.Fori(1, 2 * LOOPED // RING) as it:
                for b in range(RING):
                    pe.wait_ge(lo_made, RING * it + (b + 1))
                    pe.wait_ge(bank_free[b], it)
                    columns(b, inA)

            def scores(h):
                pe.wait_ge(q_made, h // 2 * 2 + 2)
                pe.wait_ge(k_made, h // 2 * 2 + 2)
                if h < 2:
                    pe.wait_ge(mem_lo, KT)
                else:
                    pe.wait_ge(exps, 2 * (h - 1))
                for t in range(TT):
                    for c in range(2):
                        last = mm(ps[:, 6 + h % 2, t * T:(t + 1) * T], qT[:, 2 * h + c, t * P:(t + 1) * P],
                                  kT[:, 2 * h + c, :], start=(c == 0), stop=(c == 1))
                last.then_inc(scored, 1)

            def turn_probs(h):
                pe.wait_ge(prob_made, 2 * h + 2)
                if h < 2:
                    pe.wait_ge(exps, 2 * (h + 2) + 2)
                else:
                    pe.wait_ge(probsT_made, h - 1)
                for m in range(TT):
                    for t in range(TT):
                        last = nc.tensor.transpose(ps[:, 6 + h % 2, m * T + t * P:m * T + (t + 1) * P],
                                                   probs[:, h, t, m * P:(m + 1) * P], ident)
                last.then_inc(probs_turned, 1)

            def attend(h):
                pe.wait_ge(v_made, h // 2 + 1)
                pe.wait_ge(probsT_made, 4 if h < 2 else 4)
                if h >= 2:
                    pe.wait_ge(att_lo, h - 1)
                for c in range(2):
                    for m in range(TT):
                        last = mm(ps[:, 6 + h % 2, c * T:(c + 1) * T],
                                  v_sb[:, m, (2 * h + c) * P:(2 * h + c + 1) * P], probsT[:, h, m, :],
                                  start=(m == 0), stop=(m == TT - 1))
                last.then_inc(attended, 1)

            def mem_turn(c2):
                if c2 >= 2:
                    pe.wait_ge(mem_lo, 2 * (c2 - 2) + 2)
                turn(6 + c2 % 2, lambda t, k: mem_sb[:, t, (2 * c2 + k) * P:(2 * c2 + k + 1) * P], None, memT_turned)

            def channel_sum(bank, src, needs, done):
                for c in range(KT):
                    if c in needs:
                        pe.wait_ge(*needs[c])
                    last = mm(ps[:, bank, 0:T], ones, src[:, c, :], start=(c == 0), stop=(c == KT - 1))
                last.then_inc(done, 1)

            F = FIRST
            extra = {F["q"] - 1: [lambda: pe.wait_ge(scaled, 4), lambda: mem_turn(0), lambda: mem_turn(1)],
                     F["q"] + 1: [lambda: mem_turn(2), lambda: mem_turn(3)],
                     F["v"] - 1: [lambda: scores(0), lambda: scores(1)],
                     F["v"] + 1: [lambda: scores(2), lambda: scores(3)],
                     F["v"] + 2: [lambda: turn_probs(0), lambda: turn_probs(1)],
                     F["v"] + 3: [lambda: turn_probs(2), lambda: turn_probs(3)],
                     F["gate2"]: [lambda: attend(0), lambda: attend(1)],
                     F["gate2"] + 1: [lambda: attend(2), lambda: attend(3)],
                     F["out_x"]: [lambda: channel_sum(6, conv, {0: (conv_step, TAPS_B * DVE_TILES),
                                                                      DVE_TILES: (conv_pool, (2 * TAPS_B - 1) * (KT - DVE_TILES))},
                                                            ln_sum)],
                     F["out_x"] + 2: [lambda: channel_sum(7, u_sb, {0: (ln_square, 1), 4: (ln_square, 2)}, ln_sumsq)],
                     F["w_o"] + 2: [lambda: x2_turn(0), lambda: x2_turn(1)]}
            ready = {F["out_a"]: (a_lo, 4), F["k"]: (mem_lo, KT), F["out_x"]: (att_lo, HEADS),
                     F["out_b"]: (b_lo, 1), F["w_o"]: (merged_lo, 2), F["w_o"] + 1: (merged_lo, 4)}
            for N in range(2 * LOOPED, DENSE):
                name = UNITS[N // 2][0]
                if N in ready:
                    pe.wait_ge(*ready[N])
                acts = inB if name in ("out_a", "k", "v", "out_x", "out_b") else inA
                pe.wait_ge(lo_made, N + 1)
                if name in K_SPLIT:
                    if N % 2 == 0:
                        for t in range(TT):
                            pe.wait_ge(bank_free[(N + t) % RING], N // RING)
                    contraction(N, acts)
                else:
                    pe.wait_ge(bank_free[N % RING], N // RING)
                    columns(N, acts)
                for work in extra.get(N, ()):
                    work()

            x2_turn(2)
            x2_turn(3)
            pe.wait_ge(wr_loaded, 32)
            NL = GROUPS + E
            for t in range(TT):
                for c in range(KT):
                    if t == 0:
                        pe.wait_ge(zT_made, c + 1)
                    last = mm(ps[:, 4, 64 * t:64 * t + NL], zT[:, c, t * P:(t + 1) * P], wr[:, c, :],
                              start=(c == 0), stop=(c == KT - 1))
                last.then_inc(logits_done, 1)
            for b in range(4):
                g = b % 2
                mm(Y[b], ident, x2[:, b // 2, g * 512:(g + 1) * 512], start=True, stop=False, skip_group_check=True)
            pe.wait_ge(member_made, 1)
            member = route[:, 360:360 + TT * E].rearrange("p (t e) -> p t e", e=E)
            mm(ps[:, 5, 0:E], before, member[:, 0, :], start=True, stop=True)
            mm(ps[:, 5, E:2 * E], ones, member[:, 0, :], start=True, stop=False)
            mm(ps[:, 5, E:2 * E], before, member[:, 1, :], start=False, stop=True)
            mm(ps[:, 5, 2 * E:3 * E], ones, member[:, 0, :], start=True, stop=False)
            mm(ps[:, 5, 2 * E:3 * E], ones, member[:, 1, :], start=False, stop=True).then_inc(ranked, 1)

            def gather(i, par):
                pe.wait_ge(pick_made, i + 1)
                for c in range(KT):
                    dst = ps[:, 6, c * SLOTS:(c + 1) * SLOTS]
                    for k in range(3 * TT):
                        part_, t = k // TT, k % TT
                        if isinstance(i, int) and i == 0 and c == 0:
                            pe.wait_ge((z_part0, z_part1, z_part2)[part_], t + 1)
                        last = mm(dst, z_parts[:, part_, t, c * P:(c + 1) * P], pick[:, par, t, 0:SLOTS],
                                  start=(k == 0), stop=(k == 3 * TT - 1))
                last.then_inc(gathered, 1)

            def gate_or_up(j, m0, k, par):
                N = DENSE + 2 * m0 + k
                pe.wait_ge(lo_made, 12 * j + (N + 1))
                dst = G0 if k < 2 else G1
                for kt in range(4):
                    for w in (hi, lo):
                        last = mm(dst, xeT[:, par, 4 * (k % 2) + kt, :], w[:, N % CONV, kt * 512:(kt + 1) * 512],
                                  start=(k % 2 == 0 and kt == 0 and w is hi),
                                  stop=(k % 2 == 1 and kt == 3 and w is lo), skip_group_check=True)
                last.then_inc(half_used, 1)

            def down(j, m0, k, h):
                N = DENSE + 2 * m0 + k
                pe.wait_ge(lo_made, 12 * j + (N + 1))
                for kt in range(2):
                    for w in (hi, lo):
                        for g in range(2):
                            a = kt * D + g * 512
                            last = mm(DN[g], hT[:, 2 * h + kt, :], w[:, N % CONV, a:a + 512],
                                      start=(h == 0 and kt == 0 and w is hi),
                                      stop=(h == 1 and kt == 1 and w is lo), skip_group_check=True)
                last.then_inc(half_used, 1)

            def combine(i):
                pe.wait_ge(put_made, i + 1)
                pe.wait_ge(y_lo, i + 1)
                for t in range(TT):
                    for part_ in range(2):
                        for g in range(2):
                            last = mm(Y[2 * t + g], put[:, t * P:(t + 1) * P], y_parts[:, part_, g * 512:(g + 1) * 512],
                                      start=False, stop=False, skip_group_check=True)
                last.then_inc(combined, 1)

            gather(0, 0)
            pe.wait_ge(loops_made, 1)
            rank = rank_tab[:, :, 0:E]
            for t in range(TT):
                nc.tensor.transpose(ps[0:E, 5, 256 + t * P:256 + (t + 1) * P], rank[:, t, :], ident).then_inc(rank_turned, 1)
            last_pair = nc.tensor.value_load(loops[0:1, 0:1], min_val=E // 2 - 1, max_val=MAX_ROUNDS * E // 2 - 1)

            def step(j, r, e_col):
                first = isinstance(j, int)
                i = 2 * j + r
                start = first and i == 0
                m0 = 0 if start else 3 * r - 1
                pe.wait_ge(xeT_made, i + 1)
                if not start:
                    pe.wait_ge(comb_slot_made, i)
                gate_or_up(j, m0, 0, r)
                gate_or_up(j, m0, 1, r)
                if not first:
                    combine(i - 2)
                gather(i + 1, (r + 1) % 2)
                if not start:
                    pe.wait_ge(h_made, i)
                elif start:
                    pe.wait_ge(rank_copied, 1)
                gate_or_up(j, m0, 2, r)
                gate_or_up(j, m0, 3, r)
                pe.wait_ge(gate_out, i + 1)
                for t in range(TT):
                    if start and t == 0:
                        pe.wait_ge(comb_made, 1)
                    last = mm(G0[:, 0:3], pick[:, r, t, :], comb[:, t, e_col, 0:3].rearrange("p a b -> p (a b)"),
                              start=(t == 0), stop=(t == TT - 1), skip_group_check=True)
                last.then_inc(slotted, 1)
                if not start:
                    pe.wait_ge(xeT_made, i + 2)
                    pe.wait_ge(h_lo, i)
                    down(j, m0, 4, 0)
                    down(j, m0, 5, 1)
                pe.wait_ge(up_out, i + 1)
                for f in range(2 * FF // P):
                    last = mm(G1[:, f * SLOTS:(f + 1) * SLOTS], gu_sb[:, f * P:(f + 1) * P], fold,
                              start=True, stop=True, skip_group_check=True)
                last.then_inc(folded, 1)

            step(0, 0, slice(0, 1))
            step(0, 1, slice(1, 2))
            with pe.Fori(1, last_pair + 1) as j:
                step(j, 0, bass.ds(j % (E // 2) * 2, 1))
                step(j, 1, bass.ds(j % (E // 2) * 2 + 1, 1))
            combine(2 * last_pair)
            pe.wait_ge(xeT_made, 2 * last_pair + 3)
            pe.wait_ge(h_lo, 2 * last_pair + 2)
            down(last_pair, 5, 0, 0)
            down(last_pair, 5, 1, 1)
            combine(2 * last_pair + 1)


def kernel(x, mem, mix_norm_g, mem_norm_g, w_in, b_gate, conv_a_w, w_out_a, b_glu,
           conv_b_w, conv_b_b, ln_b_g, ln_b_b, w_out_b, b_out_b, w_kv, w_out_x, w_o,
           ffn_norm_g, w_group, b_group, w_router, b_router, w_gate_up, w_down, final_norm_g):
    import numpy as np
    import concourse.bacc as bacc
    from concourse.bass_utils import run_bass_kernel_spmd as run

    def per_channel(v):
        return np.asarray(v).reshape(-1, P).T

    consts = np.zeros((P, N_CST), np.float32)

    def put_const(name, values):
        consts[:, CST[name][0]:CST[name][1]] = values

    put_const("ident", np.eye(P))
    put_const("ones", 1.0)
    put_const("before", np.triu(np.ones((P, P)), 1))
    put_const("fold", np.concatenate([np.eye(SLOTS), np.eye(SLOTS)]))
    put_const("slot_row", np.arange(P) % SLOTS)
    put_const("slot_col", np.arange(P)[:, None] % SLOTS + SLOTS * (np.arange(MAX_ROUNDS * E)[None, :] // E))
    put_const("desc_g", np.arange(GROUPS, 0, -1))
    put_const("desc_e", np.arange(E, 0, -1))
    vectors = (mix_norm_g, mem_norm_g, b_gate, b_glu, conv_a_w, conv_b_w, conv_b_b, ln_b_g, ln_b_b, b_out_b, ffn_norm_g)
    arrays = {
        "x": x[0], "mem": mem[0], "w_in": w_in[0], "w_out_a": w_out_a[0], "w_out_b": w_out_b[0],
        "w_out_x": w_out_x[0], "w_kv": w_kv[0], "w_o": w_o[0], "w_gate_up": w_gate_up[0], "w_down": w_down[0],
        "w_route": np.concatenate([w_group[0], w_router[0]], axis=1),
        "cols": np.concatenate([per_channel(v[0]) for v in vectors], axis=1),
        "rows": np.stack([np.asarray(ffn_norm_g[0]), np.asarray(final_norm_g)]),
        "b_route": np.concatenate([b_group[0], b_router[0]])[None, :],
        "consts": consts,
    }
    nc = bacc.Bacc("TRN2", target_bir_lowering=False, num_devices=1, dynamic_dma_scratch_size=1024)
    feeds, args = {}, []
    for name, a in arrays.items():
        a = np.ascontiguousarray(a)
        feeds[f"in_{name}"] = a
        args.append(nc.dram_tensor(f"in_{name}", a.shape, mybir.dt.from_np(a.dtype), kind="ExternalInput").ap())
    out = nc.dram_tensor("out", (T, D), f32, kind="ExternalOutput").ap()
    hybrid_moe_kernel(nc, *args, out)
    return run(nc, [feeds], core_ids=[0]).results[0]["out"].reshape(1, T, D)
```

```python
import concourse.bass as bass
from concourse import mybir
from contextlib import ExitStack

D = 1024
T = 256
P = 128
KT = D // P
TT = T // P
HEADS = 4
HEAD_DIM = D // HEADS
TAPS_A = 3
TAPS_B = 31
GROUPS = 4
EPG = 8
E = GROUPS * EPG
FF = 512
EPS = 1e-6
SLOTS = 64
MAX_ROUNDS = T // SLOTS
HALF = 2048
UNIT = 2 * HALF
RAW = 6
RAW_DENSE = 4
CONV = 3
BIG = 1.0e30

COL = {}
_at = 0
for _name, _n in (("mix_g", 1), ("mem_g", 1), ("b_gate", 3), ("b_glu", 2), ("conv_a", TAPS_A),
                  ("conv_b", TAPS_B), ("conv_b_b", 1), ("ln_g", 1), ("ln_b", 1), ("b_out", 1), ("ffn_g", 1)):
    COL[_name] = _at
    _at += _n * KT
N_COLS = _at

CST = {}
_at = 0
for _name, _n in (("ident", P), ("ones", P), ("before", P), ("fold", SLOTS), ("slot_row", P), ("desc_g", GROUPS), ("desc_e", E)):
    CST[_name] = (_at, _at + _n)
    _at += _n
N_CST = _at

UNITS = []
for _g in range(2):
    UNITS += [("glu_value", "w_in", 3 * D + 512 * _g), ("glu_gate", "w_in", 4 * D + 512 * _g)]
for _g in range(2):
    UNITS += [("a_value", "w_in", 512 * _g), ("a_c", "w_in", 2 * D + 512 * _g), ("a_b", "w_in", D + 512 * _g)]
for _name, _m, _c in (("gate0", "w_in", 6 * D), ("out_a", "w_out_a", 0), ("q", "w_in", 5 * D),
                      ("k", "w_kv", 0), ("v", "w_kv", D), ("gate2", "w_in", 8 * D),
                      ("out_x", "w_out_x", 0), ("gate1", "w_in", 7 * D), ("out_b", "w_out_b", 0),
                      ("w_o", "w_o", 0)):
    UNITS += [(_name, _m, _c + 512 * _g) for _g in range(2)]
N_UNITS = len(UNITS)
DENSE = 2 * N_UNITS
FIRST = {}
for _u, (_name, _, _) in enumerate(UNITS):
    FIRST.setdefault(_name, 2 * _u)
K_SPLIT = ("v", "w_o")
RING = 6
DVE_TILES = 6
LOOPED = 12

f32 = mybir.dt.float32
r32 = mybir.dt.float32r
bf16 = mybir.dt.bfloat16
i32 = mybir.dt.int32
ACT = mybir.ActivationFunctionType
ALU = mybir.AluOpType
AX = mybir.AxisListType


def hybrid_moe_kernel(nc, x, mem, w_in, w_out_a, w_out_b, w_out_x, w_kv, w_o, w_gate_up, w_down,
                      w_route, cols, rows, b_route, consts, out):
    matrices = {"w_in": w_in, "w_out_a": w_out_a, "w_out_b": w_out_b, "w_out_x": w_out_x,
                "w_kv": w_kv, "w_o": w_o}
    ctx = ExitStack()
    with ctx:
        base = (nc.sbuf_base + 63) // 64 * 64

        def at(name, offset, shape, dt=f32):
            return nc.alloc_sbuf_tensor_at(name, [P] + shape, dt, offset=base + offset)

        KB = 1024
        raw = at("raw", 0, [RAW, UNIT])
        hi = at("hi", 96 * KB, [CONV, HALF], r32)
        lo = at("lo", 120 * KB, [CONV, HALF], r32)
        kT = at("kT", 64 * KB, [KT, T])
        v_sb = at("v_sb", 72 * KB, [TT, D])
        qT = at("qT", 80 * KB, [KT, T])
        probsT = at("probsT", 80 * KB, [HEADS, TT, T])
        mem_sb = at("mem_sb", 88 * KB, [TT, D])
        probs = at("probs", 88 * KB, [HEADS, TT, T])
        A0 = 144 * KB
        inA = at("inA", A0, [2, KT, T], r32)
        z_parts = at("z_parts", A0, [3, TT, D], bf16)
        inB = at("inB", A0 + 16 * KB, [2, KT, T], r32)
        ffn_row = at("ffn_row", A0 + 16 * KB, [D])
        route = at("route", A0 + 28 * KB, [768])
        xeT = at("xeT", A0 + 16 * KB, [2, KT, 2 * SLOTS], r32)
        y_last = at("y_last", A0 + 16 * KB, [2, D], r32)
        y_parts = at("y_parts", A0 + 24 * KB, [2, D], r32)
        B0 = A0 + 32 * KB
        a_mid = at("a_mid", B0, [KT, T])
        merged = at("merged", B0, [KT, T])
        x2 = at("x2", B0, [TT, D])
        gate = at("gate", B0 + 8 * KB, [KT, T])
        zT = at("zT", B0 + 8 * KB, [KT, T])
        conv = at("conv", B0 + 16 * KB, [KT, T])
        x_again = at("x_again", B0 + 16 * KB, [TT, D])
        lo_last = at("lo_last", B0 + 8 * KB, [HALF], r32)
        hi_last = at("hi_last", B0 + 16 * KB, [HALF], r32)
        u_sb = at("u_sb", B0 + 24 * KB, [KT, T])
        x_sb = at("x_sb", B0 + 24 * KB, [TT, D])
        z_sb = at("z_sb", B0 + 24 * KB, [TT, D])
        gu_sb = at("gu_sb", B0 + 24 * KB, [2 * FF])
        silu_sb = at("silu_sb", B0 + 28 * KB, [4, SLOTS])
        h_sb = at("h_sb", B0 + 29 * KB, [4, SLOTS])
        x3 = at("x3", B0 + 24 * KB, [TT, D])
        S0 = B0 + 32 * KB
        pick = at("pick", S0, [2, TT, 2 * SLOTS], bf16)
        put = at("put", A0 + 12 * KB, [2, T], r32)
        ident_bf = at("ident_bf", A0 + 14 * KB, [P], bf16)
        hT = at("hT", S0 + 3 * KB, [4, 2 * SLOTS], r32)
        part = at("part", S0, [2, T])
        square_out = at("square_out", S0, [512])
        conv_prod = at("conv_prod", S0 + 2 * KB, [KT - DVE_TILES, T])
        ln_mean = at("ln_mean", S0 + 2 * KB, [T])
        ln_rstd = at("ln_rstd", S0 + 3 * KB, [T])
        S1 = S0 + 5 * KB
        cst = at("cst", S1, [N_CST])
        S2 = S1 + (4 * N_CST + 63) // 64 * 64
        col = at("col", S2, [N_COLS])
        S3 = S2 + (4 * N_COLS + 63) // 64 * 64
        wr = at("wr", S3, [KT, GROUPS + E])
        S4 = S3 + (4 * KT * (GROUPS + E) + 63) // 64 * 64
        rank_tab = at("rank_tab", S4, [TT, (MAX_ROUNDS + 1) * E])
        S5 = S4 + 4 * TT * (MAX_ROUNDS + 1) * E
        comb = at("comb", S5, [TT, E, 4], bf16)
        S6 = S5 + 8 * TT * E
        stat = at("stat", S6, [24])
        comb_slot = at("comb_slot", S6 + 96, [2])
        loops = at("loops", S6 + 128, [2], i32)
        br = at("br", S6 + 160, [GROUPS + E])

        ps = ctx.enter_context(nc.psum_tensor("ps", [P, 8, 512], f32))

        def c_(name):
            return cst[:, CST[name][0]:CST[name][1]]

        ident, ones, before, fold = c_("ident"), c_("ones"), c_("before"), c_("fold")

        def vec(name, c, k=0):
            a = COL[name] + k * KT + c
            return col[:, a:a + 1]

        def sem(name):
            return ctx.enter_context(nc.semaphore(name))

        first_loaded = sem("first_loaded")
        raw_loaded = [sem(f"raw_loaded{s}") for s in range(RAW)]
        hi_made, lo_made, half_used = sem("hi_made"), sem("lo_made"), sem("half_used")
        bank_free = [sem(f"bank_free{b}") for b in range(RING)]
        x_loaded, mem_loaded, cst_loaded, col_loaded = map(sem, ("x_loaded", "mem_loaded", "cst_loaded", "col_loaded"))
        wr_loaded, ffn_loaded, final_loaded, xagain_loaded = map(sem, ("wr_loaded", "ffn_loaded", "final_loaded", "xagain_loaded"))
        sumsq, meansq, root, scaled, xT_turned, x_hi, x_lo = map(sem, ("sumsq", "meansq", "root", "scaled", "xT_turned", "x_hi", "x_lo"))
        memT_turned, mem_hi, mem_lo = map(sem, ("memT_turned", "mem_hi", "mem_lo"))
        glu_value, glu_gate, u_ready = map(sem, ("glu_value", "glu_gate", "u_ready"))
        a_value, a_cv, a_prod, a_hi, a_lo = map(sem, ("a_value", "a_cv", "a_prod", "a_hi", "a_lo"))
        gate_made, merged_a, merged_x, merged_all, merged_hi, merged_lo = map(
            sem, ("gate_made", "merged_a", "merged_x", "merged_all", "merged_hi", "merged_lo"))
        q_made, k_made, v_made = map(sem, ("q_made", "k_made", "v_made"))
        scored, score_max, exps, prob_made, probs_turned, probsT_made, attended, att_hi, att_lo = map(
            sem, ("scored", "score_max", "exps", "prob_made", "probs_turned", "probsT_made", "attended", "att_hi", "att_lo"))
        conv_step, ln_sum, ln_centred, ln_square, ln_sumsq, ln_var, ln_root, ln_scaled, b_silu, b_hi, b_lo = map(
            sem, ("conv_step", "ln_sum", "ln_centred", "ln_square", "ln_sumsq", "ln_var", "ln_root", "ln_scaled", "b_silu", "b_hi", "b_lo"))
        x2_made, z_made, z_part0, z_rest, z_part1, z_part2, zT_turned, zT_made, logits_done = map(
            sem, ("x2_made", "z_made", "z_part0", "z_rest", "z_part1", "z_part2", "zT_turned", "zT_made", "logits_done"))
        route_for_exp, route_exp, member_made, ranked, rank_made = map(
            sem, ("route_for_exp", "route_exp", "member_made", "ranked", "rank_made"))
        loops_made, comb_made = sem("loops_made"), sem("comb_made")
        pick_made, put_made, gathered, xeT_hi, xeT_made = map(sem, ("pick_made", "put_made", "gathered", "xeT_hi", "xeT_made"))
        gate_out, up_out, slotted, comb_slot_made, folded = map(sem, ("gate_out", "up_out", "slotted", "comb_slot_made", "folded"))
        silu_made, h_made, h_hi, h_lo = map(sem, ("silu_made", "h_made", "h_hi", "h_lo"))
        y_hi, y_lo, y_seeded, combined = map(sem, ("y_hi", "y_lo", "y_seeded", "combined"))
        x3_made, sumsq3, root3, out_made, stored = map(sem, ("x3_made", "sumsq3", "root3", "out_made", "stored"))
        ident_made, w_o_done, inverses, pool_chain = map(sem, ("ident_made", "w_o_done", "inverses", "pool_chain"))
        dve_chain, warm_ready, warm_used = map(sem, ("dve_chain", "warm_ready", "warm_used"))
        conv_pool, ln_mean_made, ln_rstd_made, ln_centred_b, ln_scaled_b = map(
            sem, ("conv_pool", "ln_mean_made", "ln_rstd_made", "ln_centred_b", "ln_scaled_b"))

        X2_BANK = (6, 0, 1, 0)
        LOGIT_BANK = (7, 6)
        Y = [ps[:, b, :] for b in range(4)]
        G0, G1 = ps[:, 4, :], ps[:, 5, :]
        DN = [ps[:, 6, :], ps[:, 7, :]]

        def sums(t):
            return ps[:, 2 * t:2 * t + 2, :].rearrange("p a b -> p (a b)")

        def raw_slot(u):
            return (u + 2) % RAW_DENSE, u // RAW_DENSE

        RAW_BASE = [0] * RAW
        for u in range(N_UNITS):
            RAW_BASE[raw_slot(u)[0]] += 1

        def expert_slot(m):
            return (m + 4) % RAW

        def raw_flat(slot, h):
            return raw[:, slot, h * HALF:(h + 1) * HALF]

        def raw_half(slot, h, k_split):
            flat = raw[:, slot, :]
            if k_split:
                return flat[:, h * HALF:(h + 1) * HALF].rearrange("p (a b) -> p a b", b=T)
            return flat.rearrange("p (a b) -> p a b", b=2 * T)[:, :, h * T:(h + 1) * T]

        def conv_half(buf, N):
            return buf[:, N % CONV, :].rearrange("p (a b) -> p a b", b=T)

        def expert_half(buf, N):
            fourth = hi_last if buf is hi else lo_last
            return fourth[:, :] if N % (CONV + 1) == CONV else buf[:, N % (CONV + 1), :]

        NL = GROUPS + E
        R, route_at = {}, 0
        for name, n in (("logit", NL), ("g_max", 0), ("m1", 0), ("m2", 0), ("low", 0), ("diff", 0), ("p_g", 0),
                        ("w1", 0), ("w2", 0), ("g_exp", GROUPS), ("g_hot", GROUPS), ("e_masked", E), ("e1", E),
                        ("e2", E), ("tmp", E), ("member", E), ("weight", E), ("rank", E)):
            size = TT * max(n, 1)
            R[name] = route[:, route_at:route_at + size]
            if n:
                R[name] = R[name].rearrange("p (t e) -> p t e", e=n)
            route_at += size

        def wide(a, n):
            return a.rearrange("p (t o) -> p t o", o=1).to_broadcast([P, TT, n])

        block = ctx.enter_context(nc.Block())

        @block.sync
        def _(sp):
            sp.dma_start(x_sb[:, :, :], x.rearrange("(t p) d -> p t d", p=P)).then_inc(x_loaded, 16)
            sp.dma_start(cst[:, :], consts).then_inc(cst_loaded, 16)
            sp.dma_start(col[:, :], cols).then_inc(col_loaded, 16)
            for u, (name, matrix, c0) in enumerate(UNITS):
                slot = raw_slot(u)[0]
                if u >= RAW_DENSE:
                    sp.wait_ge(lo_made, 2 * (u - RAW_DENSE) + 2)
                src = matrices[matrix][:, c0:c0 + 512].rearrange("(k p) n -> p k n", p=P)
                dst = raw[:, slot, :].rearrange("p (k n) -> p k n", n=512)
                if u == 0:
                    sp.dma_start(dst[:, :, 0:T], src[:, :, 0:T]).then_inc(first_loaded, 16)
                    sp.dma_start(dst[:, :, T:2 * T], src[:, :, T:2 * T]).then_inc(raw_loaded[slot], 16)
                else:
                    sp.dma_start(dst, src).then_inc(raw_loaded[slot], 16)

            gate_up = w_gate_up.rearrange("(j u) (k p) n -> u p j k n", u=2, p=P)
            down = w_down.rearrange("(j u) (k p) n -> u p j k n", u=2, p=P)

            def load_gate_up(slot, parity, j, c):
                src = gate_up[parity, :, bass.ds(j, 1), :, c * FF:(c + 1) * FF]
                sp.dma_start(raw[:, slot, :].rearrange("p (a k n) -> p a k n", a=1, n=FF), src)\
                    .then_inc(raw_loaded[slot], 16)

            def load_down(slot, parity, j):
                src = down[parity, :, bass.ds(j, 1), :, :]
                sp.dma_start(raw[:, slot, :].rearrange("p (a k n) -> p a k n", a=1, n=D), src)\
                    .then_inc(raw_loaded[slot], 16)

            def lo_of(m):
                return DENSE + 2 * (m - RAW) + 2

            sp.wait_ge(attended, HEADS)
            load_gate_up(expert_slot(0), 0, 0, 0)
            load_gate_up(expert_slot(1), 0, 0, 1)
            for m in (2, 3, 4):
                sp.wait_ge(lo_made, lo_of(m))
                if m < 4:
                    load_gate_up(expert_slot(m), 1, 0, m - 2)
                else:
                    load_down(expert_slot(m), 0, 0)

            def pair(j, j_mod, j_before):
                for r, load in enumerate((lambda s: load_gate_up(s, 0, j_mod, 0),
                                          lambda s: load_gate_up(s, 0, j_mod, 1),
                                          lambda s: load_down(s, 1, j_before),
                                          lambda s: load_gate_up(s, 1, j_mod, 0),
                                          lambda s: load_gate_up(s, 1, j_mod, 1),
                                          lambda s: load_down(s, 0, j_mod))):
                    sp.wait_ge(lo_made, 12 * j + (lo_of(r - 1)))
                    load(expert_slot(5 + r))

            with sp.Fori(1, E // 2) as j:
                pair(j, j, j - 1)
            sp.wait_ge(loops_made, 1)
            last_pair = nc.sync.value_load(loops[0:1, 0:1], min_val=E // 2 - 1, max_val=MAX_ROUNDS * E // 2 - 1)
            with sp.If(last_pair > E // 2 - 1):
                with sp.Fori(E // 2, last_pair + 1) as j:
                    pair(j, j % (E // 2), (j + (E // 2 - 1)) % (E // 2))
            sp.wait_ge(lo_made, 12 * last_pair + lo_of(5))
            load_down(expert_slot(5), 1, E // 2 - 1)
            sp.wait_ge(lo_made, 12 * last_pair + (DENSE + 6))
            sp.dma_start(raw[:, 0, 0:D], rows[1:2, :].to_broadcast([P, D])).then_inc(final_loaded, 16)
            for t in range(TT):
                sp.wait_ge(out_made, t + 1)
                sp.dma_start(out[t * P:(t + 1) * P, :], x3[:, t, :]).then_inc(stored, 16)
            sp.wait_ge(stored, 16 * TT)

        @block.gpsimd
        def _(pool):
            for i in range(4):
                pool.wait_ge(glu_value, i + 1)
                pool.wait_ge(glu_gate, i + 1)
                nc.gpsimd.tensor_tensor(u_sb[:, 2 * i:2 * i + 2, :], u_sb[:, 2 * i:2 * i + 2, :],
                                        gate[:, 2 * i:2 * i + 2, :], ALU.mult).then_inc(u_ready, 1)

            pool_tiles = list(enumerate(range(DVE_TILES, KT)))
            n_pool = len(pool_tiles)
            pool.wait_ge(u_ready, 4)
            pool.wait_ge(sumsq, 4)
            for k, c in pool_tiles:
                nc.gpsimd.tensor_scalar(conv[:, c, :], u_sb[:, c, :], vec("conv_b", c, TAPS_B - 1), vec("conv_b_b", c),
                                        ALU.mult, ALU.add).then_inc(conv_pool, 1)
            for shift in range(1, TAPS_B):
                done = n_pool + 2 * n_pool * (shift - 1)
                for k, c in pool_tiles:
                    pool.wait_ge(conv_pool, done - n_pool + k + 1)
                    nc.gpsimd.tensor_scalar(conv_prod[:, k, shift:T], u_sb[:, c, 0:T - shift],
                                            vec("conv_b", c, TAPS_B - 1 - shift), None, ALU.mult).then_inc(conv_pool, 1)
                for k, c in pool_tiles:
                    pool.wait_ge(conv_pool, done + k + 1)
                    nc.gpsimd.tensor_tensor(conv[:, c, shift:T], conv[:, c, shift:T], conv_prod[:, k, shift:T],
                                            ALU.add).then_inc(conv_pool, 1)
            def all_channels(a):
                return a.rearrange("p (o t) -> p o t", o=1).to_broadcast([P, KT // 2, T])

            pool.wait_ge(ln_mean_made, 1)
            nc.gpsimd.tensor_tensor(conv[:, 4:8, :], conv[:, 4:8, :], all_channels(ln_mean[:, :]),
                                    ALU.subtract).then_inc(ln_centred_b, 1)
            pool.wait_ge(ln_rstd_made, 1)
            nc.gpsimd.tensor_tensor(conv[:, 4:8, :], conv[:, 4:8, :], all_channels(ln_mean[:, :]),
                                    ALU.mult).then_inc(ln_scaled_b, 1)

            for t in range(TT):
                pool.wait_ge(z_part0, t + 1)
                nc.gpsimd.tensor_tensor(z_sb[:, t, :], z_sb[:, t, :], z_parts[:, 0, t, :], ALU.subtract).then_inc(z_rest, 1)
            for t in range(TT):
                pool.wait_ge(z_part1, t + 1)
                nc.gpsimd.tensor_tensor(z_parts[:, 2, t, :], z_sb[:, t, :], z_parts[:, 1, t, :],
                                        ALU.subtract).then_inc(z_part2, 1)

            pool_steps = [0]

            def pool_link(ins):
                pool_steps[0] += 1
                ins.then_inc(pool_chain, 1)
                pool.wait_ge(pool_chain, pool_steps[0])

            w1, w2, diff, p_g = R["w1"], R["w2"], R["diff"], R["p_g"]
            pool.wait_ge(inverses, 2)
            pool.wait_ge(member_made, 1)
            pool_link(nc.gpsimd.tensor_tensor(w1, w1, p_g, ALU.mult))
            pool_link(nc.gpsimd.tensor_tensor(w2, diff, w1, ALU.mult))
            pool_link(nc.gpsimd.tensor_tensor(R["weight"], R["e1"], wide(w1, E), ALU.mult))
            pool_link(nc.gpsimd.tensor_tensor(R["tmp"], R["e2"], wide(w2, E), ALU.mult))
            pool_link(nc.gpsimd.tensor_tensor(R["weight"], R["weight"], R["tmp"], ALU.add))
            for k in range(2):
                pool_link(nc.gpsimd.tensor_copy(comb[:, :, :, k], R["weight"]))
                pool_link(nc.gpsimd.tensor_tensor(R["weight"], R["weight"], comb[:, :, :, k], ALU.subtract))
            nc.gpsimd.tensor_copy(comb[:, :, :, 2], R["weight"]).then_inc(comb_made, 1)

            def hidden_lo(i):
                pool.wait_ge(h_hi, i + 1)
                nc.gpsimd.tensor_tensor(hT[:, :, SLOTS:2 * SLOTS], h_sb[:, :, :], hT[:, :, 0:SLOTS].bitcast(f32),
                                        ALU.subtract).then_inc(h_lo, 1)

            hidden_lo(0)
            hidden_lo(1)
            pool.wait_ge(loops_made, 1)
            last_pair = nc.gpsimd.value_load(loops[0:1, 0:1], min_val=E // 2 - 1, max_val=MAX_ROUNDS * E // 2 - 1)
            with pool.Fori(1, last_pair + 1) as j:
                hidden_lo(2 * j)
                hidden_lo(2 * j + 1)

        def stage_of(n):
            name = UNITS[n // 2][0]
            g = UNITS[n // 2][2] % D // 512
            return name, 2 * g + n % 2

        @block.scalar
        def _(act):
            def make_hi(N, slot, loaded, h, k_split):
                if N == 0:
                    act.wait_ge(first_loaded, 16)
                else:
                    act.wait_ge(raw_loaded[slot], loaded)
                if N >= CONV:
                    act.wait_ge(half_used, N - (CONV - 1))
                return nc.scalar.activation(conv_half(hi, N), raw_half(slot, h, k_split), ACT.Copy)

            def dense_hi(N):
                if N < DENSE:
                    slot, before_ = raw_slot(N // 2)
                    make_hi(N, slot, 16 * (before_ + 1), N % 2, UNITS[N // 2][0] in K_SPLIT).then_inc(hi_made, 1)
                else:
                    m = (N - DENSE) // 2
                    slot = expert_slot(m)
                    make_hi(N, slot, 16 * (RAW_BASE[slot] + 1 + m // RAW), N % 2, True).then_inc(hi_made, 1)

            act.wait_ge(warm_ready, 1)
            nc.scalar.activation(stat[:, 23:24], stat[:, 23:24], ACT.Sqrt).then_inc(warm_used, 1)
            act.wait_ge(x_loaded, 16)
            for t in range(TT):
                nc.scalar.activation(conv[:, 4 * t:4 * t + 4, :].rearrange("p a b -> p (a b)"), x_sb[:, t, :],
                                     ACT.Square, accum_out=stat[:, t:t + 1]).then_inc(sumsq, 1)
            act.wait_ge(meansq, 1)
            nc.scalar.activation(stat[:, 6:8], stat[:, 4:6], ACT.Sqrt).then_inc(root, 1)
            dense_hi(0)
            act.wait_ge(col_loaded, 16)
            for c in range(KT):
                act.wait_ge(xT_turned, c // 2 + 1)
                nc.scalar.activation(inA[:, 0, c, :], ps[:, 4 + c // 2, (c % 2) * T:(c % 2 + 1) * T], ACT.Copy,
                                     scale=vec("mix_g", c)).then_inc(x_hi, 1)
            act.dma_start(mem_sb[:, :, :], mem.rearrange("(t p) d -> p t d", p=P)).then_inc(mem_loaded, 16)
            act.dma_start(wr[:, :, :], w_route.rearrange("(k p) n -> p k n", p=P)).then_inc(wr_loaded, 16)
            act.dma_start(br[:, :], b_route.to_broadcast([P, GROUPS + E])).then_inc(wr_loaded, 16)
            dense_hi(1)
            dense_hi(2)

            def mem_squares():
                act.wait_ge(mem_loaded, 16)
                act.wait_ge(sumsq, 2)
                for t in range(TT):
                    nc.scalar.activation(conv[:, 4 * t:4 * t + 4, :].rearrange("p a b -> p (a b)"), mem_sb[:, t, :],
                                         ACT.Square, accum_out=stat[:, 2 + t:3 + t]).then_inc(sumsq, 1)
                act.wait_ge(meansq, 2)
                nc.scalar.activation(stat[:, 10:12], stat[:, 8:10], ACT.Sqrt).then_inc(root, 1)

            def mem_parts(pair_):
                for c in (2 * pair_, 2 * pair_ + 1):
                    act.wait_ge(memT_turned, pair_ + 1)
                    nc.scalar.activation(inB[:, 0, c, :], ps[:, 6 + pair_ % 2, (c % 2) * T:(c % 2 + 1) * T],
                                         ACT.Copy, scale=vec("mem_g", c)).then_inc(mem_hi, 1)

            def softmax_exp(h):
                for t in range(TT):
                    act.wait_ge(score_max, h + 1)
                    nc.scalar.activation(probs[:, h, t, :], ps[:, 6 + h % 2, t * T:(t + 1) * T], ACT.Exp,
                                         bias=stat[:, 12 + t + 2 * (h % 2):13 + t + 2 * (h % 2)],
                                         scale=HEAD_DIM ** -0.5,
                                         accum_out=stat[:, 16 + t + 2 * (h % 2):17 + t + 2 * (h % 2)]).then_inc(exps, 1)

            def turned_probs(h):
                act.wait_ge(probs_turned, h + 1)
                nc.scalar.activation(probsT[:, h, :, :].rearrange("p a b -> p (a b)"), ps[:, 6 + h % 2, :],
                                     ACT.Copy).then_inc(probsT_made, 1)

            def attention_hi(h):
                act.wait_ge(attended, h + 1)
                nc.scalar.activation(inB[:, 0, 2 * h:2 * h + 2, :].rearrange("p a b -> p (a b)"),
                                     ps[:, 6 + h % 2, :], ACT.Copy).then_inc(att_hi, 1)

            def ln_squares():
                for h, centred in enumerate((ln_centred, ln_centred_b)):
                    act.wait_ge(centred, 1)
                    nc.scalar.activation(u_sb[:, 4 * h:4 * h + 4, :], conv[:, 4 * h:4 * h + 4, :],
                                         ACT.Square).then_inc(ln_square, 1)

            def branch_b_act():
                act.wait_ge(ln_var, 1)
                nc.scalar.activation(ln_rstd[:, :], ln_rstd[:, :], ACT.Sqrt).then_inc(ln_root, 1)
                for c in range(KT):
                    if c % 4 == 0:
                        act.wait_ge((ln_scaled, ln_scaled_b)[c // 4], 1)
                    nc.scalar.activation(u_sb[:, c, :], conv[:, c, :], ACT.Silu, bias=vec("ln_b", c),
                                         scale=vec("ln_g", c)).then_inc(b_silu, 1)

            def branch_b_hi():
                act.wait_ge(b_silu, KT)
                act.dma_start(x_again[:, :, :], x.rearrange("(t p) d -> p t d", p=P)).then_inc(xagain_loaded, 16)
                act.wait_ge(half_used, FIRST["out_x"] + 4)
                nc.scalar.activation(inB[:, 0, :, :], u_sb[:, :, :], ACT.Copy).then_inc(b_hi, 1)

            def expert_xeT(i, par):
                act.wait_ge(gathered, i + 1)
                nc.scalar.activation(xeT[:, par, :, 0:SLOTS], ps[:, 6, :].rearrange("p (a b) -> p a b", b=SLOTS),
                                     ACT.Copy).then_inc(xeT_hi, 1)

            def x2_square(g, t):
                act.wait_ge(x2_made, 2 * g + t + 1)
                act.wait_ge(sumsq, 4 + 2 * g + t)
                nc.scalar.activation(square_out[:, :], x2[:, t, 512 * g:512 * g + 512], ACT.Square,
                                     accum_out=stat[:, 2 * t + g:2 * t + g + 1]).then_inc(sumsq, 1)

            def x2_turned(c2):
                act.wait_ge(zT_turned, c2 + 1)
                for k in range(2):
                    nc.scalar.activation(zT[:, 2 * c2 + k, :], ps[:, X2_BANK[c2], k * T:(k + 1) * T], ACT.Copy,
                                         scale=vec("ffn_g", 2 * c2 + k)).then_inc(zT_made, 1)

            def load_ffn_row():
                act.wait_ge(half_used, FIRST["w_o"])
                act.dma_start(ffn_row[:, :], rows[0:1, :].to_broadcast([P, D])).then_inc(ffn_loaded, 16)

            F = FIRST
            extra = {4: [mem_squares],
                     F["q"] - 1: [lambda: mem_parts(0), lambda: mem_parts(1)],
                     F["q"] + 1: [lambda: mem_parts(2), lambda: mem_parts(3)],
                     F["v"] - 1: [lambda: softmax_exp(0), lambda: softmax_exp(1)],
                     F["v"] + 1: [lambda: softmax_exp(2), lambda: softmax_exp(3)],
                     F["v"] + 2: [lambda: turned_probs(0), lambda: turned_probs(1)],
                     F["v"] + 3: [lambda: turned_probs(2), lambda: turned_probs(3)],
                     F["gate2"]: [lambda: attention_hi(0), lambda: attention_hi(1)],
                     F["gate2"] + 1: [lambda: attention_hi(2), lambda: attention_hi(3)],
                     F["out_x"] + 1: [ln_squares], F["out_x"] + 3: [branch_b_act], F["gate1"]: [branch_b_hi],
                     F["w_o"]: [load_ffn_row], F["w_o"] + 2: [lambda: x2_square(0, 0), lambda: x2_square(0, 1), lambda: x2_turned(0), lambda: x2_turned(1)]}
            gates_done = 0
            for n in range(DENSE):
                name, q4 = stage_of(n)
                bank, b = ps[:, n % RING, :], n % RING
                two = slice(2 * q4, 2 * q4 + 2)
                if name in ("glu_value", "glu_gate", "gate0", "gate1", "gate2", "a_value", "q", "k"):
                    act.wait_ge(half_used, n + 1)
                if name in ("glu_value", "glu_gate"):
                    dst = u_sb if name == "glu_value" else gate
                    fn = ACT.Identity if name == "glu_value" else ACT.Sigmoid
                    for k in range(2):
                        last = nc.scalar.activation(dst[:, 2 * q4 + k, :], bank[:, k * T:(k + 1) * T], fn,
                                                    bias=vec("b_glu", 2 * q4 + k, int(name == "glu_gate")))
                    last.then_inc(bank_free[b], 1)
                    act.wait_ge(bank_free[b], n // RING + 1)
                    act.sem_inc(glu_value if name == "glu_value" else glu_gate, 1)
                elif name in ("gate0", "gate1", "gate2"):
                    if name == "gate0":
                        act.wait_ge(a_lo, 4)
                    elif name == "gate2":
                        act.wait_ge(merged_a, 4)
                    else:
                        act.wait_ge(merged_x, 4)
                    for k in range(2):
                        last = nc.scalar.activation(gate[:, 2 * q4 + k, :], bank[:, k * T:(k + 1) * T], ACT.Sigmoid,
                                                    bias=vec("b_gate", 2 * q4 + k, int(name[-1])))
                    last.then_inc(bank_free[b], 1)
                    act.wait_ge(bank_free[b], n // RING + 1)
                    act.sem_inc(gate_made, 1)
                elif name in ("a_value", "q", "k"):
                    dst, made = {"a_value": (a_mid, a_value), "q": (qT, q_made), "k": (kT, k_made)}[name]
                    nc.scalar.activation(dst[:, two, :].rearrange("p a b -> p (a b)"), bank, ACT.Copy).then_inc(made, 1)
                    act.wait_ge(made, q4 + 1)
                    act.sem_inc(bank_free[b], 1)
                elif name == "a_b":
                    act.wait_ge(a_prod, q4 + 1)
                    nc.scalar.activation(inB[:, 0, two, :], gate[:, two, :], ACT.Copy).then_inc(a_hi, 1)
                elif name == "v" and n % 2 == 1:
                    act.wait_ge(half_used, n + 1)
                    g = q4 // 2
                    for t in range(TT):
                        nc.scalar.activation(v_sb[:, t, 512 * g:512 * g + 512], ps[:, (n - 1 + t) % RING, :],
                                             ACT.Copy).then_inc(bank_free[(n - 1 + t) % RING], 1)
                    for t in range(TT):
                        act.wait_ge(bank_free[(n - 1 + t) % RING], n // RING + 1)
                    act.sem_inc(v_made, 1)
                elif name == "out_b":
                    act.wait_ge(merged_all, q4 + 1)
                    nc.scalar.activation(inA[:, 0, two, :], merged[:, two, :], ACT.Copy).then_inc(merged_hi, 1)
                if n + 3 <= DENSE + 1:
                    dense_hi(n + 3)
                for work in extra.get(n, ()):
                    work()

            def expert_hi(j, m0, k):
                m = m0 + k // 2
                slot = expert_slot(m)
                N0 = DENSE + 2 * m0 + k
                act.wait_ge(raw_loaded[slot], 16 * j + 16 * (RAW_BASE[slot] + 1 + m // RAW))
                act.wait_ge(half_used, 12 * j + (N0 - CONV))
                nc.scalar.activation(expert_half(hi, N0), raw_flat(slot, k % 2), ACT.Copy).then_inc(hi_made, 1)

            x2_square(1, 0)
            act.wait_ge(warm_used, 1)
            nc.scalar.activation(stat[:, 23:24], stat[:, 23:24], ACT.Sqrt).then_inc(warm_used, 1)
            x2_square(1, 1)
            x2_turned(2)
            act.wait_ge(meansq, 3)
            nc.scalar.activation(stat[:, 6:8], stat[:, 4:6], ACT.Sqrt).then_inc(root, 1)
            x2_turned(3)
            for t in range(TT):
                act.wait_ge(z_made, t + 1)
                nc.scalar.activation(z_parts[:, 0, t, :], z_sb[:, t, :], ACT.Copy).then_inc(z_part0, 1)
            act.wait_ge(route_for_exp, 1)
            nc.scalar.activation(R["g_exp"], R["g_exp"], ACT.Exp).then_inc(route_exp, 1)
            act.wait_ge(z_rest, 1)
            nc.scalar.activation(z_parts[:, 1, 0, :], z_sb[:, 0, :], ACT.Copy).then_inc(z_part1, 1)
            dense_hi(DENSE + 2)
            act.wait_ge(z_rest, 2)
            nc.scalar.activation(z_parts[:, 1, 1, :], z_sb[:, 1, :], ACT.Copy).then_inc(z_part1, 1)
            act.wait_ge(route_for_exp, 2)
            nc.scalar.activation(R["diff"], R["diff"], ACT.Exp).then_inc(route_exp, 1)
            act.wait_ge(x2_made, 4)
            expert_hi(0, 0, 3)
            nc.scalar.activation(ident_bf[:, :], ident, ACT.Copy).then_inc(ident_made, 1)
            expert_xeT(0, 0)
            def y_out_hi(i, par, y_parts, bank=6):
                act.wait_ge(comb_slot_made, i + 1)
                nc.scalar.activation(y_parts[:, 0, :], ps[:, bank:bank + 2, :].rearrange("p a b -> p (a b)"), ACT.Copy,
                                     scale=comb_slot[:, par:par + 1]).then_inc(y_hi, 1)

            def hidden_hi(i):
                act.wait_ge(h_made, i + 1)
                nc.scalar.activation(hT[:, :, 0:SLOTS], h_sb[:, :, :], ACT.Copy).then_inc(h_hi, 1)

            def step(j, r):
                first = isinstance(j, int)
                i = 2 * j + r
                m0 = 0 if first and i == 0 else 3 * r - 1
                done = 12 * j + (DENSE + 2 * m0 + 1)

                def more(k):
                    expert_hi(j, m0, k)
                start = first and i == 0
                if not start:
                    more(2)
                    more(3)
                    hidden_hi(i - 1)
                else:
                    more(4)
                act.wait_ge(half_used, done + 1)
                if not start:
                    act.wait_ge(folded, i)
                nc.scalar.activation(gu_sb[:, 0:FF], G0, ACT.Copy).then_inc(gate_out, 1)
                if not start:
                    more(4)
                expert_xeT(i + 1, (r + 1) % 2)
                more(5)
                act.wait_ge(half_used, done + 3)
                nc.scalar.activation(gu_sb[:, FF:2 * FF], G1, ACT.Copy).then_inc(up_out, 1)
                if not start:
                    more(6)
                act.wait_ge(comb_slot_made, i + 1)
                nc.scalar.activation(put[:, r, :], G0[:, T:2 * T], ACT.Copy).then_inc(put_made, 1)
                act.wait_ge(folded, i + 1)
                if not start:
                    act.wait_ge(h_made, i)
                nc.scalar.activation(silu_sb[:, :, :], G1.rearrange("p (a b) -> p a b", b=SLOTS)[:, 0:4, :],
                                     ACT.Silu).then_inc(silu_made, 1)
                if not start:
                    more(7)
                    act.wait_ge(half_used, done + 5)
                    y_out_hi(i - 1, (r + 1) % 2, y_parts)

            step(0, 0)
            step(0, 1)
            act.wait_ge(loops_made, 1)
            last_pair = nc.scalar.value_load(loops[0:1, 0:1], min_val=E // 2 - 1, max_val=MAX_ROUNDS * E // 2 - 1)
            with act.Fori(1, last_pair + 1) as j:
                step(j, 0)
                step(j, 1)
            hidden_hi(2 * last_pair + 1)
            act.wait_ge(half_used, 12 * last_pair + (DENSE + 12))
            y_out_hi(2 * last_pair + 1, 1, y_last, 4)
            nc.scalar.activation(stat[:, 23:24], stat[:, 23:24], ACT.Sqrt).then_inc(warm_used, 1)
            act.wait_ge(warm_used, 3)

            for t in range(TT):
                act.wait_ge(combined, (TT * 2) * last_pair + (TT + t + 1))
                nc.scalar.activation(gate[:, 4 * t:4 * t + 4, :].rearrange("p a b -> p (a b)"), sums(t),
                                     ACT.Square, accum_out=stat[:, t:t + 1]).then_inc(sumsq3, 1)
            act.wait_ge(meansq, 4)
            nc.scalar.activation(stat[:, 6:8], stat[:, 4:6], ACT.Sqrt).then_inc(root, 1)

        @block.vector
        def _(dve):
            chain = [0]

            def link(ins):
                chain[0] += 1
                ins.then_inc(dve_chain, 1)
                dve.wait_ge(dve_chain, chain[0])

            def make_lo(N, slot, h, k_split):
                dve.wait_ge(hi_made, N + 1)
                nc.vector.tensor_tensor(conv_half(lo, N), raw_half(slot, h, k_split), conv_half(hi, N).bitcast(f32),
                                        ALU.subtract).then_inc(lo_made, 1)

            def dense_lo(N):
                if N < DENSE:
                    make_lo(N, raw_slot(N // 2)[0], N % 2, UNITS[N // 2][0] in K_SPLIT)
                else:
                    make_lo(N, expert_slot((N - DENSE) // 2), N % 2, True)

            roots = [0]

            def rstd(sums, mean, rooted, r):
                roots[0] += 1
                nc.vector.tensor_scalar(stat[:, mean:mean + 2], stat[:, sums:sums + 2], 1.0 / D, EPS,
                                        ALU.mult, ALU.add).then_inc(meansq, 1)
                dve.wait_ge(root, roots[0])
                link(nc.vector.reciprocal(stat[:, r:r + 2], stat[:, rooted:rooted + 2]))

            nc.vector.memset(stat[:, 23:24], 1.0).then_inc(warm_ready, 1)
            dve.wait_ge(sumsq, 2)
            rstd(0, 4, 6, 20)
            for t in range(TT):
                nc.vector.tensor_scalar(x_sb[:, t, :], x_sb[:, t, :], stat[:, 20 + t:21 + t], None,
                                        ALU.mult).then_inc(scaled, 1)
            dense_lo(0)
            dve.wait_ge(col_loaded, 16)
            for c in range(KT):
                dve.wait_ge(x_hi, c // 2 * 2 + 2)
                nc.vector.scalar_tensor_tensor(inA[:, 1, c, :], ps[:, 4 + c // 2, (c % 2) * T:(c % 2 + 1) * T],
                                               vec("mix_g", c), inA[:, 0, c, :].bitcast(f32), ALU.mult,
                                               ALU.subtract).then_inc(x_lo, 1)
            dense_lo(1)

            def mem_scale():
                dve.wait_ge(sumsq, 4)
                dve.wait_ge(warm_used, 1)
                rstd(2, 8, 10, 22)
                for t in range(TT):
                    nc.vector.tensor_scalar(mem_sb[:, t, :], mem_sb[:, t, :], stat[:, 22 + t:23 + t], None,
                                            ALU.mult).then_inc(scaled, 1)

            def mem_parts(pair_):
                for c in (2 * pair_, 2 * pair_ + 1):
                    dve.wait_ge(mem_hi, 2 * pair_ + 2)
                    nc.vector.scalar_tensor_tensor(inB[:, 1, c, :], ps[:, 6 + pair_ % 2, (c % 2) * T:(c % 2 + 1) * T],
                                                   vec("mem_g", c), inB[:, 0, c, :].bitcast(f32), ALU.mult,
                                                   ALU.subtract).then_inc(mem_lo, 1)

            def softmax_max(h):
                dve.wait_ge(scored, h + 1)
                if h >= 2:
                    dve.wait_ge(exps, 2 * (h - 1))
                m = stat[:, 12 + 2 * (h % 2):14 + 2 * (h % 2)]
                link(nc.vector.tensor_reduce(m, ps[:, 6 + h % 2, :].rearrange("p (t m) -> p t m", t=TT), AX.X,
                                             ALU.max, negate=True))
                nc.vector.tensor_scalar(m, m, HEAD_DIM ** -0.5, None, ALU.mult).then_inc(score_max, 1)

            def softmax_norm(h):
                dve.wait_ge(exps, 2 * h + 2)
                s = 16 + 2 * (h % 2)
                link(nc.vector.reciprocal(stat[:, s:s + 2], stat[:, s:s + 2]))
                for t in range(TT):
                    nc.vector.tensor_scalar(probs[:, h, t, :], probs[:, h, t, :], stat[:, s + t:s + t + 1], None,
                                            ALU.mult).then_inc(prob_made, 1)

            def attention_lo(h):
                dve.wait_ge(att_hi, h + 1)
                nc.vector.tensor_tensor(inB[:, 1, 2 * h:2 * h + 2, :].rearrange("p a b -> p (a b)"),
                                        ps[:, 6 + h % 2, :],
                                        inB[:, 0, 2 * h:2 * h + 2, :].rearrange("p a b -> p (a b)").bitcast(f32),
                                        ALU.subtract).then_inc(att_lo, 1)

            conv_done = [0]

            def conv_taps(count):
                for s in range(conv_done[0], min(conv_done[0] + count, TAPS_B * DVE_TILES)):
                    shift, c = s // DVE_TILES, s % DVE_TILES
                    w = vec("conv_b", c, TAPS_B - 1 - shift)
                    if shift == 0:
                        dve.wait_ge(u_ready, c // 2 + 1)
                        nc.vector.tensor_scalar(conv[:, c, :], u_sb[:, c, :], w, vec("conv_b_b", c), ALU.mult,
                                                ALU.add).then_inc(conv_step, 1)
                    else:
                        dve.wait_ge(conv_step, s - DVE_TILES + 1)
                        nc.vector.scalar_tensor_tensor(conv[:, c, shift:T], u_sb[:, c, 0:T - shift], w,
                                                       conv[:, c, shift:T], ALU.mult, ALU.add).then_inc(conv_step, 1)
                    conv_done[0] += 1

            def all_channels(a):
                return a.rearrange("p (o t) -> p o t", o=1).to_broadcast([P, KT // 2, T])

            def ln_centre():
                dve.wait_ge(ln_sum, 1)
                nc.vector.tensor_scalar(ln_mean[:, :], ps[:, 6, 0:T], 1.0 / D, None, ALU.mult).then_inc(ln_mean_made, 1)
                dve.wait_ge(ln_mean_made, 1)
                nc.vector.tensor_tensor(conv[:, 0:4, :], conv[:, 0:4, :], all_channels(ln_mean[:, :]),
                                        ALU.subtract).then_inc(ln_centred, 1)

            def ln_variance():
                dve.wait_ge(ln_sumsq, 1)
                nc.vector.tensor_scalar(ln_rstd[:, :], ps[:, 7, 0:T], 1.0 / D, EPS, ALU.mult, ALU.add).then_inc(ln_var, 1)

            def ln_scale():
                dve.wait_ge(ln_root, 1)
                dve.wait_ge(ln_centred_b, 1)
                nc.vector.reciprocal(ln_mean[:, :], ln_rstd[:, :]).then_inc(ln_rstd_made, 1)
                dve.wait_ge(ln_rstd_made, 1)
                dve.wait_ge(ln_centred, 1)
                nc.vector.tensor_tensor(conv[:, 0:4, :], conv[:, 0:4, :], all_channels(ln_mean[:, :]),
                                        ALU.mult).then_inc(ln_scaled, 1)

            def branch_b_lo():
                dve.wait_ge(b_hi, 1)
                nc.vector.tensor_tensor(inB[:, 1, :, :], u_sb[:, :, :], inB[:, 0, :, :].bitcast(f32),
                                        ALU.subtract).then_inc(b_lo, 1)

            F = FIRST
            extra = {4: [mem_scale],
                     F["q"] - 1: [lambda: mem_parts(0), lambda: mem_parts(1)],
                     F["q"] + 1: [lambda: mem_parts(2), lambda: mem_parts(3)],
                     F["v"] - 1: [lambda: softmax_max(0), lambda: softmax_max(1), lambda: softmax_norm(0),
                                  lambda: softmax_norm(1)],
                     F["v"] + 1: [lambda: softmax_max(2), lambda: softmax_max(3), lambda: softmax_norm(2),
                                  lambda: softmax_norm(3)],
                     F["gate2"]: [lambda: attention_lo(0), lambda: attention_lo(1)],
                     F["gate2"] + 1: [lambda: attention_lo(2), lambda: attention_lo(3)],
                     F["out_x"] + 3: [ln_scale], F["gate1"] + 1: [branch_b_lo]}
            urgent = {F["out_x"] + 1: ln_centre, F["out_x"] + 3: ln_variance}
            taps = {"a_value": [7] * 4, "a_c": [2] * 4, "a_b": [3] * 4, "gate0": [7] * 4, "out_a": [6, 6, 6, 3],
                    "q": [7, 3, 7, 7], "k": [7, 7, 7, 0], "v": [7, 0, 7, 7], "gate2": [5, 5, 99, 0]}
            for n in range(DENSE):
                name, q4 = stage_of(n)
                b = n % RING
                bank = ps[:, b, :]
                bank2 = bank.rearrange("p (a b) -> p a b", b=T)
                two = slice(2 * q4, 2 * q4 + 2)
                if name in ("a_c", "a_b", "out_a", "out_x", "out_b"):
                    dve.wait_ge(half_used, n + 1)
                if name == "a_c":
                    dve.wait_ge(a_value, q4 + 1)
                    nc.vector.tensor_tensor(a_mid[:, two, :], bank2, a_mid[:, two, :], ALU.mult).then_inc(bank_free[b], 1)
                    dve.wait_ge(bank_free[b], n // RING + 1)
                    dve.wait_ge(u_ready, 4)
                    for c in (2 * q4, 2 * q4 + 1):
                        nc.vector.tensor_scalar(gate[:, c, :], a_mid[:, c, :], vec("conv_a", c, TAPS_A - 1), None,
                                                ALU.mult).then_inc(a_cv, 1)
                    for shift in range(1, TAPS_A):
                        for c in (2 * q4, 2 * q4 + 1):
                            dve.wait_ge(a_cv, 2 * TAPS_A * q4 + 2 * (shift - 1) + c % 2 + 1)
                            nc.vector.scalar_tensor_tensor(gate[:, c, shift:T], a_mid[:, c, 0:T - shift],
                                                           vec("conv_a", c, TAPS_A - 1 - shift),
                                                           gate[:, c, shift:T], ALU.mult, ALU.add).then_inc(a_cv, 1)
                elif name == "a_b":
                    dve.wait_ge(a_cv, 2 * TAPS_A * (q4 + 1))
                    nc.vector.tensor_tensor(gate[:, two, :], bank2, gate[:, two, :], ALU.mult).then_inc(a_prod, 1)
                    dve.wait_ge(a_prod, q4 + 1)
                    dve.sem_inc(bank_free[b], 1)
                elif name == "out_a":
                    dve.wait_ge(gate_made, q4 + 1)
                    nc.vector.tensor_tensor(merged[:, two, :], bank2, gate[:, two, :], ALU.mult).then_inc(merged_a, 1)
                    dve.wait_ge(merged_a, q4 + 1)
                    dve.sem_inc(bank_free[b], 1)
                elif name == "out_x":
                    dve.wait_ge(gate_made, 4 + q4 + 1)
                    link(nc.vector.tensor_tensor(part[:, :, :], bank2, gate[:, two, :], ALU.mult))
                    dve.sem_inc(bank_free[b], 1)
                    nc.vector.tensor_tensor(merged[:, two, :], merged[:, two, :], part[:, :, :], ALU.add).then_inc(merged_x, 1)
                    dve.wait_ge(merged_x, q4 + 1)
                elif name == "out_b":
                    dve.wait_ge(gate_made, 8 + q4 + 1)
                    for k in range(2):
                        c = 2 * q4 + k
                        link(nc.vector.scalar_tensor_tensor(part[:, k, :], bank2[:, k, :], vec("b_out", c),
                                                            gate[:, c, :], ALU.add, ALU.mult))
                    dve.sem_inc(bank_free[b], 1)
                    nc.vector.tensor_tensor(merged[:, two, :], merged[:, two, :], part[:, :, :], ALU.add).then_inc(merged_all, 1)
                elif name == "w_o" and n % 2 == 1:
                    dve.wait_ge(xagain_loaded, 16)
                    dve.wait_ge(merged_lo, 4)
                    g = q4 // 2
                    for t in range(TT):
                        if t == 0:
                            dve.wait_ge(w_o_done, g + 1)
                        else:
                            dense_lo(n + 2)
                            dve.wait_ge(half_used, n + 1)
                        nc.vector.tensor_tensor(x2[:, t, 512 * g:512 * g + 512], ps[:, (n - 1 + t) % RING, :],
                                                x_again[:, t, 512 * g:512 * g + 512], ALU.add).then_inc(x2_made, 1)
                if n in urgent:
                    urgent[n]()
                if not (name == "w_o" and n % 2 == 1):
                    dense_lo(n + 2)
                if name == "a_b":
                    dve.wait_ge(a_hi, q4 + 1)
                    nc.vector.tensor_tensor(inB[:, 1, two, :], gate[:, two, :], inB[:, 0, two, :].bitcast(f32),
                                            ALU.subtract).then_inc(a_lo, 1)
                elif name == "out_b":
                    dve.wait_ge(merged_hi, q4 + 1)
                    nc.vector.tensor_tensor(inA[:, 1, two, :], merged[:, two, :], inA[:, 0, two, :].bitcast(f32),
                                            ALU.subtract).then_inc(merged_lo, 1)
                for work in extra.get(n, ()):
                    work()
                if name in taps:
                    conv_taps(taps[name][q4])

            def expert_lo(j, m0, k):
                m = m0 + k // 2
                N0 = DENSE + 2 * m0 + k
                dve.wait_ge(hi_made, 12 * j + (N0 + 1))
                nc.vector.tensor_tensor(expert_half(lo, N0), raw_flat(expert_slot(m), k % 2),
                                        expert_half(hi, N0).bitcast(f32), ALU.subtract).then_inc(lo_made, 1)

            dve.wait_ge(sumsq, 8)
            link(nc.vector.tensor_reduce(stat[:, 8:10], stat[:, 0:4].rearrange("p (t g) -> p t g", g=2), AX.X, ALU.add))
            rstd(8, 4, 6, 20)
            dve.wait_ge(ffn_loaded, 16)
            for t in range(TT):
                nc.vector.scalar_tensor_tensor(z_sb[:, t, :], x2[:, t, :], stat[:, 20 + t:21 + t], ffn_row[:, :],
                                               ALU.mult, ALU.mult).then_inc(z_made, 1)

            logit, g_max, g_exp, diff, p_g, w1, g_hot, e_masked, e1, e2, m1, m2, member, rank, low = (
                R[k] for k in ("logit", "g_max", "g_exp", "diff", "p_g", "w1", "g_hot", "e_masked", "e1", "e2",
                               "m1", "m2", "member", "rank", "low"))

            def first_hot(hot, values, top, desc):
                link(nc.vector.tensor_reduce(top, values, AX.X, ALU.max))
                nc.vector.scalar_tensor_tensor(hot[:, 0, :], values[:, 0, :], top[:, 0:1], desc, ALU.is_equal, ALU.mult)
                link(nc.vector.scalar_tensor_tensor(hot[:, 1, :], values[:, 1, :], top[:, 1:2], desc, ALU.is_equal,
                                                    ALU.mult))
                link(nc.vector.tensor_reduce(low, hot, AX.X, ALU.max))

            def is_low(hot, t, n):
                return nc.vector.tensor_scalar(hot[:, t, :], hot[:, t, :], low[:, t:t + 1], None, ALU.is_equal)

            dve.wait_ge(logits_done, 1)
            nc.vector.scalar_tensor_tensor(logit[:, 0, :], ps[:, LOGIT_BANK[0], 0:NL], stat[:, 20:21], br[:, :], ALU.mult, ALU.add)
            link(nc.vector.scalar_tensor_tensor(logit[:, 1, :], ps[:, LOGIT_BANK[1], 0:NL], stat[:, 21:22], br[:, :], ALU.mult, ALU.add))
            first_hot(g_hot, logit[:, :, 0:GROUPS], g_max, c_("desc_g"))
            nc.vector.tensor_tensor(g_exp, logit[:, :, 0:GROUPS], wide(g_max, GROUPS), ALU.subtract).then_inc(route_for_exp, 1)
            is_low(g_hot, 0, GROUPS)
            link(is_low(g_hot, 1, GROUPS))
            link(nc.vector.tensor_scalar(g_hot, g_hot, -1.0, BIG, ALU.add, ALU.mult))
            for t in range(TT):
                ins = nc.vector.tensor_tensor(e_masked[:, t, :].rearrange("p (g e) -> p g e", e=EPG),
                                              logit[:, t, GROUPS:NL].rearrange("p (g e) -> p g e", e=EPG),
                                              g_hot[:, t, :].rearrange("p (g o) -> p g o", o=1).to_broadcast([P, GROUPS, EPG]),
                                              ALU.add)
            link(ins)
            first_hot(e1, e_masked, m1, c_("desc_e"))
            is_low(e1, 0, E)
            link(is_low(e1, 1, E))
            link(nc.vector.scalar_tensor_tensor(e_masked, e1, -4.0 * BIG, e_masked, ALU.mult, ALU.add))
            first_hot(e2, e_masked, m2, c_("desc_e"))
            nc.vector.tensor_tensor(diff, m2, m1, ALU.subtract).then_inc(route_for_exp, 1)
            is_low(e2, 0, E)
            link(is_low(e2, 1, E))
            nc.vector.tensor_tensor(member, e1, e2, ALU.add).then_inc(member_made, 1)
            def xeT_lo(i, par):
                dve.wait_ge(xeT_hi, i + 1)
                nc.vector.tensor_tensor(xeT[:, par, :, SLOTS:2 * SLOTS],
                                        ps[:, 6, :].rearrange("p (a b) -> p a b", b=SLOTS),
                                        xeT[:, par, :, 0:SLOTS].bitcast(f32), ALU.subtract).then_inc(xeT_made, 1)

            def make_pick(par, i):
                for t in range(TT):
                    ins = nc.vector.tensor_scalar(pick[:, par, t, :], c_("slot_row"), rank_tab[:, t, i], None, ALU.is_equal)
                ins.then_inc(pick_made, 1)

            dve.wait_ge(route_exp, 1)
            link(nc.vector.tensor_reduce(p_g, g_exp, AX.X, ALU.add))
            nc.vector.reciprocal(p_g, p_g).then_inc(inverses, 1)
            dve.wait_ge(route_exp, 2)
            link(nc.vector.tensor_scalar(w1, diff, 1.0, None, ALU.add))
            nc.vector.reciprocal(w1, w1).then_inc(inverses, 1)
            dve.wait_ge(ranked, 1)
            rk = ps[:, 5, 0:2 * E].rearrange("p (t e) -> p t e", e=E)
            link(nc.vector.scalar_tensor_tensor(rank, rk, 1.0, member, ALU.add, ALU.mult))
            nc.vector.tensor_scalar(rank_tab[:, :, 0:E], rank, -1.0, None, ALU.add).then_inc(rank_made, 1)
            dve.wait_ge(rank_made, 1)
            make_pick(0, slice(0, 1))
            make_pick(1, slice(1, 2))
            expert_lo(0, 0, 2)
            xeT_lo(0, 0)
            expert_lo(0, 0, 3)
            for r in range(1, MAX_ROUNDS + 1):
                ins = nc.vector.tensor_scalar(rank_tab[:, :, r * E:(r + 1) * E], rank, -1.0 - float(SLOTS * r), None, ALU.add)
            link(ins)
            link(nc.vector.tensor_reduce(stat[:, 12:13], ps[:, 5, 2 * E:3 * E], AX.X, ALU.max))
            link(nc.vector.tensor_scalar(stat[:, 13:14], stat[:, 12:13], float(SLOTS), float(E // 2), ALU.is_gt, ALU.mult))
            for r in range(2, MAX_ROUNDS):
                link(nc.vector.tensor_scalar(stat[:, 14:15], stat[:, 12:13], float(SLOTS * r), float(E // 2), ALU.is_gt, ALU.mult))
                link(nc.vector.tensor_tensor(stat[:, 13:14], stat[:, 13:14], stat[:, 14:15], ALU.add))
            nc.vector.tensor_scalar(loops[:, 0:1], stat[:, 13:14], float(E // 2 - 1), None, ALU.add).then_inc(loops_made, 1)


            def y_out_lo(i, par, y_parts, bank=6):
                dve.wait_ge(y_hi, i + 1)
                nc.vector.scalar_tensor_tensor(y_parts[:, 1, :], ps[:, bank:bank + 2, :].rearrange("p a b -> p (a b)"),
                                               comb_slot[:, par:par + 1], y_parts[:, 0, :].bitcast(f32),
                                               ALU.mult, ALU.subtract).then_inc(y_lo, 1)

            def step(j, r):
                first = isinstance(j, int)
                i = 2 * j + r
                start = first and i == 0
                m0 = 0 if start else 3 * r - 1
                if not start:
                    expert_lo(j, m0, 2)
                    expert_lo(j, m0, 3)
                if start:
                    expert_lo(j, m0, 4)
                xeT_lo(i + 1, (r + 1) % 2)
                if not start:
                    expert_lo(j, m0, 4)
                expert_lo(j, m0, 5)
                dve.wait_ge(slotted, i + 1)
                nc.vector.tensor_reduce(comb_slot[:, r:r + 1], G0[:, 0:3], AX.X, ALU.add).then_inc(comb_slot_made, 1)
                make_pick(r, slice(r + 2, r + 3) if first else bass.ds(2 * j + (r + 2), 1))
                dve.wait_ge(silu_made, i + 1)
                if not start:
                    dve.wait_ge(h_lo, i)
                nc.vector.tensor_tensor(h_sb[:, :, :], silu_sb[:, :, :],
                                        G1.rearrange("p (a b) -> p a b", b=SLOTS)[:, 4:8, :], ALU.mult).then_inc(h_made, 1)
                if not start:
                    expert_lo(j, m0, 6)
                    expert_lo(j, m0, 7)
                    y_out_lo(i - 1, (r + 1) % 2, y_parts)

            step(0, 0)
            step(0, 1)
            dve.wait_ge(loops_made, 1)
            last_pair = nc.vector.value_load(loops[0:1, 0:1], min_val=E // 2 - 1, max_val=MAX_ROUNDS * E // 2 - 1)
            with dve.Fori(1, last_pair + 1) as j:
                step(j, 0)
                step(j, 1)
            y_out_lo(2 * last_pair + 1, 1, y_last, 4)

            dve.wait_ge(sumsq3, 2)
            rstd(0, 4, 6, 20)
            dve.wait_ge(final_loaded, 16)
            for t in range(TT):
                nc.vector.scalar_tensor_tensor(x3[:, t, :], sums(t), stat[:, 20 + t:21 + t], raw[:, 0, 0:D],
                                               ALU.mult, ALU.mult).then_inc(out_made, 1)

        @block.tensor
        def _(pe):
            mm = nc.tensor.matmul
            pe.wait_ge(cst_loaded, 16)

            def turn(dst_bank, src, need, done):
                for k in range(2):
                    for t in range(TT):
                        last = nc.tensor.transpose(ps[:, dst_bank, k * T + t * P:k * T + (t + 1) * P], src(t, k), ident)
                last.then_inc(done, 1)

            pe.wait_ge(scaled, 2)
            for c2 in range(4):
                turn(4 + c2, lambda t, k: x_sb[:, t, (2 * c2 + k) * P:(2 * c2 + k + 1) * P], None, xT_turned)

            def x2_turn(c2):
                pe.wait_ge(x2_made, 2 * (c2 // 2) + 2)
                if c2 == 3:
                    pe.wait_ge(zT_made, 4)
                turn(X2_BANK[c2], lambda t, k: x2[:, t, (2 * c2 + k) * P:(2 * c2 + k + 1) * P], None, zT_turned)

            def columns(N, acts, arriving=False):
                w_hi, w_lo = conv_half(hi, N), conv_half(lo, N)
                for c in range(2):
                    dst = ps[:, N % RING, c * T:(c + 1) * T]
                    for k in range(KT):
                        if arriving and c == 0:
                            pe.wait_ge(x_lo, k + 1)
                        mm(dst, w_hi[:, k, c * P:(c + 1) * P], acts[:, 0, k, :], start=(k == 0), stop=False)
                        mm(dst, w_hi[:, k, c * P:(c + 1) * P], acts[:, 1, k, :], start=False, stop=False)
                        last = mm(dst, w_lo[:, k, c * P:(c + 1) * P], acts[:, 0, k, :], start=False, stop=(k == KT - 1))
                last.then_inc(half_used, 1)

            def contraction(N, acts, tile_done=None, between=lambda: None):
                h = N % 2
                w_hi = hi[:, N % CONV, :].rearrange("p (k n) -> p k n", n=512)
                w_lo = lo[:, N % CONV, :].rearrange("p (k n) -> p k n", n=512)
                for t in range(TT):
                    dst = ps[:, (N - h + t) % RING, :]
                    for k in range(4):
                        tok = slice(t * P, (t + 1) * P)
                        first, end = h == 0 and k == 0, h == 1 and k == 3
                        mm(dst, acts[:, 0, 4 * h + k, tok], w_hi[:, k, :], start=first, stop=False, skip_group_check=True)
                        mm(dst, acts[:, 1, 4 * h + k, tok], w_hi[:, k, :], start=False, stop=False, skip_group_check=True)
                        last = mm(dst, acts[:, 0, 4 * h + k, tok], w_lo[:, k, :], start=False, stop=end, skip_group_check=True)
                    if tile_done and h == 1 and t == 0:
                        last.then_inc(tile_done, 1)
                    if t == 0:
                        between()
                last.then_inc(half_used, 1)

            for N in range(RING):
                pe.wait_ge(lo_made, N + 1)
                columns(N, inA, arriving=(N == 0))
            with pe.Fori(1, 2 * LOOPED // RING) as it:
                for b in range(RING):
                    pe.wait_ge(lo_made, RING * it + (b + 1))
                    pe.wait_ge(bank_free[b], it)
                    columns(b, inA)

            def scores(h):
                pe.wait_ge(q_made, h // 2 * 2 + 2)
                pe.wait_ge(k_made, h // 2 * 2 + 2)
                if h < 2:
                    pe.wait_ge(mem_lo, KT)
                else:
                    pe.wait_ge(exps, 2 * (h - 1))
                for t in range(TT):
                    for c in range(2):
                        last = mm(ps[:, 6 + h % 2, t * T:(t + 1) * T], qT[:, 2 * h + c, t * P:(t + 1) * P],
                                  kT[:, 2 * h + c, :], start=(c == 0), stop=(c == 1))
                last.then_inc(scored, 1)

            def turn_probs(h):
                pe.wait_ge(prob_made, 2 * h + 2)
                if h < 2:
                    pe.wait_ge(exps, 2 * (h + 2) + 2)
                else:
                    pe.wait_ge(probsT_made, h - 1)
                for m in range(TT):
                    for t in range(TT):
                        last = nc.tensor.transpose(ps[:, 6 + h % 2, m * T + t * P:m * T + (t + 1) * P],
                                                   probs[:, h, t, m * P:(m + 1) * P], ident)
                last.then_inc(probs_turned, 1)

            def attend(h):
                pe.wait_ge(v_made, h // 2 + 1)
                pe.wait_ge(probsT_made, 4 if h < 2 else 4)
                if h >= 2:
                    pe.wait_ge(att_lo, h - 1)
                for c in range(2):
                    for m in range(TT):
                        last = mm(ps[:, 6 + h % 2, c * T:(c + 1) * T],
                                  v_sb[:, m, (2 * h + c) * P:(2 * h + c + 1) * P], probsT[:, h, m, :],
                                  start=(m == 0), stop=(m == TT - 1))
                last.then_inc(attended, 1)

            def mem_turn(c2):
                if c2 >= 2:
                    pe.wait_ge(mem_lo, 2 * (c2 - 2) + 2)
                turn(6 + c2 % 2, lambda t, k: mem_sb[:, t, (2 * c2 + k) * P:(2 * c2 + k + 1) * P], None, memT_turned)

            def channel_sum(bank, src, needs, done):
                for c in range(KT):
                    if c in needs:
                        pe.wait_ge(*needs[c])
                    last = mm(ps[:, bank, 0:T], ones, src[:, c, :], start=(c == 0), stop=(c == KT - 1))
                last.then_inc(done, 1)

            def logits(g):
                if g == 0:
                    pe.wait_ge(wr_loaded, 32)
                    pe.wait_ge(att_lo, HEADS)
                    pe.wait_ge(zT_made, 2)
                for c in range(4 * g, 4 * g + 4):
                    pe.wait_ge(zT_made, c + 1)
                    for t in range(TT):
                        last = mm(ps[:, LOGIT_BANK[t], 0:GROUPS + E], zT[:, c, t * P:(t + 1) * P], wr[:, c, :],
                                  start=(c == 0), stop=(c == KT - 1), skip_group_check=True)
                if g == 1:
                    last.then_inc(logits_done, 1)

            F = FIRST
            extra = {F["q"] - 1: [lambda: pe.wait_ge(scaled, 4), lambda: mem_turn(0), lambda: mem_turn(1)],
                     F["q"] + 1: [lambda: mem_turn(2), lambda: mem_turn(3)],
                     F["v"] - 1: [lambda: scores(0), lambda: scores(1)],
                     F["v"] + 1: [lambda: scores(2), lambda: scores(3)],
                     F["v"] + 2: [lambda: turn_probs(0), lambda: turn_probs(1)],
                     F["v"] + 3: [lambda: turn_probs(2), lambda: turn_probs(3)],
                     F["gate2"]: [lambda: attend(0), lambda: attend(1)],
                     F["gate2"] + 1: [lambda: attend(2), lambda: attend(3)],
                     F["out_x"]: [lambda: channel_sum(6, conv, {0: (conv_step, TAPS_B * DVE_TILES),
                                                                      DVE_TILES: (conv_pool, (2 * TAPS_B - 1) * (KT - DVE_TILES))},
                                                            ln_sum)],
                     F["out_x"] + 2: [lambda: channel_sum(7, u_sb, {0: (ln_square, 1), 4: (ln_square, 2)}, ln_sumsq)],
                     F["w_o"] + 2: [lambda: x2_turn(0), lambda: x2_turn(1)]}
            ready = {F["out_a"]: (a_lo, 4), F["k"]: (mem_lo, KT), F["out_x"]: (att_lo, HEADS),
                     F["out_b"]: (b_lo, 1), F["w_o"]: (merged_lo, 2), F["w_o"] + 1: (merged_lo, 4)}
            for N in range(2 * LOOPED, DENSE):
                name = UNITS[N // 2][0]
                if N in ready:
                    pe.wait_ge(*ready[N])
                acts = inB if name in ("out_a", "k", "v", "out_x", "out_b") else inA
                pe.wait_ge(lo_made, N + 1)
                if name in K_SPLIT:
                    if N % 2 == 0:
                        for t in range(TT):
                            pe.wait_ge(bank_free[(N + t) % RING], N // RING)
                    if name == "w_o":
                        contraction(N, acts, w_o_done, (lambda: logits(0)) if N == DENSE - 1 else (lambda: None))
                    else:
                        contraction(N, acts)
                else:
                    pe.wait_ge(bank_free[N % RING], N // RING)
                    columns(N, acts)
                for work in extra.get(N, ()):
                    work()

            x2_turn(2)
            x2_turn(3)
            logits(1)
            for b in range(4):
                g = b % 2
                mm(Y[b], ident, x2[:, b // 2, g * 512:(g + 1) * 512], start=True, stop=False,
                   skip_group_check=True).then_inc(y_seeded, 1)
            pe.wait_ge(member_made, 1)
            member = R["member"]
            mm(ps[:, 5, 0:E], before, member[:, 0, :], start=True, stop=True)
            mm(ps[:, 5, E:2 * E], ones, member[:, 0, :], start=True, stop=False)
            mm(ps[:, 5, E:2 * E], before, member[:, 1, :], start=False, stop=True)
            mm(ps[:, 5, 2 * E:3 * E], ones, member[:, 0, :], start=True, stop=False)
            mm(ps[:, 5, 2 * E:3 * E], ones, member[:, 1, :], start=False, stop=True).then_inc(ranked, 1)

            def gather(i, par):
                pe.wait_ge(pick_made, i + 1)
                for c in range(KT):
                    dst = ps[:, 6, c * SLOTS:(c + 1) * SLOTS]
                    for k in range(3 * TT):
                        part_, t = k // TT, k % TT
                        if isinstance(i, int) and i == 0 and c == 0:
                            pe.wait_ge((z_part0, z_part1, z_part2)[part_], t + 1)
                        last = mm(dst, z_parts[:, part_, t, c * P:(c + 1) * P], pick[:, par, t, 0:SLOTS],
                                  start=(k == 0), stop=(k == 3 * TT - 1))
                last.then_inc(gathered, 1)

            def gate_or_up(j, m0, k, par):
                N = DENSE + 2 * m0 + k
                pe.wait_ge(lo_made, 12 * j + (N + 1))
                dst = G0 if k < 2 else G1
                for kt in range(4):
                    for w in (hi, lo):
                        last = mm(dst, xeT[:, par, 4 * (k % 2) + kt, :], expert_half(w, N)[:, kt * 512:(kt + 1) * 512],
                                  start=(k % 2 == 0 and kt == 0 and w is hi),
                                  stop=(k % 2 == 1 and kt == 3 and w is lo), skip_group_check=True)
                last.then_inc(half_used, 1)

            def down(j, m0, k, h, DN=DN):
                N = DENSE + 2 * m0 + k
                pe.wait_ge(lo_made, 12 * j + (N + 1))
                for kt in range(2):
                    for w in (hi, lo):
                        for g in range(2):
                            a = kt * D + g * 512
                            last = mm(DN[g], hT[:, 2 * h + kt, :], expert_half(w, N)[:, a:a + 512],
                                      start=(h == 0 and kt == 0 and w is hi),
                                      stop=(h == 1 and kt == 1 and w is lo), skip_group_check=True)
                last.then_inc(half_used, 1)

            def combine(i, par, y_parts=y_parts):
                pe.wait_ge(put_made, i + 1)
                pe.wait_ge(y_lo, i + 1)
                for t in range(TT):
                    for part_ in range(2):
                        for g in range(2):
                            last = mm(Y[2 * t + g], put[:, par, t * P:(t + 1) * P], y_parts[:, part_, g * 512:(g + 1) * 512],
                                      start=False, stop=False, skip_group_check=True)
                    last.then_inc(combined, 1)

            gather(0, 0)

            def step(j, r, e_col):
                first = isinstance(j, int)
                i = 2 * j + r
                start = first and i == 0
                m0 = 0 if start else 3 * r - 1
                pe.wait_ge(xeT_made, i + 1)
                if not start:
                    pe.wait_ge(put_made, i)
                gate_or_up(j, m0, 0, r)
                gate_or_up(j, m0, 1, r)
                if not first:
                    combine(i - 2, r)
                gather(i + 1, (r + 1) % 2)
                if not start:
                    pe.wait_ge(h_made, i)
                else:
                    pe.wait_ge(loops_made, 1)
                gate_or_up(j, m0, 2, r)
                gate_or_up(j, m0, 3, r)
                pe.wait_ge(gate_out, i + 1)
                for t in range(TT):
                    if start and t == 0:
                        pe.wait_ge(comb_made, 1)
                        pe.wait_ge(ident_made, 1)
                    mm(G0[:, 0:3], pick[:, r, t, :], comb[:, t, e_col, 0:3].rearrange("p a b -> p (a b)"),
                       start=(t == 0), stop=(t == TT - 1), skip_group_check=True)
                for t in range(TT):
                    last = mm(G0[:, T + t * P:T + (t + 1) * P], pick[:, r, t, :], ident_bf[:, :],
                              start=True, stop=True, skip_group_check=True)
                last.then_inc(slotted, 1)
                pe.wait_ge(up_out, i + 1)
                for f in range(2 * FF // P):
                    last = mm(G1[:, f * SLOTS:(f + 1) * SLOTS], gu_sb[:, f * P:(f + 1) * P], fold,
                              start=True, stop=True, skip_group_check=True)
                last.then_inc(folded, 1)
                if not start:
                    pe.wait_ge(xeT_made, i + 2)
                    pe.wait_ge(h_lo, i)
                    down(j, m0, 4, 0)
                    down(j, m0, 5, 1)

            step(0, 0, slice(0, 1))
            step(0, 1, slice(1, 2))
            last_pair = nc.tensor.value_load(loops[0:1, 0:1], min_val=E // 2 - 1, max_val=MAX_ROUNDS * E // 2 - 1)
            with pe.Fori(1, last_pair + 1) as j:
                step(j, 0, bass.ds(j % (E // 2) * 2, 1))
                step(j, 1, bass.ds(j % (E // 2) * 2 + 1, 1))
            pe.wait_ge(xeT_made, 2 * last_pair + 3)
            pe.wait_ge(h_lo, 2 * last_pair + 2)
            pe.wait_ge(put_made, 2 * last_pair + 2)
            pe.wait_ge(h_made, 2 * last_pair + 2)
            down(last_pair, 5, 0, 0, (G0, G1))
            down(last_pair, 5, 1, 1, (G0, G1))
            combine(2 * last_pair, 0)
            combine(2 * last_pair + 1, 1, y_last)


def kernel(x, mem, mix_norm_g, mem_norm_g, w_in, b_gate, conv_a_w, w_out_a, b_glu,
           conv_b_w, conv_b_b, ln_b_g, ln_b_b, w_out_b, b_out_b, w_kv, w_out_x, w_o,
           ffn_norm_g, w_group, b_group, w_router, b_router, w_gate_up, w_down, final_norm_g):
    import numpy as np
    import concourse.bacc as bacc
    from concourse.bass_utils import run_bass_kernel_spmd as run

    def per_channel(v):
        return np.asarray(v).reshape(-1, P).T

    consts = np.zeros((P, N_CST), np.float32)

    def put_const(name, values):
        consts[:, CST[name][0]:CST[name][1]] = values

    put_const("ident", np.eye(P))
    put_const("ones", 1.0)
    put_const("before", np.triu(np.ones((P, P)), 1))
    put_const("fold", np.concatenate([np.eye(SLOTS), np.eye(SLOTS)]))
    put_const("slot_row", np.arange(P) % SLOTS)
    put_const("desc_g", np.arange(GROUPS, 0, -1))
    put_const("desc_e", np.arange(E, 0, -1))
    vectors = (mix_norm_g, mem_norm_g, b_gate, b_glu, conv_a_w, conv_b_w, conv_b_b, ln_b_g, ln_b_b, b_out_b, ffn_norm_g)
    arrays = {
        "x": x[0], "mem": mem[0], "w_in": w_in[0], "w_out_a": w_out_a[0], "w_out_b": w_out_b[0],
        "w_out_x": w_out_x[0], "w_kv": w_kv[0], "w_o": w_o[0], "w_gate_up": w_gate_up[0], "w_down": w_down[0],
        "w_route": np.concatenate([w_group[0], w_router[0]], axis=1),
        "cols": np.concatenate([per_channel(v[0]) for v in vectors], axis=1),
        "rows": np.stack([np.asarray(ffn_norm_g[0]), np.asarray(final_norm_g)]),
        "b_route": np.concatenate([b_group[0], b_router[0]])[None, :],
        "consts": consts,
    }
    nc = bacc.Bacc("TRN2", target_bir_lowering=False, num_devices=1, dynamic_dma_scratch_size=1024)
    feeds, args = {}, []
    for name, a in arrays.items():
        a = np.ascontiguousarray(a)
        feeds[f"in_{name}"] = a
        args.append(nc.dram_tensor(f"in_{name}", a.shape, mybir.dt.from_np(a.dtype), kind="ExternalInput").ap())
    out = nc.dram_tensor("out", (T, D), f32, kind="ExternalOutput").ap()
    hybrid_moe_kernel(nc, *args, out)
    return run(nc, [feeds], core_ids=[0]).results[0]["out"].reshape(1, T, D)
```
